# Optimizing a Trainium2 kernel written in Bass

```python
import math
import jax, jax.numpy as jnp
from jax import lax
import numpy as np

D_MODEL = 1024
BATCH = 1
SEQ = 1024
DEPTH = 2
DEC_BATCH = 8
DEC_SEQ = 4
PAST_LEN = 4096
PAGE_SIZE = 128

N_EVEN = (DEPTH + 1) // 2
N_ODD = DEPTH // 2

H_M = 4
DK_M = 256
DV_M = 256
D_QKM = H_M * DK_M
D_M = H_M * DV_M
CONV_W = 4
F_BIAS_LO = 3.0
F_BIAS_HI = 6.0
H_R = 4
DK_R = 256
DV_R = 256
D_QKR = H_R * DK_R
D_R = H_R * DV_R
RET_THETA = 10000.0
H_C = 8
HD_C = 64
D_QKC = 2 * H_C * HD_C
D_C = H_C * 2 * HD_C
ROPE_THETA = 500000.0
ROPE_DIM = HD_C // 4
Q_BLOCK = 128
CHUNK = 64
EPS = 1e-6

SIZES_A = (2 * D_QKM, D_M, D_M, H_M, H_M, D_QKR, D_QKR, D_R, D_R)
PROJ_A = sum(SIZES_A)
SIZES_C = (D_QKC, D_QKC, D_C, D_C)
PROJ_C = sum(SIZES_C)

kernel_name = 'hybrid_mlstm_retention_diffattn_step'

F32 = jnp.float32

def _split_idx(sizes):
    return [int(s) for s in np.cumsum(sizes)[:-1]]

def rms_norm(x, g):
    xf = x.astype(F32)
    y = xf * lax.rsqrt(jnp.mean(xf * xf, axis=-1, keepdims=True) + EPS)
    return (y * g.astype(F32)).astype(x.dtype)

def rope(x, pos, rot_dim, theta):
    half = rot_dim // 2
    inv = jnp.power(theta, -jnp.arange(half, dtype=F32) / half)
    ang = pos.astype(F32)[:, None] * inv[None, :]
    cos = jnp.cos(ang)[None, :, None, :]
    sin = jnp.sin(ang)[None, :, None, :]
    xf = x.astype(F32)
    x1 = xf[..., :half]
    x2 = xf[..., half:rot_dim]
    out = jnp.concatenate([x1 * cos - x2 * sin, x1 * sin + x2 * cos, xf[..., rot_dim:]], axis=-1)
    return out.astype(x.dtype)

def _chunks(a, L):
    B, T = a.shape[:2]
    return jnp.moveaxis(a.reshape(B, T // L, L, *a.shape[2:]), 1, 0)

def _unchunk(a):
    NC, B, L = a.shape[:3]
    return jnp.moveaxis(a, 0, 1).reshape(B, NC * L, *a.shape[3:])

def mlstm_scan(q, k, v, ig, fg, C0, n0, m0):
    T = q.shape[1]
    L = CHUNK if T % CHUNK == 0 else T
    causal = jnp.tril(jnp.ones((L, L), dtype=bool))[None, :, :, None]
    xs = (_chunks((q * DK_M ** -0.5).astype(F32), L), _chunks(k.astype(F32), L),
          _chunks(v.astype(F32), L), _chunks(ig.astype(F32), L),
          _chunks(jax.nn.log_sigmoid(fg.astype(F32)), L))

    def step(carry, inp):
        C, n, m = carry
        q_, k_, v_, i_, lf = inp
        b = jnp.cumsum(lf, axis=1)
        inter = b + m[:, None, :]
        Dm = b[:, :, None, :] - b[:, None, :, :] + i_[:, None, :, :]
        Dm = jnp.where(causal, Dm, -jnp.inf)
        m_t = jnp.maximum(inter, jnp.max(Dm, axis=2))
        w = jnp.exp(Dm - m_t[:, :, None, :])
        s_inter = jnp.exp(inter - m_t)
        qk = jnp.einsum('bthd,bshd->btsh', q_, k_) * w
        num = (jnp.einsum('btsh,bshv->bthv', qk, v_)
               + s_inter[..., None] * jnp.einsum('bthd,bhdv->bthv', q_, C))
        den = jnp.sum(qk, axis=2) + s_inter * jnp.einsum('bthd,bhd->bth', q_, n)
        h = num / jnp.maximum(jnp.abs(den), jnp.exp(-m_t))[..., None]
        bL = b[:, -1]
        dec = bL[:, None, :] - b + i_
        m_new = jnp.maximum(bL + m, jnp.max(dec, axis=1))
        ws = jnp.exp(dec - m_new[:, None, :])
        sc = jnp.exp(bL + m - m_new)
        C_new = sc[..., None, None] * C + jnp.einsum('bshd,bshv->bhdv', k_ * ws[..., None], v_)
        n_new = sc[..., None] * n + jnp.einsum('bshd->bhd', k_ * ws[..., None])
        return (C_new, n_new, m_new), h

    (C, n, m), hs = lax.scan(step, (C0.astype(F32), n0.astype(F32), m0.astype(F32)), xs)
    return _unchunk(hs), C, n, m

def retention_scan(q, k, v, S0):
    T = q.shape[1]
    L = CHUNK if T % CHUNK == 0 else T
    lg = jnp.log(1.0 - jnp.power(2.0, -5.0 - jnp.arange(H_R, dtype=F32)))
    j = jnp.arange(L, dtype=F32)
    rel = j[:, None] - j[None, :]
    decay = jnp.where((rel >= 0)[:, :, None], jnp.exp(rel[:, :, None] * lg), 0.0)
    q_in = jnp.exp((j + 1.0)[:, None] * lg)[None, :, :, None]
    k_out = jnp.exp((L - 1.0 - j)[:, None] * lg)[None, :, :, None]
    c_dec = jnp.exp(L * lg)[None, :, None, None]
    xs = (_chunks(q.astype(F32), L), _chunks(k.astype(F32), L), _chunks(v.astype(F32), L))

    def step(S, inp):
        q_, k_, v_ = inp
        qk = jnp.einsum('bthd,bshd->btsh', q_, k_) * decay
        o = jnp.einsum('btsh,bshv->bthv', qk, v_) + jnp.einsum('bthd,bhdv->bthv', q_ * q_in, S)
        S_new = c_dec * S + jnp.einsum('bshd,bshv->bhdv', k_ * k_out, v_)
        return S_new, o

    S, os_ = lax.scan(step, S0.astype(F32), xs)
    return _unchunk(os_), S

def even_mixer(h, pos0, C0, n0, m0, buf0, S0, w_in, b_i, b_f, cw, cb, gn_m, gn_r, w_out):
    B, T, _ = h.shape
    p = h @ w_in
    qk_m, v_m, z_m, ig, fg, q_r, k_r, v_r, z_r = jnp.split(p, _split_idx(SIZES_A), axis=-1)
    xpad = jnp.concatenate([buf0.astype(qk_m.dtype), qk_m], axis=1)
    acc = cb + xpad[:, 0:T] * cw[0]
    for j in range(1, CONV_W):
        acc = acc + xpad[:, j:j + T] * cw[j]
    qk_c = jax.nn.silu(acc)
    q_m = qk_c[..., :D_QKM].reshape(B, T, H_M, DK_M)
    k_m = qk_c[..., D_QKM:].reshape(B, T, H_M, DK_M)
    hm, C, n, m = mlstm_scan(q_m, k_m, v_m.reshape(B, T, H_M, DV_M),
                             ig.astype(F32) + b_i, fg.astype(F32) + b_f, C0, n0, m0)
    hm = rms_norm(hm.astype(h.dtype), gn_m) * jax.nn.silu(z_m).reshape(B, T, H_M, DV_M)
    pos = pos0 + jnp.arange(T)
    q_r = rope(q_r.reshape(B, T, H_R, DK_R), pos, DK_R, RET_THETA)
    k_r = rope(k_r.reshape(B, T, H_R, DK_R), pos, DK_R, RET_THETA) * DK_R ** -0.5
    hr, S = retention_scan(q_r, k_r, v_r.reshape(B, T, H_R, DV_R), S0)
    hr = rms_norm(hr.astype(h.dtype), gn_r) * jax.nn.silu(z_r).reshape(B, T, H_R, DV_R)
    out = jnp.concatenate([hm.reshape(B, T, D_M), hr.reshape(B, T, D_R)], axis=-1) @ w_out
    return out.astype(h.dtype), (C, n, m, xpad[:, T:], S)

def _diff_combine(s, lam):
    p = jax.nn.softmax(s, axis=-1)
    B, _, Q, K = p.shape
    p = p.reshape(B, H_C, 2, Q, K)
    return p[:, :, 0] - lam * p[:, :, 1]

def diff_attn_prompt(o, q, k, v, lam):
    B, T = q.shape[:2]
    nb = T // Q_BLOCK
    kpos = jnp.arange(T)
    vf = v.astype(F32)
    qb = _chunks(q, Q_BLOCK)

    def block(args):
        qi, bi = args
        s = jnp.einsum('bqhd,bkhd->bhqk', qi, k).astype(F32) * HD_C ** -0.5
        qpos = bi * Q_BLOCK + jnp.arange(Q_BLOCK)
        s = jnp.where((kpos[None, :] <= qpos[:, None])[None, None], s, -jnp.inf)
        a = _diff_combine(s, lam)
        return jnp.einsum('bhqk,bkhe->bqhe', a, vf)

    out = lax.map(block, (qb, jnp.arange(nb)))
    return _unchunk(out)

def diff_attn_cached(q, k, v, kp, vp, lam):
    Q = q.shape[1]
    P = kp.shape[1]
    scale = HD_C ** -0.5
    s_p = jnp.einsum('bqhd,bkhd->bhqk', q, kp).astype(F32) * scale
    s_n = jnp.einsum('bqhd,bkhd->bhqk', q, k).astype(F32) * scale
    s_n = jnp.where(jnp.tril(jnp.ones((Q, Q), dtype=bool))[None, None], s_n, -jnp.inf)
    a = _diff_combine(jnp.concatenate([s_p, s_n], axis=-1), lam)
    return (jnp.einsum('bhqk,bkhe->bqhe', a[..., :P], vp.astype(F32))
            + jnp.einsum('bhqk,bkhe->bqhe', a[..., P:], v.astype(F32)))

def odd_mixer(h, pos0, layer_idx, o, attend, w_in, lam_p, gn, w_out):
    B, T, _ = h.shape
    p = h @ w_in
    q, k, v, z = jnp.split(p, _split_idx(SIZES_C), axis=-1)
    pos = pos0 + jnp.arange(T)
    q = rope(q.reshape(B, T, 2 * H_C, HD_C), pos, ROPE_DIM, ROPE_THETA)
    k = rope(k.reshape(B, T, 2 * H_C, HD_C), pos, ROPE_DIM, ROPE_THETA)
    v = v.reshape(B, T, H_C, 2 * HD_C)
    lam_init = 0.8 - 0.6 * math.exp(-0.3 * layer_idx)
    lf = lam_p.astype(F32)
    lam = jnp.exp(jnp.sum(lf[0] * lf[1])) - jnp.exp(jnp.sum(lf[2] * lf[3])) + lam_init
    a = attend(o, q, k, v, lam)
    a = rms_norm(a.astype(h.dtype), gn) * (1.0 - lam_init)
    out = (a.reshape(B, T, D_C) * jax.nn.silu(z)) @ w_out
    return out.astype(h.dtype), k, v

def forward(x, pos0, st_C, st_n, st_m, st_conv, st_S, attend, norm_pre, norm_post,
            w_in_a, b_gate_i, b_gate_f, conv_w, conv_b, gn_mlstm, gn_ret, w_out_a,
            w_in_c, lambda_qk, gn_diff, w_out_c):
    Cs, ns, ms, bufs, Ss, ks, vs = [], [], [], [], [], [], []
    for i in range(DEPTH):
        h = rms_norm(x, norm_pre[i])
        if i % 2 == 0:
            e = i // 2
            out, (C, n, m, buf, S) = even_mixer(
                h, pos0, st_C[e], st_n[e], st_m[e], st_conv[e], st_S[e], w_in_a[e],
                b_gate_i[e], b_gate_f[e], conv_w[e], conv_b[e], gn_mlstm[e], gn_ret[e], w_out_a[e])
            Cs.append(C); ns.append(n); ms.append(m); bufs.append(buf); Ss.append(S)
        else:
            o = i // 2
            out, k, v = odd_mixer(h, pos0, i, o, attend, w_in_c[o], lambda_qk[o], gn_diff[o], w_out_c[o])
            ks.append(k); vs.append(v)
        x = x + rms_norm(out, norm_post[i])
    return (x, jnp.stack(Cs), jnp.stack(ns), jnp.stack(ms), jnp.stack(bufs), jnp.stack(Ss),
            jnp.stack(ks), jnp.stack(vs))

def setup_inputs(seed: int = 0) -> dict:
    key = jax.random.key(seed)
    ks = jax.random.split(key, 26)
    n_pages = PAST_LEN // PAGE_SIZE
    n_used = DEC_BATCH * n_pages
    n_pool = n_used + n_used // 4

    def nrm(k, shape, s):
        return jax.random.normal(k, shape, F32) * s

    return {
        'x_prompt': nrm(ks[0], (BATCH, SEQ, D_MODEL), 1.0),
        'x_sample': nrm(ks[1], (DEC_BATCH, DEC_SEQ, D_MODEL), 1.0),
        'state_mlstm_C': nrm(ks[2], (N_EVEN, DEC_BATCH, H_M, DK_M, DV_M), 0.5),
        'state_mlstm_n': nrm(ks[3], (N_EVEN, DEC_BATCH, H_M, DK_M), 0.5),
        'state_mlstm_m': nrm(ks[4], (N_EVEN, DEC_BATCH, H_M), 1.0),
        'state_mlstm_conv': nrm(ks[5], (N_EVEN, DEC_BATCH, CONV_W - 1, 2 * D_QKM), 1.0),
        'state_ret_S': nrm(ks[6], (N_EVEN, DEC_BATCH, H_R, DK_R, DV_R), 1.0),
        'cache_k': nrm(ks[7], (N_ODD, n_pool, PAGE_SIZE, 2 * H_C, HD_C), 1.0),
        'cache_v': nrm(ks[8], (N_ODD, n_pool, PAGE_SIZE, H_C, 2 * HD_C), 1.0),
        'page_table': jax.random.permutation(ks[9], n_pool)[:n_used].reshape(DEC_BATCH, n_pages).astype(jnp.int32),
        'norm_pre': 1.0 + nrm(ks[10], (DEPTH, D_MODEL), 0.05),
        'norm_post': 1.0 + nrm(ks[11], (DEPTH, D_MODEL), 0.05),
        'w_in_a': nrm(ks[12], (N_EVEN, D_MODEL, PROJ_A), D_MODEL ** -0.5),
        'b_gate_i': nrm(ks[13], (N_EVEN, H_M), 0.1),
        'b_gate_f': jnp.linspace(F_BIAS_LO, F_BIAS_HI, H_M, dtype=F32)[None, :] + nrm(ks[14], (N_EVEN, H_M), 0.1),
        'conv_w': nrm(ks[15], (N_EVEN, CONV_W, 2 * D_QKM), CONV_W ** -0.5),
        'conv_b': nrm(ks[16], (N_EVEN, 2 * D_QKM), 0.02),
        'gn_mlstm': 1.0 + nrm(ks[17], (N_EVEN, H_M, DV_M), 0.05),
        'gn_ret': 1.0 + nrm(ks[18], (N_EVEN, H_R, DV_R), 0.05),
        'w_out_a': nrm(ks[19], (N_EVEN, D_M + D_R, D_MODEL), (D_M + D_R) ** -0.5),
        'w_in_c': nrm(ks[20], (N_ODD, D_MODEL, PROJ_C), D_MODEL ** -0.5),
        'lambda_qk': nrm(ks[21], (N_ODD, 4, HD_C), 0.1),
        'gn_diff': 1.0 + nrm(ks[22], (N_ODD, H_C, 2 * HD_C), 0.05),
        'w_out_c': nrm(ks[23], (N_ODD, D_C, D_MODEL), D_C ** -0.5),
    }

def reference(x_prompt, x_sample, state_mlstm_C, state_mlstm_n, state_mlstm_m, state_mlstm_conv,
              state_ret_S, cache_k, cache_v, page_table, norm_pre, norm_post, w_in_a, b_gate_i,
              b_gate_f, conv_w, conv_b, gn_mlstm, gn_ret, w_out_a, w_in_c, lambda_qk, gn_diff, w_out_c):
    weights = (norm_pre, norm_post, w_in_a, b_gate_i, b_gate_f, conv_w, conv_b, gn_mlstm, gn_ret,
               w_out_a, w_in_c, lambda_qk, gn_diff, w_out_c)
    Bp = x_prompt.shape[0]
    (y_prompt, C_p, n_p, m_p, conv_p, S_p, k_p, v_p) = forward(
        x_prompt, 0,
        jnp.zeros((N_EVEN, Bp, H_M, DK_M, DV_M), F32),
        jnp.zeros((N_EVEN, Bp, H_M, DK_M), F32),
        jnp.zeros((N_EVEN, Bp, H_M), F32),
        jnp.zeros((N_EVEN, Bp, CONV_W - 1, 2 * D_QKM), x_prompt.dtype),
        jnp.zeros((N_EVEN, Bp, H_R, DK_R, DV_R), F32),
        diff_attn_prompt, *weights)

    def sample_attend(o, q, k, v, lam):
        Bs = q.shape[0]
        past = page_table.shape[1] * cache_k.shape[2]
        kp = cache_k[o][page_table].reshape(Bs, past, 2 * H_C, HD_C)
        vp = cache_v[o][page_table].reshape(Bs, past, H_C, 2 * HD_C)
        return diff_attn_cached(q, k, v, kp, vp, lam)

    pos_s = page_table.shape[1] * cache_k.shape[2]
    (y_sample, C_s, n_s, m_s, conv_s, S_s, k_s, v_s) = forward(
        x_sample, pos_s, state_mlstm_C, state_mlstm_n, state_mlstm_m, state_mlstm_conv,
        state_ret_S, sample_attend, *weights)
    return (y_prompt, y_sample, C_p, n_p, m_p, conv_p, S_p, k_p, v_p,
            C_s, n_s, m_s, conv_s, S_s, k_s, v_s)


_drawn_inputs = setup_inputs


def setup_inputs(seed=0):
    import zlib

    import numpy as np

    out = dict(_drawn_inputs(seed))
    spreads = {}
    factors = {}
    for name, (base, spread) in spreads.items():
        noise = np.random.default_rng([zlib.crc32(name.encode()), seed]).standard_normal(out[name].shape)
        drawn = base * np.exp(spread * noise) if base else spread * noise
        out[name] = __import__('jax').numpy.asarray(drawn.astype(out[name].dtype))
    for name, factor in factors.items():
        out[name] = (out[name] * factor).astype(out[name].dtype)
    return out
```

```python
import math
from contextlib import ExitStack

import numpy as np

import concourse.bass as bass
from concourse import mybir

F32 = mybir.dt.float32
I32 = mybir.dt.int32
ALU = mybir.AluOpType
ACT = mybir.ActivationFunctionType
AX_X = mybir.AxisListType.X

P = 128
D = 1024
KD = D // P
T = 1024
NB = T // P
DB, DS = 8, 4
S = DB * DS
NT = T + S
H = 4
DK = 256
QK = 2 * H * DK
CW = 4
HC, HD = 8, 64
ROT = HD // 8
PAGE = 128
PAST = 4096
NPG = PAST // PAGE
N_POOL = DB * NPG + DB * NPG // 4
EPS = 1e-6
NEG = -1e30
OFF_GATE = QK + 2 * D
OFF_RET = OFF_GATE + 2 * H
PROJ_A = OFF_RET + 4 * D
LAM_INIT = 0.8 - 0.6 * math.exp(-0.3)


def shape_tables():
    f = np.float32
    t = np.arange(P)
    same = (np.arange(S)[:, None] // DS == np.arange(S)[None, :] // DS)
    st = np.arange(S)
    gam = 1.0 - 2.0 ** (-5.0 - np.arange(H))
    rel = t[None, :] - t[:, None]
    dec = np.where(rel[:, None, :] >= 0, gam[None, :, None] ** np.maximum(rel, 0)[:, None, :], 0.0)
    rs = st[None, :] - st[:, None]
    decs = np.where((same & (rs >= 0))[:, None, :], gam[None, :, None] ** np.maximum(rs, 0)[:, None, :], 0.0)
    pos = np.concatenate([np.arange(T), PAST + st % DS]).astype(f)

    def angles(half, theta):
        inv = np.power(f(theta), -np.arange(half, dtype=f) / f(half)).astype(f)
        return (pos[:, None] * inv[None, :]).astype(f).astype(np.float64)

    a0 = angles(DK // 2, 10000.0).T
    a1 = angles(ROT, 500000.0)
    pad = np.zeros((NB * P + P, ROT))
    pad[:NT] = a1
    a1 = pad.reshape(NB + 1, P, ROT).transpose(1, 0, 2)
    reset = np.ones((H, NT))
    reset[:, 0:T:P] = 0
    reset[:, T::DS] = 0
    first = np.zeros((H, DB, DS + 1))
    first[:, :, 0] = -3e38
    newmask = np.full((2 * S, DB, S), NEG)
    for b in range(DB):
        for j in range(DS):
            q = np.arange(2 * S) % DS
            newmask[q >= j, b, DS * b + j] = 0.0
    r2 = np.arange(2 * S)
    tabs = {
        "ident": np.eye(P),
        "mask_st": np.where(rel >= 0, 0.0, NEG),
        "mask_qk": np.where(rel.T >= 0, 0.0, NEG),
        "mask_st_s": np.where(same & (rs >= 0), 0.0, NEG),
        "decay": dec.reshape(P, H * P),
        "decay_s": decs.reshape(S, H * S),
        "gin": np.broadcast_to((gam[:, None] ** (t + 1)).reshape(1, H * P), (P, H * P)),
        "gin_s": np.broadcast_to((gam[:, None] ** (st % DS + 1)).reshape(1, H * S), (P, H * S)),
        "kout": gam[None, :] ** (P - 1 - t)[:, None],
        "kout_s": gam[None, :] ** (DS - 1 - st % DS)[:, None],
        "batch_of": (st[:, None] // DS == np.arange(DB)[None, :]),
        "cos0": np.cos(a0), "sin0": np.sin(a0),
        "rot1": np.stack([np.cos(a1), np.sin(a1)], 1).reshape(P, 2 * (NB + 1) * ROT),
        "reset": reset, "first": first.reshape(H, DB * (DS + 1)),
        "ones4": np.ones((H, P)),
        "select": np.eye(H)[:, :, None] * np.ones((1, 1, P)),
        "pair_sum": (r2[:, None] % S == np.arange(S)[None, :]),
        "own_head": (np.arange(S)[:, None] // DS == np.arange(HC)[None, :]),
        "to_query": (np.arange(S)[:, None] % DS == np.arange(DS)[None, :]),
        "new_mask": newmask.reshape(2 * S, DB * S),
    }
    return {k: np.ascontiguousarray(v.reshape(v.shape[0], -1), dtype=f) for k, v in tabs.items()}


class Chain:

    def __init__(self, eng, sem):
        self.eng, self.sem, self.n = eng, sem, 0

    def link(self, ins):
        self.n += 1
        ins.then_inc(self.sem, 1)
        self.eng.wait_ge(self.sem, self.n)

    def clear(self):
        self.eng.sem_clear(self.sem)
        self.n = 0


class Core:

    def __init__(self, nc, ins, tabs, outs, ctx):
        self.nc, self.x, self.tab, self.out, self.ctx = nc, ins, tabs, outs, ctx

        def dram(name, shape):
            return nc.dram_tensor(name, shape, F32, kind="Internal").ap()

        self.s_qk = dram("s_qk", (2 * QK // P, P, NT))
        self.s_v = dram("s_v", (NT, 2 * D))
        self.s_g = dram("s_g", (NT, 2 * D))
        self.s_x1 = dram("s_x1", (NT, D))
        self.s_y1 = dram("s_y1", (NT, D))
        self.s_a1 = dram("s_a1", (S, D))
        self.hT = ctx.enter_context(nc.sbuf_tensor("hT", [P, KD, NT], F32))
        SPACER["sem"] = ctx.enter_context(nc.semaphore("spacer"))
        self.ident = ctx.enter_context(nc.sbuf_tensor("ident", [P, P], F32))


class Stage:

    def __init__(self, nc, name):
        self.nc, self.name, self.ctx, self.held = nc, name, ExitStack(), []

    def __enter__(self):
        return self

    def __exit__(self, kind, *a):
        self.ctx.close()
        if kind is None:
            self.nc.clear_and_free_semaphores(self.held)
            self.nc.all_engine_barrier()

    def sb(self, name, shape, dt=F32):
        return self.ctx.enter_context(self.nc.sbuf_tensor(f"{self.name}_{name}", shape, dt))

    def ps(self, name, shape):
        return self.ctx.enter_context(self.nc.psum_tensor(f"{self.name}_{name}", shape, F32))

    def sem(self, name):
        self.held.append(self.nc.alloc_semaphore(name=f"{self.name}_{name}"))
        return self.held[-1]

    def sems(self, name, n):
        return [self.sem(f"{name}{i}") for i in range(n)]


SPACER = {}


def wait_counted(eng, sem, value):
    eng.wait_ge(sem, value)
    eng.sem_inc(SPACER["sem"], 1)


def rows_of(b):
    return S if b == NB else P


def norm_to_columns(c):
    nc, g = c.nc, c.x
    with Stage(nc, "nx") as st:
        xb = st.sb("xb", [P, 2, D])
        junk = st.sb("junk", [P, D])
        ms = st.sb("ms", [P, 2])
        rstd = st.sb("rstd", [P, 2])
        half = st.sb("half", [P, 1])
        gcol = st.sb("gcol", [P, KD])
        grow = st.sb("grow", [KD, P])
        ps = st.ps("ps", [P, 4, 512])
        psg = st.ps("psg", [P, 512])
        s_const, s_g, s_gcol = st.sem("const"), st.sem("g"), st.sem("gcol")
        loaded = st.sems("loaded", 2)
        summed, scaled, rooted, turned, taken = (st.sem(n) for n in ("summed", "scaled", "rooted", "turned", "taken"))
        act_chain, pool_chain = st.sem("act_chain"), st.sem("pool_chain")
        x_prompt = g["x_prompt"].rearrange("a (n p) d -> (a n) p d", p=P)
        x_sample = g["x_sample"].rearrange("a t d -> (a t) d")

        with nc.Block() as block:

            @block.sync
            def _(sp):
                sp.dma_start(c.ident[:], c.tab["ident"]).then_inc(s_const, 16)
                sp.dma_start(grow[:], g["norm_pre"][0, :].rearrange("(k p) -> k p", p=P)).then_inc(s_g, 16)
                for b in range(2):
                    sp.dma_start(xb[:, b, :], x_prompt[b]).then_inc(loaded[b], 16)
                with sp.Fori(1, NB // 2) as i:
                    for s in range(2):
                        sp.wait_ge(turned, 2 * i + s - 1)
                        sp.dma_start(xb[:, s, :], x_prompt[bass.ds(2 * i + s, 1)].rearrange("a p d -> (a p) d")).then_inc(loaded[s], 16)
                sp.wait_ge(turned, NB - 1)
                sp.dma_start(xb[0:S, 0, :], x_sample).then_inc(loaded[0], 16)

            @block.scalar
            def _(act):
                def one(i, s, rows):
                    act.wait_ge(loaded[s], 16 * i + 16)
                    act.activation(junk[0:rows, :], xb[0:rows, s, :], ACT.Square, accum_out=ms[0:rows, s:s + 1]).then_inc(summed, 1)
                    act.wait_ge(rooted, 2 * i + s + 1)
                    act.activation(xb[0:rows, s, :], xb[0:rows, s, :], ACT.Copy, scale=rstd[0:rows, s:s + 1]).then_inc(scaled, 1)

                with act.Fori(0, NB // 2) as i:
                    for s in range(2):
                        one(i, s, P)
                one(NB // 2, 0, S)

            @block.gpsimd
            def _(pool):
                ch = Chain(pool, pool_chain)
                ch.link(pool.memset(half[:], -0.5))
                ch.clear()

                def one(i, s, rows):
                    wait_counted(pool, summed, 2 * i + s + 1)
                    ch.link(pool.tensor_scalar(ms[0:rows, s:s + 1], ms[0:rows, s:s + 1], 1.0 / D, EPS, ALU.mult, ALU.add))
                    ch.clear()
                    pool.tensor_tensor(rstd[0:rows, s:s + 1], ms[0:rows, s:s + 1], half[0:rows, :], ALU.pow).then_inc(rooted, 1)

                with pool.Fori(0, NB // 2) as i:
                    for s in range(2):
                        one(i, s, P)
                one(NB // 2, 0, S)

            @block.tensor
            def _(pe):
                pe.wait_ge(s_const, 16)
                pe.wait_ge(s_g, 16)
                pe.transpose(psg[:, 0:KD], grow[:], c.ident[0:KD, 0:KD]).then_inc(s_gcol, 1)

                def one(i, s, rows):
                    pe.wait_ge(scaled, 2 * i + s + 1)
                    pe.wait_ge(taken, 2 * i + s + 1)
                    for k in range(KD):
                        last = pe.transpose(ps[:, 2 * s + k // 4, (k % 4) * P:(k % 4) * P + rows],
                                            xb[0:rows, s, k * P:(k + 1) * P], c.ident[0:rows, 0:rows])
                    last.then_inc(turned, 1)

                with pe.Fori(0, NB // 2) as i:
                    for s in range(2):
                        one(i, s, P)
                one(NB // 2, 0, S)

            @block.vector
            def _(dve):
                dve.sem_inc(taken, 2)
                dve.wait_ge(s_gcol, 1)
                dve.tensor_copy(gcol[:], psg[:, 0:KD]).then_inc(act_chain, 1)
                dve.wait_ge(act_chain, 1)

                def one(i, s, rows, token):
                    dve.wait_ge(turned, 2 * i + s + 1)
                    for b in range(2):
                        last = dve.tensor_tensor(
                            c.hT[:, 4 * b:4 * b + 4, token],
                            ps[:, 2 * s + b, :].rearrange("p (k t) -> p k t", t=P)[:, :, 0:rows],
                            gcol[:, 4 * b:4 * b + 4].unsqueeze(2).broadcast_to([P, 4, rows]), ALU.mult)
                    last.then_inc(taken, 1)

                with dve.Fori(0, NB // 2) as i:
                    for s in range(2):
                        one(i, s, P, bass.ds(i * (2 * P) + s * P, P))
                one(NB // 2, 0, S, slice(T, NT))


HALVES = [(0, 512), (512, 512), (T, S)]
RAW = T + CW - 1 + DB * (DS + CW - 1)


def project_layer0(c, gates):
    nc, g = c.nc, c.x
    w = g["w_in_a"][0].rearrange("(k p) n -> p k n", p=P)
    with Stage(nc, "p0") as st:
        wqk = st.sb("wqk", [P, KD, 512])
        wvz = st.sb("wvz", [P, KD, 512])
        wg = st.sb("wg", [P, KD, 2 * H])
        raw = st.sb("raw", [P, 2, RAW])
        acc = st.sb("acc", [P, 2, NT])
        sig = st.sb("sig", [P, 2, NT])
        cos = st.sb("cos", [P, NT])
        sin = st.sb("sin", [P, NT])
        res = st.sb("res", [P, 2, NT])
        taps = st.sb("taps", [P, QK // P, CW + 1])
        tap_rows = st.sb("tap_rows", [CW + 1, QK])
        buf_rows = st.sb("buf_rows", [DB * (CW - 1), QK])
        bufT = st.sb("bufT", [P, QK // P, DB * (CW - 1)])
        tail = st.sb("tail", [P, 2, CW - 1 + DB * (CW - 1)])
        tail_rows = st.sb("tail_rows", [(DB + 1) * (CW - 1), QK])
        vst = st.sb("vst", [P, 2, 2 * DK])
        gst = st.sb("gst", [P, 2, DK])
        ez = st.sb("ez", [P, 2, DK])
        gnb = st.sb("gnb", [P, DK])
        gate_bias = st.sb("gate_bias", [H, 2])
        col = [st.ps(f"col{i}", [P, 3, 512]) for i in range(2)]
        row = st.ps("row", [P, 2, 512])
        s_const, s_wg, s_tr, s_tr2, s_gate = (st.sem(n) for n in ("const", "wg", "tr", "tr2", "gate"))
        s_wqk, s_wvz, qk_used, vz_used = (st.sem(n) for n in ("wqk", "wvz", "qk_used", "vz_used"))
        tile_ready, tile_taken, row_ready = (st.sem(n) for n in ("tile_ready", "tile_taken", "row_ready"))
        raw_ready, raw_free, acc_ready, sig_ready = (st.sem(n) for n in ("raw_ready", "raw_free", "acc_ready", "sig_ready"))
        res_ready, tail_ready, tail_turned, tail_saved = (st.sem(n) for n in ("res_ready", "tail_ready", "tail_turned", "tail_saved"))
        v_taken, e_ready, z_taken = st.sem("v_taken"), st.sem("e_ready"), st.sem("z_taken")
        s_gnb, gnb_used = st.sem("gnb"), st.sem("gnb_used")
        res_stored, v_stored, g_stored = st.sems("res_stored", 2), st.sems("v_stored", 2), st.sems("g_stored", 2)
        s_end = st.sem("end")
        dve_chain, act_chain, pool_chain = st.sem("dve_chain"), st.sem("act_chain"), st.sem("pool_chain")
        HEADS = 2 * H
        NR = CW - 1

        def head_loop(eng, body):
            with eng.Fori(0, H) as m:
                body(m, m, True)
            with eng.Fori(H, HEADS) as m:
                body(m, m - H, False)

        def v_count(m, b):
            per = (NB + 2 - b % 2) // 2
            return m * (16 * per) + (b // 2 + 1) * 16

        with nc.Block() as block:

            @block.sync
            def _(sp):
                sp.dma_start(wg[:], w[:, :, OFF_GATE:OFF_GATE + 2 * H]).then_inc(s_wg, 16)
                sp.dma_start(gate_bias[:, 0:1], g["b_gate_i"].rearrange("a h -> h a")).then_inc(s_wg, 16)
                sp.dma_start(gate_bias[:, 1:2], g["b_gate_f"].rearrange("a h -> h a")).then_inc(s_wg, 16)
                sp.dma_start(tap_rows[0:CW, :], g["conv_w"][0]).then_inc(s_const, 16)
                sp.dma_start(tap_rows[CW:CW + 1, :], g["conv_b"]).then_inc(s_const, 16)
                sp.dma_start(buf_rows[:], g["state_mlstm_conv"].rearrange("a b r n -> (a b r) n")).then_inc(s_const, 16)
                sp.dma_start(cos[:], c.tab["cos0"]).then_inc(s_const, 16)
                sp.dma_start(sin[:], c.tab["sin0"]).then_inc(s_const, 16)

                def load_qk(m, h, base):
                    wait_counted(sp, qk_used, m + 1)
                    for q in range(2):
                        sp.dma_start(wqk[:, :, q * DK:(q + 1) * DK],
                                     w[:, :, bass.ds(h * DK + (base + q * D), DK)]).then_inc(s_wqk, 16)

                def load_vz(m, h, base, gn):
                    wait_counted(sp, vz_used, m + 1)
                    for q in range(2):
                        sp.dma_start(wvz[:, :, q * DK:(q + 1) * DK],
                                     w[:, :, bass.ds(h * DK + (base + (2 + q) * D), DK)]).then_inc(s_wvz, 16)
                    wait_counted(sp, gnb_used, m + 1)
                    sp.dma_start(gnb[:], gn[0, bass.ds(h, 1), :].broadcast_to([P, DK])).then_inc(s_gnb, 16)

                def store_tiles(m, h, first_tile):
                    for j in range(4):
                        wait_counted(sp, res_ready, m * 4 + (j + 1))
                        tile = first_tile + (j // 2) * (D // P) + j % 2
                        sp.dma_start(c.s_qk[bass.ds(h * 2 + tile, 1)].rearrange("a p t -> (a p) t"), res[:, j % 2, :]).then_inc(res_stored[j % 2], 16)

                def store_rows(m):
                    at = bass.ds(m * DK, DK)
                    for b in range(NB + 1):
                        n, s = rows_of(b), b % 2
                        wait_counted(sp, v_taken, m * (NB + 1) + (b + 3))
                        sp.dma_start(c.s_v[b * P:b * P + n, at], vst[0:n, s, 0:DK]).then_inc(v_stored[s], 16)
                        wait_counted(sp, z_taken, m * (NB + 1) + (b + 3))
                        sp.dma_start(c.s_g[b * P:b * P + n, at], gst[0:n, s, :]).then_inc(g_stored[s], 16)

                load_qk(0, 0, 0)
                load_vz(0, 0, 0, g["gn_mlstm"])
                store_tiles(0, 0, 0)
                with sp.Fori(1, H) as m:
                    load_qk(m, m, 0)
                    store_rows(m - 1)
                    load_vz(m, m, 0, g["gn_mlstm"])
                    store_tiles(m, m, 0)
                with sp.Fori(H, HEADS) as m:
                    load_qk(m, m - H, OFF_RET)
                    store_rows(m - 1)
                    load_vz(m, m - H, OFF_RET, g["gn_ret"])
                    store_tiles(m, m - H, QK // P)
                store_rows(HEADS - 1)
                for s in range(2):
                    sp.wait_ge(res_stored[s], 16 + 32 * HEADS)
                    sp.wait_ge(v_stored[s], 16 + 16 * HEADS * ((NB + 2 - s) // 2))
                    sp.wait_ge(g_stored[s], 16 + 16 * HEADS * ((NB + 2 - s) // 2))
                sp.wait_ge(tail_saved, 4 * H)
                sp.dma_start(c.out["conv_p"][0, 0], tail_rows[0:NR, :]).then_inc(s_end, 16)
                sp.dma_start(c.out["conv_s"].rearrange("a b r n -> (a b r) n"),
                             tail_rows[NR:NR + DB * NR, :]).then_inc(s_end, 16)
                sp.wait_ge(s_end, 32)

            @block.tensor
            def _(pe):
                pe.wait_ge(s_const, 80)
                n = QK // P
                for t in range(n):
                    last = pe.transpose(row[:, 0, t * (CW + 1):(t + 1) * (CW + 1)],
                                        tap_rows[:, t * P:(t + 1) * P], c.ident[0:CW + 1, 0:CW + 1])
                for t in range(n):
                    last = pe.transpose(row[:, 1, t * DB * NR:(t + 1) * DB * NR],
                                        buf_rows[:, t * P:(t + 1) * P], c.ident[0:DB * NR, 0:DB * NR])
                last.then_inc(s_tr, 1)
                pe.wait_ge(s_wg, 48)
                for q in range(2):
                    for r, (t0, tn) in enumerate(HALVES):
                        for k in range(KD):
                            last = pe.matmul(col[q][0:H, r, 0:tn], wg[:, k, q * H:(q + 1) * H],
                                             c.hT[:, k, t0:t0 + tn], start=k == 0, stop=k == KD - 1)
                last.then_inc(s_gate, 1)
                pe.wait_ge(s_tr2, 4)

                def body(m, h, mlstm):
                    pe.wait_ge(s_wqk, m * 32 + 32)
                    for j in range(4):
                        pe.wait_ge(tile_taken, m * 4 + (j + 1))
                        for r, (t0, tn) in enumerate(HALVES):
                            for k in range(KD):
                                last = pe.matmul(col[j % 2][:, r, 0:tn], wqk[:, k, j * P:(j + 1) * P],
                                                 c.hT[:, k, t0:t0 + tn], start=k == 0, stop=k == KD - 1)
                        last.then_inc(tile_ready, 1)
                        if mlstm and j > 0:
                            turn_tail(m, j - 1)
                    last = None
                    pe.wait_ge(s_wvz, m * 32 + 32)
                    for b in range(NB + 1):
                        pe.wait_ge(v_taken, m * (NB + 1) + (b + 1))
                        for k in range(KD):
                            last = pe.matmul(row[0:rows_of(b), b % 2, :], c.hT[:, k, b * P:b * P + rows_of(b)],
                                             wvz[:, k, :], start=k == 0, stop=k == KD - 1)
                        last.then_inc(row_ready, 1)
                        if mlstm and b == 0:
                            turn_tail(m, 3)

                def turn_tail(m, j):
                    pe.wait_ge(tail_ready, m * 4 + (j + 1))
                    pe.transpose(col[j % 2][0:(DB + 1) * NR, 2, P:2 * P], tail[:, j % 2, :], c.ident[:]).then_inc(tail_turned, 1)

                head_loop(pe, body)

            @block.scalar
            def _(act):
                act.wait_ge(s_gate, 1)
                for q in range(2):
                    for r, (t0, tn) in enumerate(HALVES):
                        last = act.activation(gates[:, q, t0:t0 + tn], col[q][0:H, r, 0:tn], ACT.Identity,
                                              bias=gate_bias[:, q:q + 1])
                    last.then_inc(s_tr2, 1)

                def copy_tile(m, j):
                    s = j % 2
                    act.wait_ge(tile_ready, m * 4 + (j + 1))
                    act.wait_ge(raw_free, m * 4 + (j + 1))
                    for r in range(2):
                        act.activation(raw[:, s, NR + r * 512:NR + r * 512 + 512], col[s][:, r, :], ACT.Copy)
                    act.activation(raw[:, s, NR + T:].rearrange("p (b t) -> p b t", b=DB)[:, :, NR:],
                                   col[s][:, 2, 0:S].rearrange("p (b t) -> p b t", b=DB), ACT.Copy).then_inc(raw_ready, 1)

                def body(m, h, mlstm):
                    for j in range(4):
                        copy_tile(m, j)
                        if mlstm:
                            if j > 0:
                                sigmoid_exp(m, j - 1)
                    if mlstm:
                        sigmoid_exp(m, 3)
                    for b in range(NB + 1):
                        n = rows_of(b)
                        s = b % 2
                        act.wait_ge(row_ready, m * (NB + 1) + (b + 1))
                        act.wait_ge(z_taken, m * (NB + 1) + (b + 1))
                        act.activation(ez[0:n, s, :], row[0:n, s, DK:], ACT.Exp, scale=-1.0).then_inc(e_ready, 1)
                        act.wait_ge(v_stored[s], v_count(m, b))
                        act.activation(vst[0:n, s, :], row[0:n, s, :], ACT.Copy).then_inc(v_taken, 1)

                def sigmoid_exp(m, j):
                    act.wait_ge(acc_ready, m * 4 + (j + 1))
                    act.activation(sig[:, j % 2, :], acc[:, j % 2, :], ACT.Exp, scale=-1.0).then_inc(sig_ready, 1)

                head_loop(act, body)

            @block.vector
            def _(dve):
                ch = Chain(dve, dve_chain)
                dve.wait_ge(s_tr, 1)
                dve.tensor_copy(taps[:], row[:, 0, 0:(QK // P) * (CW + 1)].rearrange("p (t n) -> p t n", n=CW + 1)).then_inc(s_tr2, 1)
                dve.tensor_copy(bufT[:], row[:, 1, 0:(QK // P) * DB * NR].rearrange("p (t n) -> p t n", n=DB * NR)).then_inc(s_tr2, 1)
                dve.memset(raw[:, :, 0:NR], 0.0)
                dve.wait_ge(s_tr2, 4)
                dve.sem_inc(tile_taken, 2)
                dve.sem_inc(raw_free, 2)
                dve.sem_inc(v_taken, 2)
                dve.sem_inc(z_taken, 2)
                dve.sem_inc(qk_used, 1)
                dve.sem_inc(vz_used, 1)
                dve.sem_inc(gnb_used, 1)
                for s in range(2):
                    for q in (res_stored, v_stored, g_stored):
                        dve.sem_inc(q[s], 16)

                def z_rows(m, h):
                    dve.wait_ge(s_gnb, m * 16 + 16)
                    for b in range(NB + 1):
                        n, s = rows_of(b), b % 2
                        dve.wait_ge(e_ready, m * (NB + 1) + (b + 1))
                        e = ez[0:n, s, :]
                        ch.link(dve.tensor_scalar(e, e, 1.0, None, ALU.add))
                        ch.link(dve.reciprocal(e, e))
                        dve.wait_ge(v_taken, m * (NB + 1) + (b + 3))
                        ch.link(dve.tensor_tensor(e, vst[0:n, s, DK:], e, ALU.mult))
                        dve.wait_ge(g_stored[s], v_count(m, b))
                        last = dve.tensor_tensor(gst[0:n, s, :], e, gnb[0:n, :], ALU.mult)
                        ch.link(last)
                        dve.sem_inc(z_taken, 1)
                    dve.sem_inc(gnb_used, 1)
                    dve.sem_inc(vz_used, 1)

                def conv(m, h):
                    for j in range(4):
                        s = j % 2
                        tile = (j // 2) * (D // P) + j % 2
                        dve.wait_ge(raw_ready, m * 4 + (j + 1))
                        if j == 3:
                            dve.sem_inc(qk_used, 1)
                        r = raw[:, s, :]
                        rs = r[:, NR + T:].rearrange("p (b t) -> p b t", b=DB)
                        ch.link(dve.tensor_copy(rs[:, :, 0:NR], bufT[:, bass.ds(h * 2 + tile, 1), :].rearrange("p a (b t) -> p (a b) t", b=DB)))
                        ch.link(dve.tensor_copy(tail[:, s, 0:NR], r[:, T:T + NR]))
                        dve.tensor_copy(tail[:, s, NR:].rearrange("p (b t) -> p b t", b=DB), rs[:, :, DS:]).then_inc(tail_ready, 1)
                        a = acc[:, s, 0:T]
                        a_s = acc[:, s, T:].rearrange("p (b t) -> p b t", b=DB)
                        cw = taps[:, bass.ds(h * 2 + tile, 1), :].rearrange("p a n -> p (a n)")
                        dve.tensor_scalar(a, r[:, 0:T], cw[:, 0:1], cw[:, CW:CW + 1], ALU.mult, ALU.add)
                        ch.link(dve.tensor_scalar(a_s, rs[:, :, 0:DS], cw[:, 0:1], cw[:, CW:CW + 1], ALU.mult, ALU.add))
                        for k in range(1, CW):
                            dve.scalar_tensor_tensor(out=a, in0=r[:, k:k + T], scalar=cw[:, k:k + 1], in1=a, op0=ALU.mult, op1=ALU.add)
                            ch.link(dve.scalar_tensor_tensor(out=a_s, in0=rs[:, :, k:k + DS], scalar=cw[:, k:k + 1], in1=a_s,
                                                             op0=ALU.mult, op1=ALU.add))
                        dve.sem_inc(acc_ready, 1)
                        dve.sem_inc(raw_free, 1)
                        if j > 0:
                            silu(m, j - 1)
                        save_tail(m, h, j)
                    silu(m, 3)

                def save_tail(m, h, j):
                    tile = (j // 2) * (D // P) + j % 2
                    dve.wait_ge(tail_turned, m * 4 + (j + 1))
                    ch.link(dve.tensor_copy(tail_rows[:, bass.ds((h * 2 + tile) * P, P)], col[j % 2][0:(DB + 1) * NR, 2, P:2 * P]))
                    dve.sem_inc(tail_saved, 1)
                    dve.sem_inc(tile_taken, 1)

                def silu(m, j):
                    s = j % 2
                    dve.wait_ge(sig_ready, m * 4 + (j + 1))
                    e = sig[:, s, :]
                    ch.link(dve.tensor_scalar(e, e, 1.0, None, ALU.add))
                    ch.link(dve.reciprocal(e, e))
                    dve.wait_ge(res_stored[s], m * 32 + (j // 2 + 1) * 16)
                    ch.link(dve.scalar_tensor_tensor(out=res[:, s, :], in0=acc[:, s, :], scalar=DK ** -0.5 if j < 2 else 1.0,
                                                     in1=e, op0=ALU.mult, op1=ALU.mult))
                    dve.sem_inc(res_ready, 1)

                def rotate(m, h):
                    for pair in range(2):
                        dve.wait_ge(raw_ready, m * 4 + (2 * pair + 2))
                        dve.sem_inc(tile_taken, 2)
                        if pair == 1:
                            dve.sem_inc(qk_used, 1)
                        scale = 1.0 if pair == 0 else DK ** -0.5
                        for out, x, table in ((0, 0, cos), (1, 0, sin)):
                            for part in range(2):
                                o, i = spans(part, acc[:, out, :], raw[:, x, :])
                                dve.scalar_tensor_tensor(out=o, in0=i, scalar=scale, in1=spans(part, table[:, :])[0], op0=ALU.mult, op1=ALU.mult)
                        for out, x, table in ((0, 1, sin), (1, 1, cos)):
                            for part in range(2):
                                o, i = spans(part, sig[:, out, :], raw[:, x, :])
                                last = dve.scalar_tensor_tensor(out=o, in0=i, scalar=scale, in1=spans(part, table[:, :])[0], op0=ALU.mult, op1=ALU.mult)
                        ch.link(last)
                        dve.sem_inc(raw_free, 2)
                        for s, op in ((0, ALU.subtract), (1, ALU.add)):
                            dve.wait_ge(res_stored[s], m * 32 + (pair + 1) * 16)
                            ch.link(dve.tensor_tensor(res[:, s, :], acc[:, s, :], sig[:, s, :], op))
                            dve.sem_inc(res_ready, 1)

                def spans(part, o, i=None):
                    if part == 0:
                        return o[:, 0:T], None if i is None else i[:, NR:NR + T]
                    o = o[:, T:NT].rearrange("p (b t) -> p b t", b=DB)
                    return o, None if i is None else i[:, NR + T:].rearrange("p (b t) -> p b t", b=DB)[:, :, NR:]

                def body(m, h, mlstm):
                    ch.clear()
                    if mlstm:
                        conv(m, h)
                    else:
                        rotate(m, h)
                    z_rows(m, h)

                head_loop(dve, body)


A, EM, WS = range(3)
MPREV, SCALE = range(2)


def gate_rows(c, gates, rows, cols, spread):
    nc = c.nc
    NCH = NB + DB
    with Stage(nc, "gr") as st:
        reset = st.sb("reset", [H, NT])
        first = st.sb("first", [H, DB, DS + 1])
        ext = st.sb("ext", [H, DB, DS + 1])
        mext = st.sb("mext", [H, DB, DS + 1])
        zeros = st.sb("zeros", [H, P])
        ones = st.sb("ones", [H, P])
        b = st.sb("b", [H, NT])
        a = st.sb("a", [H, NT])
        M = st.sb("M", [H, NT])
        em = st.sb("em", [H, NT])
        ws = st.sb("ws", [H, NT])
        mp = st.sb("mp", [H, NCH + 1])
        ml = st.sb("ml", [H, NCH])
        bl = st.sb("bl", [H, NCH])
        mnew = st.sb("mnew", [H, DB])
        sc = st.sb("sc", [H, NCH])
        diag = st.sb("diag", [H, 2, NCH, H])
        pt = st.ps("pt", [P, 512])
        pb = st.ps("pb", [P, 512])
        s_in, s_dve, s_act, s_pe, s_out = (st.sem(n) for n in ("in", "dve", "act", "pe", "out"))
        dve_chain, logs_ready = st.sem("dve_chain"), st.sem("logs_ready")

        def by_chunk(x, prompt):
            return x[:, 0:T].rearrange("h (n t) -> h n t", t=P) if prompt else x[:, T:].rearrange("h (n t) -> h n t", t=DS)

        with nc.Block() as block:

            @block.sync
            def _(sp):
                sp.dma_start(reset[:], c.tab["reset"]).then_inc(s_in, 16)
                sp.dma_start(first[:], c.tab["first"].rearrange("h (b t) -> h b t", b=DB)).then_inc(s_in, 16)
                sp.dma_start(ones[:], c.tab["ones4"]).then_inc(s_in, 16)
                sp.dma_start(mp[:, NB:NCH], c.x["state_mlstm_m"][0].rearrange("b h -> h b"), allow_slow_non_contiguous=True).then_inc(s_in, 16)
                sp.wait_ge(s_dve, 1)
                sp.dma_start(c.out["m_p"].rearrange("a b h -> h (a b)"), mp[:, NCH:NCH + 1]).then_inc(s_out, 16)
                sp.dma_start(c.out["m_s"][0].rearrange("b h -> h b"), mnew[:], allow_slow_non_contiguous=True).then_inc(s_out, 16)
                sp.wait_ge(s_out, 32)

            @block.vector
            def _(dve):
                ch = Chain(dve, dve_chain)
                f = gates[:, 1, :]
                ch.link(dve.scalar_tensor_tensor(out=b[:], in0=f, scalar=-1.0, in1=f, op0=ALU.mult, op1=ALU.min))
                dve.sem_inc(logs_ready, 1)
                ch.link(dve.memset(zeros[:], 0.0))
                dve.wait_ge(s_act, 2)
                ch.link(dve.scalar_tensor_tensor(out=f, in0=f, scalar=0.0, in1=b[:], op0=ALU.min, op1=ALU.subtract))
                dve.wait_ge(s_in, 64)
                ch.link(dve.tensor_tensor_scan(b[:], reset[:], f, 0.0, ALU.mult, ALU.add))
                ch.link(dve.tensor_tensor(a[:], gates[:, 0, :], b[:], ALU.subtract))
                ch.link(dve.tensor_copy(ext[:, :, 0:1], mp[:, NB:NCH].unsqueeze(2)))
                ch.link(dve.tensor_copy(ext[:, :, 1:], by_chunk(a, False)))
                flat = "h b t -> h (b t)"
                ch.link(dve.tensor_tensor_scan(mext[:].rearrange(flat), first[:].rearrange(flat), ext[:].rearrange(flat), 0.0, ALU.add, ALU.max))
                ch.link(dve.tensor_copy(by_chunk(M, False), mext[:, :, 1:]))
                for prompt, n0, n1 in ((True, 0, NB), (False, NB, NCH)):
                    ch.link(dve.tensor_copy(bl[:, n0:n1].unsqueeze(2), by_chunk(b, prompt)[:, :, -1:]))
                ch.link(dve.tensor_copy(ml[:, NB:].unsqueeze(2), mext[:, :, DS:]))
                ch.link(dve.memset(mp[:, 0:1], 0.0))
                for n in range(NB):
                    ch.link(dve.tensor_tensor_scan(M[:, n * P:(n + 1) * P], zeros[:], a[:, n * P:(n + 1) * P],
                                                   mp[:, n:n + 1], ALU.add, ALU.max))
                    ch.link(dve.tensor_copy(ml[:, n:n + 1], M[:, n * P + P - 1:n * P + P]))
                    after = n + 1 if n < NB - 1 else NCH
                    ch.link(dve.tensor_tensor(mp[:, after:after + 1], ml[:, n:n + 1], bl[:, n:n + 1], ALU.add))
                ch.link(dve.tensor_tensor(mnew[:], ml[:, NB:], bl[:, NB:], ALU.add))
                dve.sem_inc(s_dve, 1)
                ch.link(dve.tensor_scalar(rows[:, 0, :], M[:], -1.0, None, ALU.mult))
                ch.link(dve.tensor_tensor(em[:], rows[:, 0, :], b[:], ALU.subtract))
                for prompt, n0, n1, w in ((True, 0, NB, P), (False, NB, NCH, DS)):
                    shape = [H, n1 - n0, w]
                    ch.link(dve.tensor_tensor(by_chunk(rows[:, 1, :], prompt), by_chunk(rows[:, 0, :], prompt),
                                              mp[:, n0:n1].unsqueeze(2).broadcast_to(shape), ALU.add))
                    ch.link(dve.tensor_tensor(by_chunk(ws, prompt), by_chunk(a, prompt),
                                              ml[:, n0:n1].unsqueeze(2).broadcast_to(shape), ALU.subtract))
                ch.link(dve.tensor_tensor(sc[:], mp[:, 0:NCH], ml[:], ALU.subtract))
                dve.sem_inc(logs_ready, 1)
                dve.wait_ge(s_act, 3)
                for q, x in ((MPREV, mp[:, 0:NCH]), (SCALE, sc[:])):
                    last = dve.tensor_tensor(diag[:, q], x.unsqueeze(2).broadcast_to([H, NCH, H]),
                                             c.ident[0:H, 0:H].unsqueeze(1).broadcast_to([H, NCH, H]), ALU.mult)
                ch.link(last)
                dve.sem_inc(s_dve, 1)
                dve.wait_ge(s_pe, 1)
                dve.tensor_copy(cols[:, 0:NB], pt[:, 0:NB * 3 * H].rearrange("p (n q h) -> p n q h", n=NB, q=3))
                dve.tensor_copy(cols[0:S, NB], pt[0:S, NB * 3 * H:(NB + 1) * 3 * H].rearrange("p (q h) -> p q h", q=3))
                ch.link(dve.tensor_copy(spread[:], pb[:, 0:2 * NCH * H].rearrange("p (q n h) -> p q n h", q=2, n=NCH)))

            @block.scalar
            def _(act):
                act.wait_ge(logs_ready, 1)
                act.activation(b[:], b[:], ACT.Exp).then_inc(s_act, 1)
                act.wait_ge(s_act, 1)
                act.activation(b[:], b[:], ACT.Ln, bias=1.0).then_inc(s_act, 1)
                act.wait_ge(logs_ready, 2)
                act.activation(rows[:, 1, :], rows[:, 1, :], ACT.Exp)
                act.activation(em[:], em[:], ACT.Exp)
                act.activation(ws[:], ws[:], ACT.Exp)
                act.activation(sc[:], sc[:], ACT.Exp).then_inc(s_act, 1)

            @block.tensor
            def _(pe):
                pe.wait_ge(s_dve, 2)
                for n in range(NB + 1):
                    for q, x in ((A, a), (EM, em), (WS, ws)):
                        pe.transpose(pt[0:rows_of(n), (n * 3 + q) * H:(n * 3 + q + 1) * H],
                                     x[:, n * P:n * P + rows_of(n)], c.ident[0:H, 0:H])
                pe.matmul(pb[:, 0:2 * NCH * H], ones[:], diag[:].rearrange("h q n k -> h (q n k)"), start=True, stop=True).then_inc(s_pe, 1)


class Tail:

    def __init__(self, c, st, width, y, w_out, banks, junk, layer):
        self.c, self.ky, self.y, self.w, self.banks, self.layer = c, width // P, y, w_out, banks, layer
        self.last = layer == 1
        self.yT = st.sb("yT", [P, self.ky, P])
        self.res = st.sb("res", [P, D])
        self.x1 = st.sb("x1", [P, D])
        self.post = st.sb("post", [P, D])
        self.gcol = st.sb("gcol", [P, KD])
        self.grow = st.sb("grow", [KD, P])
        self.ss = st.sb("ss", [P, 4])
        self.half = st.sb("half", [P, 8])
        self.junk = junk
        self.norms_loaded, self.w_loaded, self.y_turned, self.yT_copied = (st.sem(n) for n in ("norms_loaded", "w_loaded", "y_turned", "yT_copied"))
        self.out_ready, self.out_squared, self.out_summed, self.rooted = (st.sem(n) for n in ("out_ready", "out_squared", "out_summed", "rooted"))
        self.x1_ready, self.out_taken, self.x1_squared, self.rows_scaled = (st.sem(n) for n in ("x1_ready", "out_taken", "x1_squared", "rows_scaled"))
        self.rows_turned, self.rows_taken, self.res_loaded, self.x1_stored = (st.sem(n) for n in ("rows_turned", "rows_taken", "res_loaded", "x1_stored"))
        self.tail_chain, self.tail_pool, self.gcol_turned = (st.sem(n) for n in ("tail_chain", "tail_pool", "gcol_turned"))

    def load_constants(self, sp):
        g = self.c.x
        sp.dma_start(self.post[:], g["norm_post"][self.layer:self.layer + 1, :].broadcast_to([P, D])).then_inc(self.norms_loaded, 16)
        if not self.last:
            sp.dma_start(self.grow[:], g["norm_pre"][1, :].rearrange("(k p) -> k p", p=P)).then_inc(self.norms_loaded, 16)

    def norms_wait(self, eng):
        eng.wait_ge(self.norms_loaded, 16 if self.last else 32)

    def pe_start(self, pe):
        if not self.last:
            self.norms_wait(pe)
            pe.transpose(self.banks[6][:, 0:KD], self.grow[:], self.c.ident[0:KD, 0:KD]).then_inc(self.gcol_turned, 1)

    def dve_start(self, dve):
        if not self.last:
            dve.wait_ge(self.gcol_turned, 1)
            dve.tensor_copy(self.gcol[:], self.banks[6][:, 0:KD]).then_inc(self.tail_chain, 1)
            dve.wait_ge(self.tail_chain, 1)
            dve.sem_clear(self.tail_chain)
        dve.sem_inc(self.out_taken, 1)
        dve.sem_inc(self.rows_taken, 1)

    def pool_start(self, pool):
        pool.memset(self.half[:], -0.5).then_inc(self.tail_pool, 1)
        pool.wait_ge(self.tail_pool, 1)
        pool.sem_clear(self.tail_pool)

    def pe(self, pe, n, rows, y_wait):
        y_wait()
        for k in range(self.ky):
            last = pe.transpose(self.banks[k // 4][:, (k % 4) * P:(k % 4) * P + rows],
                                self.y[0:rows, k * P:(k + 1) * P], self.c.ident[0:rows, 0:rows])
        last.then_inc(self.y_turned, 1)
        pe.wait_ge(self.yT_copied, (n + 1) * (self.ky // 4))
        pe.wait_ge(self.w_loaded, 16)
        pe.wait_ge(self.out_taken, n + 1)
        for f in range(2):
            for k in range(self.ky):
                last = pe.matmul(self.banks[4 + f][0:rows, :], self.yT[:, k, 0:rows], self.w[:, k, f * 512:(f + 1) * 512],
                                 start=k == 0, stop=k == self.ky - 1)
        last.then_inc(self.out_ready, 1)
        if self.last:
            return
        pe.wait_ge(self.rows_scaled, n + 1)
        pe.wait_ge(self.rows_taken, n + 1)
        for k in range(KD):
            last = pe.transpose(self.banks[6 + k // 4][:, (k % 4) * P:(k % 4) * P + rows],
                                self.res[0:rows, k * P:(k + 1) * P], self.c.ident[0:rows, 0:rows])
        last.then_inc(self.rows_turned, 1)

    def copy_bank(self, eng, n, rows, b):
        eng.wait_ge(self.y_turned, n + 1)
        o = self.yT[:, 4 * b:4 * b + 4, 0:rows]
        i = self.banks[b].rearrange("p (k t) -> p k t", t=P)[:, :, 0:rows]
        if b % 2 == 0:
            eng.activation(o, i, ACT.Copy).then_inc(self.yT_copied, 1)
        else:
            eng.tensor_copy(o, i).then_inc(self.yT_copied, 1)

    def act(self, act, n, rows, x1_out):
        for b in range(0, self.ky // 4, 2):
            self.copy_bank(act, n, rows, b)
        act.wait_ge(self.out_ready, n + 1)
        for f in range(2):
            last = act.activation(self.junk[0:rows, f, :], self.banks[4 + f][0:rows, :], ACT.Square, accum_out=self.ss[0:rows, f:f + 1])
        last.then_inc(self.out_squared, 1)
        act.wait_ge(self.x1_ready, n + 1)
        act.dma_start(x1_out, self.x1[0:rows, :]).then_inc(self.x1_stored, 16)
        if self.last:
            return
        for f in range(2):
            last = act.activation(self.junk[0:rows, f, :], self.x1[0:rows, f * 512:(f + 1) * 512], ACT.Square,
                                  accum_out=self.ss[0:rows, f:f + 1])
        last.then_inc(self.x1_squared, 1)
        act.wait_ge(self.rooted, 2 * n + 2)
        act.activation(self.res[0:rows, :], self.x1[0:rows, :], ACT.Copy, scale=self.ss[0:rows, 3:4]).then_inc(self.rows_scaled, 1)

    def pool(self, pool, n, rows):
        for i in range(1 if self.last else 2):
            wait_counted(pool, self.out_summed, n + 1 if self.last else 2 * n + (i + 1))
            pool.tensor_scalar(self.ss[0:rows, 2:3], self.ss[0:rows, 2:3], 1.0 / D, EPS, ALU.mult, ALU.add).then_inc(self.tail_pool, 1)
            pool.wait_ge(self.tail_pool, 1)
            pool.tensor_tensor(self.ss[0:rows, 3:4], self.ss[0:rows, 2:3], self.half[0:rows, 0:1], ALU.pow).then_inc(self.tail_pool, 1)
            pool.wait_ge(self.tail_pool, 2)
            pool.sem_clear(self.tail_pool)
            pool.sem_inc(self.rooted, 1)

    def dve(self, dve, n, rows, token):
        ch = Chain(dve, self.tail_chain)
        for b in range(1, self.ky // 4, 2):
            self.copy_bank(dve, n, rows, b)
        dve.wait_ge(self.out_squared, n + 1)
        dve.tensor_tensor(self.ss[0:rows, 2:3], self.ss[0:rows, 0:1], self.ss[0:rows, 1:2], ALU.add).then_inc(self.out_summed, 1)
        dve.wait_ge(self.rooted, n + 1 if self.last else 2 * n + 1)
        self.norms_wait(dve)
        dve.wait_ge(self.x1_stored, n * 16 + 16)
        for f in range(2):
            cols = slice(f * 512, (f + 1) * 512)
            last = dve.scalar_tensor_tensor(out=self.x1[0:rows, cols], in0=self.banks[4 + f][0:rows, :], scalar=self.ss[0:rows, 3:4],
                                            in1=self.post[0:rows, cols], op0=ALU.mult, op1=ALU.mult)
        ch.link(last)
        dve.sem_inc(self.out_taken, 1)
        dve.wait_ge(self.res_loaded, n * 16 + 16)
        ch.link(dve.tensor_tensor(self.x1[0:rows, :], self.x1[0:rows, :], self.res[0:rows, :], ALU.add))
        dve.sem_inc(self.x1_ready, 1)
        ch.clear()
        if self.last:
            return
        dve.wait_ge(self.x1_squared, n + 1)
        dve.tensor_tensor(self.ss[0:rows, 2:3], self.ss[0:rows, 0:1], self.ss[0:rows, 1:2], ALU.add).then_inc(self.out_summed, 1)
        dve.wait_ge(self.rows_turned, n + 1)
        for b in range(2):
            last = dve.tensor_tensor(self.c.hT[:, 4 * b:4 * b + 4, token],
                                     self.banks[6 + b].rearrange("p (k t) -> p k t", t=P)[:, :, 0:rows],
                                     self.gcol[:, 4 * b:4 * b + 4].unsqueeze(2).broadcast_to([P, 4, rows]), ALU.mult)
        last.then_inc(self.rows_taken, 1)


def apply_norms(dve, ch, n, hn, ssq, inv, fac, fac2, em, sums_ready, wait_rooted, wait_gates, y):
    HH = 2 * H
    den = hn[0:n, 0:H, DK:DK + 1].rearrange("p h a -> p (h a)")
    ch.link(dve.scalar_tensor_tensor(out=inv[0:n, 0:H], in0=den, scalar=-1.0, in1=den, op0=ALU.mult, op1=ALU.max))
    ch.link(dve.tensor_tensor(inv[0:n, 0:H], inv[0:n, 0:H], em, ALU.max))
    ch.link(dve.reciprocal(inv[0:n, 0:H], inv[0:n, 0:H]))
    f = fac[0:n, :]
    ch.link(dve.tensor_tensor(f, ssq[0:n, :], inv[0:n, :], ALU.mult))
    ch.link(dve.tensor_tensor(f, f, inv[0:n, :], ALU.mult))
    ch.link(dve.tensor_scalar(f, f, 1.0 / DK, EPS, ALU.mult, ALU.add))
    dve.sem_inc(sums_ready, 1)
    wait_rooted()
    ch.link(dve.tensor_tensor(f, fac2[0:n, :], inv[0:n, :], ALU.mult))
    wait_gates()
    for j in range(HH):
        yj = y[0:n, j * DK:(j + 1) * DK]
        last = dve.scalar_tensor_tensor(out=yj, in0=hn[0:n, j, 0:DK], scalar=fac[0:n, j:j + 1], in1=yj, op0=ALU.mult, op1=ALU.mult)
    ch.link(last)


def mix_prompt(c, rows, cols, spread):
    nc, g = c.nc, c.x
    VX = DK + 1
    with Stage(nc, "mp") as st:
        qk = st.sb("qk", [P, 2 * QK // P, P])
        vx = st.sb("vx", [P, 2 * H, VX])
        y = st.sb("y", [P, 2 * D])
        state = st.sb("state", [P, 2 * H, 2, VX])
        hn = st.sb("hn", [P, 2 * H, VX])
        kw = st.sb("kw", [P, 2 * H, DK])
        wt = st.sb("wt", [P, 2, H, P])
        decay = st.sb("decay", [P, H, P])
        gin = st.sb("gin", [P, H, P])
        kout = st.sb("kout", [P, H])
        mask = st.sb("mask", [P, P])
        select = st.sb("select", [H, H, P])
        w_out = st.sb("w_out", [P, 2 * D // P, D])
        ssq = st.sb("ssq", [P, 2 * H])
        inv = st.sb("inv", [P, 2 * H])
        fac = st.sb("fac", [P, 2 * H])
        fac2 = st.sb("fac2", [P, 2 * H])
        junk = st.sb("junk2", [P, 2, DK])
        banks = [st.ps(f"bank{i}", [P, 512]) for i in range(8)]
        bA, bB, bKN, bNUM, bCU = banks[0], banks[1], banks[2:4], banks[4:6], banks[6:8]
        tail = Tail(c, st, 2 * D, y, w_out, banks, hn[:].rearrange("p j v -> p (j v)")[:, 0:D].rearrange("p (f n) -> p f n", f=2), 0)
        s_const, qk_loaded, v_loaded, g_loaded = (st.sem(n) for n in ("const", "qk_loaded", "v_loaded", "g_loaded"))
        rows_spread, masked, st_ready, wt_ready, q_scaled = (st.sem(n) for n in ("rows_spread", "masked", "st_ready", "wt_ready", "q_scaled"))
        weighed, kn_ready, kw_ready, num_ready, num_taken = (st.sem(n) for n in ("weighed", "kn_ready", "kw_ready", "num_ready", "num_taken"))
        cu_ready, updated, sums_ready, fac_rooted, y_ready = (st.sem(n) for n in ("cu_ready", "updated", "sums_ready", "fac_rooted", "y_ready"))
        chunk_done, dve_chain, pool_chain, s_end, s_start = (st.sem(n) for n in ("chunk_done", "dve_chain", "pool_chain", "end", "start"))
        HH = 2 * H

        def q_tile(j, d):
            return (j // H) * (QK // P) + (j % H) * 2 + d

        def k_tile(j, d):
            return q_tile(j, d) + D // P

        with nc.Block() as block:

            @block.sync
            def _(sp):
                sp.dma_start(mask[:], c.tab["mask_st"]).then_inc(s_const, 16)
                sp.dma_start(decay[:].rearrange("p h t -> p (h t)"), c.tab["decay"]).then_inc(s_const, 16)
                sp.dma_start(gin[:].rearrange("p h t -> p (h t)"), c.tab["gin"]).then_inc(s_const, 16)
                sp.dma_start(kout[:], c.tab["kout"]).then_inc(s_const, 16)
                sp.dma_start(select[:].rearrange("p h t -> p (h t)"), c.tab["select"]).then_inc(s_const, 16)
                tail.load_constants(sp)

                def loads(n):
                    at = bass.ds(n * P, P)
                    sp.dma_start(qk[:], c.s_qk[:, :, at].rearrange("n p t -> p n t")).then_inc(qk_loaded, 16)
                    sp.dma_start(vx[:, :, 0:DK], c.s_v[at, :].rearrange("t (h n) -> t h n", h=HH)).then_inc(v_loaded, 16)

                def late_loads(n):
                    at = bass.ds(n * P, P)
                    sp.dma_start(y[:], c.s_g[at, :]).then_inc(g_loaded, 16)
                    sp.dma_start(tail.res[:], g["x_prompt"][0, at, :]).then_inc(tail.res_loaded, 16)

                loads(0)
                late_loads(0)
                sp.dma_start(w_out[:], g["w_out_a"][0].rearrange("(k p) n -> p k n", p=P)).then_inc(tail.w_loaded, 16)
                with sp.Fori(1, NB) as n:
                    wait_counted(sp, chunk_done, n)
                    loads(n)
                    wait_counted(sp, tail.rows_turned, n)
                    late_loads(n)
                sp.wait_ge(updated, HH * NB + HH)
                for q, out in ((0, "C_p"), (1, "S_p")):
                    for d in range(2):
                        sp.dma_start(c.out[out][0, 0, :, d * P:(d + 1) * P, :].rearrange("h p v -> p h v"),
                                     state[:, q * H:(q + 1) * H, d, 0:DK]).then_inc(s_end, 16)
                for d in range(2):
                    sp.dma_start(c.out["n_p"][0, 0, :, d * P:(d + 1) * P].rearrange("h p -> p h"),
                                 state[:, 0:H, d, DK:VX].rearrange("p h a -> p (h a)"), allow_slow_non_contiguous=True).then_inc(s_end, 16)
                sp.wait_ge(s_end, 96)
                sp.wait_ge(tail.x1_stored, 16 * NB + 16)

            @block.tensor
            def _(pe):
                pe.wait_ge(s_const, 80)
                tail.pe_start(pe)
                pe.wait_ge(s_start, 1)

                def chunk(n):
                    at = bass.ds(n * P, P)
                    for q, bank in ((0, bA), (1, bB)):
                        for h in range(H):
                            last = pe.matmul(bank[:, h * P:(h + 1) * P], select[:, h, :], rows[:, q, at], start=True, stop=True)
                    last.then_inc(rows_spread, 1)
                    pe.wait_ge(qk_loaded, n * 16 + 16)
                    turn_k(n, 0)
                    pe.wait_ge(masked, n + 1)
                    scores(n, 0)
                    num(n, 0)
                    update(n, 0)
                    scores(n, 1)
                    for j in range(1, HH):
                        if j == H:
                            pe.wait_ge(kw_ready, n * HH + H)
                            turn_k(n, 1)
                        num(n, j)
                        update(n, j)
                    tail.pe(pe, n, P, lambda: pe.wait_ge(y_ready, n + 1))

                def turn_k(n, q):
                    for j in range(q * H, (q + 1) * H):
                        for d in range(2):
                            last = pe.transpose(bKN[(j % H) // 2][:, (j % 2) * DK + d * P:(j % 2) * DK + (d + 1) * P],
                                                qk[:, k_tile(j, d), :], c.ident[:])
                    last.then_inc(kn_ready, 1)

                def scores(n, q):
                    for j in range(q * H, (q + 1) * H):
                        for d in range(2):
                            last = pe.matmul(bA[:, (j % H) * P:(j % H + 1) * P], qk[:, k_tile(j, d), :], qk[:, q_tile(j, d), :],
                                             start=d == 0, stop=d == 1)
                    last.then_inc(st_ready, 1)

                def num(n, j):
                    w = VX if j < H else DK
                    q = j // H
                    if j % H == 0:
                        pe.wait_ge(v_loaded, n * 16 + 16)
                        pe.wait_ge(weighed, n * 2 + (q + 1))
                        pe.wait_ge(q_scaled, n * 2 + (q + 1))
                    pe.wait_ge(num_taken, n * HH + (j + 1))
                    if j < 2:
                        pe.wait_ge(tail.out_taken, n + 1)
                    pe.wait_ge(updated, n * HH + (j + 1))
                    out = bNUM[j % 2][:, 0:w]
                    pe.matmul(out, wt[:, q, j % H, :], vx[:, j, 0:w], start=True, stop=False)
                    pe.matmul(out, qk[:, q_tile(j, 0), :], state[:, j, 0, 0:w], start=False, stop=False)
                    pe.matmul(out, qk[:, q_tile(j, 1), :], state[:, j, 1, 0:w], start=False, stop=True).then_inc(num_ready, 1)

                def update(n, j):
                    w = VX if j < H else DK
                    pe.wait_ge(kw_ready, n * HH + (j + 1))
                    pe.wait_ge(updated, n * HH + (j + HH))
                    if j == 0:
                        pe.wait_ge(tail.rows_taken, n + 1)
                    for d in range(2):
                        last = pe.matmul(bCU[d][:, 0:w], kw[:, j, d * P:(d + 1) * P], vx[:, j, 0:w], start=True, stop=True)
                    last.then_inc(cu_ready, 1)
                    if j == HH - 1:
                        pass

                with pe.Fori(0, NB) as n:
                    chunk(n)

            @block.scalar
            def _(act):
                def chunk(n):
                    act.wait_ge(masked, n + 1)
                    for h in range(H):
                        last = act.activation(wt[:, 0, h, :], wt[:, 0, h, :], ACT.Exp,
                                              bias=cols[:, bass.ds(n, 1), A, h:h + 1].rearrange("p a b -> p (a b)"))
                    last.then_inc(wt_ready, 1)
                    rows_k(n, 0)
                    for j in range(HH):
                        if j == H:
                            rows_k(n, 1)
                        w = VX if j < H else DK
                        act.wait_ge(num_ready, n * HH + (j + 1))
                        act.activation(hn[:, j, 0:w], bNUM[j % 2][:, 0:w], ACT.Copy)
                        act.wait_ge(num_taken, n * HH + (j + 1))
                        act.activation(junk[:, j % 2, :], bNUM[j % 2][:, 0:DK], ACT.Square, accum_out=ssq[:, j:j + 1]).then_inc(num_taken, 1)
                    tail.act(act, n, P, c.s_x1[bass.ds(n * P, P), :])

                def rows_k(n, q):
                    act.wait_ge(kn_ready, 2 * n + (q + 1))
                    for j in range(q * H, (q + 1) * H):
                        scale = cols[:, bass.ds(n, 1), WS, j:j + 1].rearrange("p a b -> p (a b)") if q == 0 else kout[:, j - H:j - H + 1]
                        act.activation(kw[:, j, :], bKN[(j % H) // 2][:, (j % 2) * DK:(j % 2 + 1) * DK], ACT.Copy, scale=scale).then_inc(kw_ready, 1)

                act.wait_ge(s_const, 80)
                with act.Fori(0, NB) as n:
                    chunk(n)

            @block.gpsimd
            def _(pool):
                tail.pool_start(pool)
                with pool.Fori(0, NB) as n:
                    wait_counted(pool, sums_ready, n + 1)
                    pool.tensor_tensor(fac2[:], fac[:], tail.half[:, 0:HH], ALU.pow).then_inc(fac_rooted, 1)
                    tail.pool(pool, n, P)

            @block.vector
            def _(dve):
                ch = Chain(dve, dve_chain)
                dve.memset(vx[:, :, DK:VX], 1.0)
                dve.memset(inv[:], 1.0)
                ch.link(dve.memset(state[:], 0.0))
                tail.dve_start(dve)
                dve.sem_inc(tail.x1_stored, 16)
                dve.sem_inc(num_taken, 2)
                dve.sem_inc(updated, HH)
                dve.sem_inc(s_start, 1)
                dve.wait_ge(s_const, 80)

                def chunk(n):
                    ch.clear()
                    dve.wait_ge(rows_spread, n + 1)
                    ch.link(dve.tensor_tensor(wt[:, 0], bA[:].rearrange("p (h t) -> p h t", t=P),
                                              mask[:].unsqueeze(1).broadcast_to([P, H, P]), ALU.add))
                    dve.sem_inc(masked, 1)
                    weigh(n, 0, bB[:].rearrange("p (h t) -> p h t", t=P))
                    updates(n, 0)
                    weigh(n, 1, gin[:])
                    for j in range(1, HH):
                        updates(n, j)
                    head_norms(n)
                    dve.sem_inc(chunk_done, 1)
                    tail.dve(dve, n, P, bass.ds(n * P, P))

                def weigh(n, q, q_weight):
                    dve.wait_ge(st_ready, 2 * n + (q + 1))
                    t0 = q_tile(q * H, 0)
                    qs = qk[:, t0:t0 + 2 * H, :].rearrange("p (h d) t -> p h d t", d=2)
                    if q == 0:
                        dve.wait_ge(wt_ready, n + 1)
                    ch.link(dve.tensor_tensor(wt[:, q], bA[:].rearrange("p (h t) -> p h t", t=P),
                                              wt[:, 0] if q == 0 else decay[:], ALU.mult))
                    dve.sem_inc(weighed, 1)
                    ch.link(dve.tensor_tensor(qs, qs, q_weight.unsqueeze(2).broadcast_to([P, H, 2, P]), ALU.mult))
                    dve.sem_inc(q_scaled, 1)

                def updates(n, j):
                    w = VX if j < H else DK
                    dve.wait_ge(cu_ready, n * HH + (j + 1))
                    for d in range(2):
                        s = state[:, j, d, 0:w]
                        scale = spread[:, SCALE, bass.ds(n, 1), j:j + 1].rearrange("p a b -> p (a b)") if j < H \
                            else float((1.0 - 2.0 ** (-5.0 - (j - H))) ** P)
                        last = dve.scalar_tensor_tensor(out=s, in0=s, scalar=scale, in1=bCU[d][:, 0:w], op0=ALU.mult, op1=ALU.add)
                    ch.link(last)
                    dve.sem_inc(updated, 1)

                def head_norms(n):
                    dve.wait_ge(num_taken, n * HH + (HH + 2))
                    apply_norms(dve, ch, P, hn, ssq, inv, fac, fac2, cols[:, bass.ds(n, 1), EM, :].rearrange("p a b -> p (a b)"),
                                sums_ready, lambda: dve.wait_ge(fac_rooted, n + 1), lambda: dve.wait_ge(g_loaded, n * 16 + 16), y)
                    dve.sem_inc(y_ready, 1)

                with dve.Fori(0, NB) as n:
                    chunk(n)


def mix_sample(c, rows, cols, spread):
    nc, g = c.nc, c.x
    VX = DK + 1
    HH = 2 * H
    STEP = S + DS
    with Stage(nc, "ms") as st:
        qk = st.sb("qk", [P, 2, 4, S])
        vh = st.sb("vh", [S, 2, VX])
        state = st.sb("state", [P, 2, DB, 2, VX])
        qz = st.sb("qz", [P, 2, 2, DB * STEP])
        kwz = st.sb("kwz", [S, 2, DB, DK])
        w = st.sb("w", [S, 2, S])
        wz = st.sb("wz", [S, 2, DB])
        wt = st.sb("wt", [S, HH, S])
        qw = st.sb("qw", [P, HH, S])
        ko = st.sb("ko", [S, HH])
        own = st.sb("own", [S, DB])
        mask = st.sb("mask", [S, S])
        select = st.sb("select", [H, H, P])
        scale = st.sb("scale", [P, HH, DB])
        y = st.sb("y", [S, 2 * D])
        hn = st.sb("hn", [S, HH, VX])
        w_out = st.sb("w_out", [P, 2 * D // P, D])
        ssq, inv, fac, fac2 = (st.sb(n, [S, HH]) for n in ("ssq", "inv", "fac", "fac2"))
        junk = st.sb("junk2", [S, 2, DK])
        banks = [st.ps(f"bank{i}", [P, 512]) for i in range(8)]
        bKN, bST, bNUM, bCU = banks[0:2], banks[2], banks[3], banks[4:8]
        tail = Tail(c, st, 2 * D, y, w_out, banks, hn[:].rearrange("p j v -> p (j v)")[:, 0:D].rearrange("p (f n) -> p f n", f=2), 0)
        loaded, stored = st.sems("loaded", 2), st.sems("stored", 2)
        s_const, s_m, rows_spread, masked, start = (st.sem(n) for n in ("const", "m", "rows_spread", "masked", "start"))
        kn_ready, st_ready, w_ready, qz_ready, kwz_ready = (st.sem(n) for n in ("kn_ready", "st_ready", "w_ready", "qz_ready", "kwz_ready"))
        num_ready, num_taken, cu_ready, updated = (st.sem(n) for n in ("num_ready", "num_taken", "cu_ready", "updated"))
        g_loaded, sums_ready, fac_rooted, y_ready, dve_chain = (st.sem(n) for n in ("g_loaded", "sums_ready", "fac_rooted", "y_ready", "dve_chain"))

        cu_taken = st.sem("cu_taken")

        def stores_before(j):
            return 16 + 16 * sum(4 if i < H else 2 for i in range(j % 2, j, 2))

        def loads_of(q, h, s):
            per = 16 * (7 if q == 0 else 5)
            return (h - s) * (per // 2) + (per + q * 16 * 7 * (H // 2))

        def heads(eng, body):
            for q in range(2):
                with eng.Fori(0, H // 2) as i:
                    for s in range(2):
                        body(q, i * 2 + s, i * 2 + (q * H + s), s)

        with nc.Block() as block:

            @block.sync
            def _(sp):
                sp.dma_start(mask[:], c.tab["mask_st_s"]).then_inc(s_const, 16)
                sp.dma_start(wt[:, H:, :].rearrange("p h t -> p (h t)"), c.tab["decay_s"]).then_inc(s_const, 16)
                sp.dma_start(qw[:, H:, :].rearrange("p h t -> p (h t)"), c.tab["gin_s"]).then_inc(s_const, 16)
                sp.dma_start(ko[:, H:], c.tab["kout_s"]).then_inc(s_const, 16)
                sp.dma_start(own[:], c.tab["batch_of"]).then_inc(s_const, 16)
                sp.dma_start(select[:].rearrange("p h t -> p (h t)"), c.tab["select"]).then_inc(s_const, 16)
                tail.load_constants(sp)

                def load(j):
                    q, h, s = j // H, j % H, j % 2
                    sp.wait_ge(stored[s], stores_before(j))
                    base = q * (QK // P)
                    for t in range(2):
                        at = base + t * (D // P) + 2 * h
                        sp.dma_start(qk[:, s, 2 * t:2 * t + 2, :], c.s_qk[at:at + 2, :, T:NT].rearrange("n p t -> p n t")).then_inc(loaded[s], 16)
                    sp.dma_start(vh[:, s, 0:DK], c.s_v[T:NT, j * DK:(j + 1) * DK]).then_inc(loaded[s], 16)
                    old = g["state_mlstm_C"] if q == 0 else g["state_ret_S"]
                    for d in range(2):
                        part = slice(d * P, (d + 1) * P)
                        sp.dma_start(state[:, s, :, d, 0:DK], old[0, :, h, part, :].rearrange("b p v -> p b v")).then_inc(loaded[s], 16)
                        if q == 0:
                            sp.dma_start(state[:, s, :, d, DK:VX], g["state_mlstm_n"][0, :, h, part].rearrange("b p -> p b").unsqueeze(2),
                                         allow_slow_non_contiguous=True).then_inc(loaded[s], 16)

                def store(j):
                    q, h, s = j // H, j % H, j % 2
                    sp.wait_ge(updated, (j + 1) * DB)
                    new = c.out["C_s"] if q == 0 else c.out["S_s"]
                    for d in range(2):
                        part = slice(d * P, (d + 1) * P)
                        sp.dma_start(new[0, :, h, part, :].rearrange("b p v -> p b v"), state[:, s, :, d, 0:DK]).then_inc(stored[s], 16)
                        if q == 0:
                            sp.dma_start(c.out["n_s"][0, :, h, part].rearrange("b p -> p b").unsqueeze(2),
                                         state[:, s, :, d, DK:VX], allow_slow_non_contiguous=True).then_inc(stored[s], 16)

                load(0)
                load(1)
                sp.dma_start(w_out[:], g["w_out_a"][0].rearrange("(k p) n -> p k n", p=P)).then_inc(tail.w_loaded, 16)
                sp.dma_start(y[:], c.s_g[T:NT, :]).then_inc(g_loaded, 16)
                sp.dma_start(tail.res[0:S, :], g["x_sample"].rearrange("b t d -> (b t) d")).then_inc(tail.res_loaded, 16)
                for j in range(HH):
                    store(j)
                    if j + 2 < HH:
                        load(j + 2)
                for s in range(2):
                    sp.wait_ge(stored[s], stores_before(HH + s))
                sp.wait_ge(tail.x1_stored, 32)

            @block.tensor
            def _(pe):
                pe.wait_ge(s_const, 96)
                tail.pe_start(pe)
                for q, bank in ((0, banks[0]), (1, banks[1])):
                    for h in range(H):
                        last = pe.matmul(bank[:, h * S:(h + 1) * S], select[:, h, :], rows[:, q, T:NT], start=True, stop=True)
                last.then_inc(rows_spread, 1)
                pe.wait_ge(start, 1)

                def body(q, h, j, s):
                    w_ = VX if q == 0 else DK
                    pe.wait_ge(loaded[s], loads_of(q, h, s))
                    pe.wait_ge(kwz_ready, j + 1)
                    for d in range(2):
                        last = pe.transpose(bKN[s][0:S, d * P:(d + 1) * P], qk[:, s, 2 + d, :], c.ident[:])
                    last.then_inc(kn_ready, 1)
                    pe.wait_ge(w_ready, j + 1)
                    for d in range(2):
                        last = pe.matmul(bST[0:S, 0:S], qk[:, s, 2 + d, :], qk[:, s, d, :], start=d == 0, stop=d == 1)
                    last.then_inc(st_ready, 1)
                    pe.wait_ge(w_ready, j + 2)
                    pe.wait_ge(qz_ready, j + 1)
                    wait_counted(pe, num_taken, j + 1)
                    out = bNUM[0:S, 0:w_]
                    pe.matmul(out, w[:, s, :], vh[:, s, 0:w_], start=True, stop=False)
                    for b in range(DB):
                        for d in range(2):
                            last = pe.matmul(out, qz[:, s, d, b * S:(b + 1) * S], state[:, s, b, d, 0:w_],
                                             start=False, stop=b == DB - 1 and d == 1)
                    last.then_inc(num_ready, 1)
                    pe.wait_ge(kwz_ready, j + 2)
                    for b in range(DB):
                        pe.wait_ge(cu_taken, j * DB + (b + 1))
                        for d in range(2):
                            last = pe.matmul(bCU[2 * (b % 2) + d][:, 0:w_], kwz[:, s, b, d * P:(d + 1) * P], vh[:, s, 0:w_], start=True, stop=True)
                        last.then_inc(cu_ready, 1)

                heads(pe, body)
                tail.pe(pe, 0, S, lambda: (pe.wait_ge(y_ready, 1), pe.wait_ge(cu_taken, HH * DB + 2)))

            @block.scalar
            def _(act):
                act.wait_ge(masked, 1)
                for h in range(H):
                    last = act.activation(wt[:, h, :], wt[:, h, :], ACT.Exp, bias=cols[0:S, NB, A, h:h + 1])
                last.then_inc(s_m, 1)

                def body(q, h, j, s):
                    w_ = VX if q == 0 else DK
                    act.wait_ge(num_ready, j + 1)
                    act.activation(hn[:, bass.ds(j, 1), 0:w_], bNUM[0:S, 0:w_].unsqueeze(1), ACT.Copy)
                    act.wait_ge(num_taken, j + 1)
                    act.activation(junk[:, s, :], bNUM[0:S, 0:DK], ACT.Square, accum_out=ssq[:, bass.ds(j, 1)]).then_inc(num_taken, 1)

                heads(act, body)
                tail.act(act, 0, S, c.s_x1[T:NT, :])

            @block.gpsimd
            def _(pool):
                tail.pool_start(pool)
                pool.wait_ge(sums_ready, 1)
                pool.tensor_tensor(fac2[:], fac[:], tail.half[0:S, 0:HH], ALU.pow).then_inc(fac_rooted, 1)
                tail.pool(pool, 0, S)

            @block.vector
            def _(dve):
                ch = Chain(dve, dve_chain)
                ch.link(dve.memset(vh[:, :, DK:VX], 1.0))
                dve.memset(inv[:], 1.0)
                ch.link(dve.memset(qz[:], 0.0))
                for s in range(2):
                    dve.sem_inc(stored[s], 16)
                tail.dve_start(dve)
                dve.sem_inc(tail.x1_stored, 16)
                dve.wait_ge(s_const, 96)
                dve.wait_ge(rows_spread, 1)
                ch.link(dve.tensor_tensor(wt[:, 0:H, :], banks[0][0:S, 0:H * S].rearrange("p (h t) -> p h t", t=S),
                                          mask[:].unsqueeze(1).broadcast_to([S, H, S]), ALU.add))
                dve.sem_inc(masked, 1)
                dve.tensor_copy(qw[:, 0:H, :], banks[1][:, 0:H * S].rearrange("p (h t) -> p h t", t=S))
                dve.tensor_copy(ko[:, 0:H], cols[0:S, NB, WS, :])
                dve.tensor_copy(scale[:, 0:H, :], spread[:, SCALE, NB:, :].rearrange("p b h -> p h b"))
                for h in range(H):
                    last = dve.memset(scale[:, H + h, :], float((1.0 - 2.0 ** (-5.0 - h)) ** DS))
                ch.link(last)
                dve.wait_ge(s_m, 1)
                dve.sem_inc(kwz_ready, 1)
                dve.sem_inc(w_ready, 1)
                dve.sem_inc(num_taken, 1)
                dve.sem_inc(cu_taken, 2)
                dve.sem_inc(start, 1)

                def body(q, h, j, s):
                    w_ = VX if q == 0 else DK
                    if s == 0:
                        ch.clear()
                    dve.wait_ge(kn_ready, j + 1)
                    one = bass.ds(j, 1)
                    ch.link(dve.tensor_scalar(wz[:, s, :], own[:], ko[:, one], None, ALU.mult))
                    ch.link(dve.tensor_tensor(kwz[:, s], bKN[s][0:S, 0:DK].unsqueeze(1).broadcast_to([S, DB, DK]),
                                              wz[:, s, :].unsqueeze(2).broadcast_to([S, DB, DK]), ALU.mult))
                    dve.sem_inc(kwz_ready, 1)
                    dve.wait_ge(st_ready, j + 1)
                    ch.link(dve.tensor_tensor(w[:, s, :].unsqueeze(1), bST[0:S, 0:S].unsqueeze(1), wt[:, one, :], ALU.mult))
                    dve.sem_inc(w_ready, 1)
                    for d in range(2):
                        last = dve.tensor_tensor(qz[:, s, d, :].rearrange("p (b t) -> p b t", t=STEP)[:, :, 0:DS],
                                                 qk[:, s, d, :].rearrange("p (b t) -> p b t", t=DS),
                                                 qw[:, one, :].rearrange("p a (b t) -> p (a b) t", t=DS), ALU.mult)
                    ch.link(last)
                    dve.sem_inc(qz_ready, 1)
                    for b in range(DB):
                        dve.wait_ge(cu_ready, j * DB + (b + 1))
                        for d in range(2):
                            x = state[:, s, b, d, 0:w_]
                            last = dve.scalar_tensor_tensor(out=x, in0=x, scalar=scale[:, one, b:b + 1].rearrange("p a b -> p (a b)"),
                                                            in1=bCU[2 * (b % 2) + d][:, 0:w_], op0=ALU.mult, op1=ALU.add)
                        ch.link(last)
                        dve.sem_inc(cu_taken, 1)
                        dve.sem_inc(updated, 1)

                heads(dve, body)
                dve.wait_ge(num_taken, HH + 1)
                apply_norms(dve, ch, S, hn, ssq, inv, fac, fac2, cols[0:S, NB, EM, :], sums_ready,
                            lambda: dve.wait_ge(fac_rooted, 1), lambda: dve.wait_ge(g_loaded, 16), y)
                dve.sem_inc(y_ready, 1)
                tail.dve(dve, 0, S, slice(T, NT))


def attend_prompt(c, q_s, k_s, v_s, g_s, lam):
    nc, g = c.nc, c.x
    W4 = 4 * 2 * HD
    NBK = NB + 1
    w = g["w_in_c"][0].rearrange("(k p) (q n) -> p k q n", p=P, q=4)
    USES = NB + 3
    with Stage(nc, "ap") as st:
        wh = st.sb("wh", [P, 2, KD, W4])
        raw = st.sb("raw", [P, 2, NBK, W4])
        ez = st.sb("ez", [P, NBK, P])
        gnb = st.sb("gnb", [P, 2, P])
        rot = st.sb("rot", [P, 2, NBK, ROT])
        tmp = st.sb("tmp", [P, 4, 4, 4, ROT])
        qT = st.sb("qT", [P, 2, T])
        kT = st.sb("kT", [P, 2, T])
        pr = st.sb("pr", [P, 2, 2, T])
        aT = st.sb("aT", [P, NB, P])
        o = st.sb("o", [P, 2, NB, P])
        ms = st.sb("ms", [P, 2, NB])
        rstd = st.sb("rstd", [P, NB])
        half = st.sb("half", [P, NB])
        junk = st.sb("junk", [P, 2, P])
        mask = st.sb("mask", [P, P])
        mx = st.sb("mx", [P, 2, 2])
        den = st.sb("den", [P, 2, 2])
        lq = st.sb("lq", [P, 4, HD])
        lsum = st.sb("lsum", [P, 2])
        sc = st.ps("sc", [P, 2, T])
        gm = st.ps("gm", [P, 512])
        at = st.ps("at", [P, 2, 512])
        ob = st.ps("ob", [P, 512])
        s_const, s_lam, w_loaded, g_loaded = st.sem("const"), st.sem("lam"), st.sems("w_loaded", 2), st.sems("g_loaded", 2)
        kv_stored, y_stored = st.sems("kv_stored", 2), st.sems("y_stored", 2)
        gm_ready, raw_ready, roped, gated = (st.sem(n) for n in ("gm_ready", "raw_ready", "roped", "gated"))
        at_turned, at_taken = st.sem("at_turned"), st.sem("at_taken")
        sc_ready, max_ready, sc_taken, a_ready, o_ready, o_taken = (
            st.sem(n) for n in ("sc_ready", "max_ready", "sc_taken", "a_ready", "o_ready", "o_taken"))
        sq_ready, rooted, y_ready, dve_chain, pool_chain, start = (
            st.sem(n) for n in ("sq_ready", "rooted", "y_ready", "dve_chain", "pool_chain", "start"))

        def heads(eng, step):
            with eng.Fori(0, HC // 2 - 1) as i:
                for s in range(2):
                    step(2 * i + s, s, True)
            step(HC - 2, 0, True)
            step(HC - 1, 1, False)

        def use(hd, k, more=True):
            return hd * USES + (k + 1)

        def weights_use(j, more):
            return j if j < 3 else j + 2 if j < 6 or not more else j + 3

        Q1, Q2, Q0 = 3, 4, 8

        with nc.Block() as block:

            @block.sync
            def _(sp):
                def load_w(hd, s):
                    for q in range(4):
                        sp.dma_start(wh[:, s, :, q * P:(q + 1) * P], w[:, :, q, bass.ds(hd * P, P)]).then_inc(w_loaded[s], 16)
                    sp.dma_start(gnb[:, s, :], g["gn_diff"][0, bass.ds(hd, 1), :].broadcast_to([P, P])).then_inc(g_loaded[s], 16)

                load_w(0, 0)
                load_w(1, 1)
                sp.dma_start(rot[:].rearrange("p q b r -> p (q b r)"), c.tab["rot1"]).then_inc(s_const, 16)
                sp.dma_start(mask[:], c.tab["mask_qk"]).then_inc(s_const, 16)
                sp.dma_start(lq[:].rearrange("p a b -> p (a b)"),
                             g["lambda_qk"].rearrange("a b c -> a (b c)").broadcast_to([P, 4 * HD])).then_inc(s_const, 16)

                def step(hd, s, more):
                    wait_counted(sp, roped, hd * 3 + 3)
                    at_h = bass.ds(hd * P, P)
                    for name, q in (("k", 1), ("v", 2)):
                        flat = "a b t h d -> (a b t) (h d)"
                        cols = slice(q * P, (q + 1) * P)
                        sp.dma_start(c.out[name + "_p"].rearrange(flat)[:, at_h].rearrange("(n p) d -> p n d", p=P),
                                     raw[:, s, 0:NB, cols]).then_inc(kv_stored[s], 16)
                        sp.dma_start(c.out[name + "_s"].rearrange(flat)[:, at_h], raw[0:S, s, NB, cols]).then_inc(kv_stored[s], 16)
                    if more is True and not isinstance(hd, int):
                        wait_counted(sp, gm_ready, hd * NBK + NBK)
                        wait_counted(sp, gated, hd + 2)
                        load_w(hd + 2, s)
                    wait_counted(sp, y_ready, hd + 3)
                    sp.dma_start(c.s_y1[0:T, at_h].rearrange("(n p) d -> p n d", p=P), o[:, s]).then_inc(y_stored[s], 16)

                heads(sp, step)
                for s in range(2):
                    sp.wait_ge(kv_stored[s], 16 + 16 * 4 * (HC // 2))
                    sp.wait_ge(y_stored[s], 16 + 16 * (HC // 2))

            @block.tensor
            def _(pe):
                def project(hd, s, b):
                    if b == 0:
                        pe.wait_ge(w_loaded[s], (hd - s) * 32 + 64)
                    if not (isinstance(hd, int) and hd == 0 and b == 0):
                        pe.wait_ge(raw_ready, hd * NBK + b)
                    n = rows_of(b)
                    for k in range(KD):
                        last = pe.matmul(gm[0:n, :], c.hT[:, k, b * P:b * P + n], wh[:, s, k, :], start=k == 0, stop=k == KD - 1)
                    last.then_inc(gm_ready, 1)

                def turn_qk(hd, s, part, count):
                    pe.wait_ge(roped, hd * 3 + (part + 1))
                    wait_counted(pe, at_taken, count + 1)
                    for q in range(2):
                        if part == 2:
                            last = pe.transpose(at[:, 0, q * S:(q + 1) * S], raw[0:S, s, NB, q * P:(q + 1) * P], c.ident[0:S, 0:S])
                        else:
                            for b in range(4):
                                last = pe.transpose(at[:, q, b * P:(b + 1) * P], raw[:, s, 4 * part + b, q * P:(q + 1) * P], c.ident[:])
                    last.then_inc(at_turned, 1)

                def scores(hd, s, j):
                    wait_counted(pe, sc_taken, hd * NB + (j + 1))
                    n = (j + 1) * P
                    for m in range(2):
                        half_rows = slice(m * HD, (m + 1) * HD)
                        for k0 in range(0, n, 512):
                            kn = min(512, n - k0)
                            last = pe.matmul(sc[:, m, k0:k0 + kn], qT[half_rows, s, j * P:(j + 1) * P], kT[half_rows, s, k0:k0 + kn],
                                             start=True, stop=True)
                    last.then_inc(sc_ready, 1)

                def turn_weights(hd, s, j, more):
                    pe.wait_ge(a_ready, hd * NB + (j + 1))
                    pe.wait_ge(at_taken, use(hd, weights_use(j, more)) + 1)
                    for k in range(j + 1):
                        last = pe.transpose(at[:, k // 4, (k % 4) * P:(k % 4 + 1) * P], pr[:, j % 2, 0, k * P:(k + 1) * P], c.ident[:])
                    last.then_inc(at_turned, 1)

                def values(hd, s, j, more):
                    pe.wait_ge(at_taken, use(hd, weights_use(j, more)) + 2)
                    pe.wait_ge(o_taken, hd * NB + (j + 1))
                    for k in range(j + 1):
                        last = pe.matmul(ob[:, 0:P], aT[:, k, :], raw[:, s, k, 2 * P:3 * P], start=k == 0, stop=k == j)
                    last.then_inc(o_ready, 1)

                pe.wait_ge(start, 1)
                for b in range(NBK):
                    project(0, 0, b)
                turn_qk(0, 0, 0, 0)
                pe.wait_ge(at_taken, 2)
                scores(0, 0, 0)

                def step(hd, s, more):
                    for j in range(NB):
                        if more:
                            project(hd + 1, 1 - s, j)
                        turn_weights(hd, s, j, more)
                        if j < NB - 1:
                            scores(hd, s, j + 1)
                        elif more:
                            scores(hd + 1, 1 - s, 0)
                        values(hd, s, j, more)
                        if j == 2:
                            turn_qk(hd, s, 1, use(hd, Q1))
                            turn_qk(hd, s, 2, use(hd, Q2))
                        if j == 5 and more:
                            turn_qk(hd + 1, 1 - s, 0, use(hd, Q0))
                    if more:
                        project(hd + 1, 1 - s, NB)

                heads(pe, step)

            @block.scalar
            def _(act):
                act.wait_ge(start, 1)
                act.activation(lsum[:], lsum[:], ACT.Exp).then_inc(s_lam, 1)

                def take_rows(hd, s, b):
                    n = rows_of(b)
                    if b == 0:
                        act.wait_ge(y_ready, hd + 1)
                        act.wait_ge(kv_stored[s], (hd - s) * 32 + 16)
                        act.wait_ge(gated, hd + 1)
                    act.wait_ge(gm_ready, hd * NBK + (b + 1))
                    act.activation(ez[0:n, b, :], gm[0:n, 3 * P:], ACT.Exp, scale=-1.0)
                    act.activation(raw[0:n, s, b, :], gm[0:n, :], ACT.Copy).then_inc(raw_ready, 1)

                def take_qk(hd, s, part, count):
                    act.wait_ge(at_turned, count + 1)
                    if part == 2:
                        one = bass.ds(hd, 1)
                        act.activation(q_s[:, one, :], at[:, 0, 0:S].unsqueeze(1), ACT.Copy)
                        act.activation(k_s[:, one, :], at[:, 0, S:2 * S].unsqueeze(1), ACT.Copy).then_inc(at_taken, 1)
                    else:
                        act.activation(qT[:, s, part * 512:(part + 1) * 512], at[:, 0, :], ACT.Copy)
                        act.activation(kT[:, s, part * 512:(part + 1) * 512], at[:, 1, :], ACT.Copy).then_inc(at_taken, 1)

                def exps(hd, s, j):
                    n = (j + 1) * P
                    act.wait_ge(max_ready, hd * NB + (j + 1))
                    for m in range(2):
                        last = act.activation(pr[:, j % 2, m, 0:n], sc[:, m, 0:n], ACT.Exp, bias=mx[:, j % 2, m:m + 1], scale=HD ** -0.5,
                                              accum_out=den[:, j % 2, m:m + 1])
                    last.then_inc(sc_taken, 1)

                def take_weights(hd, s, j, more):
                    act.wait_ge(at_turned, use(hd, weights_use(j, more)) + 1)
                    last = act.activation(aT[:, 0:min(4, j + 1), :], at[:, 0, 0:min(4, j + 1) * P].rearrange("p (k t) -> p k t", t=P), ACT.Copy)
                    if j >= 4:
                        last = act.activation(aT[:, 4:j + 1, :], at[:, 1, 0:(j - 3) * P].rearrange("p (k t) -> p k t", t=P), ACT.Copy)
                    last.then_inc(at_taken, 1)

                def take_out(hd, s, j):
                    act.wait_ge(o_ready, hd * NB + (j + 1))
                    if j == 0:
                        act.wait_ge(y_stored[s], (hd - s) * 8 + 16)
                    act.activation(o[:, s, j, :], ob[:, 0:P], ACT.Copy)
                    act.wait_ge(o_taken, hd * NB + (j + 1))
                    act.activation(junk[:, j % 2, :], ob[:, 0:P], ACT.Square, accum_out=ms[:, s, j:j + 1]).then_inc(o_taken, 1)

                for b in range(NBK):
                    take_rows(0, 0, b)
                take_qk(0, 0, 0, 0)

                def step(hd, s, more):
                    for j in range(NB):
                        exps(hd, s, j)
                        if more:
                            take_rows(hd + 1, 1 - s, j)
                        take_weights(hd, s, j, more)
                        take_out(hd, s, j)
                        if j == 2:
                            take_qk(hd, s, 1, use(hd, Q1))
                            take_qk(hd, s, 2, use(hd, Q2))
                        if j == 5 and more:
                            take_qk(hd + 1, 1 - s, 0, use(hd, Q0))
                    if more:
                        take_rows(hd + 1, 1 - s, NB)

                heads(act, step)

            @block.gpsimd
            def _(pool):
                pool.memset(half[:], -0.5).then_inc(pool_chain, 1)
                pool.wait_ge(pool_chain, 1)

                def step(hd, s, more):
                    wait_counted(pool, sq_ready, hd + 1)
                    pool.tensor_tensor(rstd[:], ms[:, s, :], half[:], ALU.pow).then_inc(rooted, 1)

                heads(pool, step)

            @block.vector
            def _(dve):
                ch = Chain(dve, dve_chain)
                dve.wait_ge(s_const, 48)
                pair = lq[:].rearrange("p (a b) d -> p a b d", b=2)
                ch.link(dve.tensor_tensor(pair[:, :, 0, :], pair[:, :, 0, :], pair[:, :, 1, :], ALU.mult))
                ch.link(dve.tensor_reduce(lsum[:], pair[:, :, 0, :], AX_X, ALU.add))
                for q in (at_taken, sc_taken, o_taken, gated):
                    dve.sem_inc(q, 1)
                dve.sem_inc(y_ready, 2)
                for s in range(2):
                    dve.sem_inc(kv_stored[s], 16)
                    dve.sem_inc(y_stored[s], 16)
                dve.sem_inc(start, 1)
                dve.wait_ge(s_lam, 1)
                ch.link(dve.tensor_tensor(lam[:], lsum[:, 0:1], lsum[:, 1:2], ALU.subtract))
                ch.link(dve.tensor_scalar(lam[:], lam[:], LAM_INIT, None, ALU.add))

                def rotate(hd, s, part):
                    b0, nb, n = (4 * part, 4, P) if part < 2 else (NB, 1, S)
                    dve.wait_ge(raw_ready, hd * NBK + (b0 + nb))
                    for b in range(b0, b0 + nb, 4):
                        x = raw[0:n, s, b0:b0 + nb, 0:2 * P].rearrange("p b (m d) -> p b m d", d=HD)
                        x1, x2 = x[:, :, :, 0:ROT], x[:, :, :, ROT:2 * ROT]
                        cos, sin = (rot[0:n, i, b0:b0 + nb, :].unsqueeze(2).broadcast_to([n, nb, 4, ROT]) for i in range(2))
                        t = [tmp[0:n, i, 0:nb] for i in range(4)]
                        for o_, x_, f_ in ((t[0], x1, cos), (t[1], x2, sin), (t[2], x1, sin), (t[3], x2, cos)):
                            last = dve.tensor_tensor(o_, x_, f_, ALU.mult)
                        ch.link(last)
                        dve.tensor_tensor(x1, t[0], t[1], ALU.subtract)
                        ch.link(dve.tensor_tensor(x2, t[2], t[3], ALU.add))
                    dve.sem_inc(roped, 1)

                def gates(hd, s):
                    dve.wait_ge(g_loaded[s], (hd - s) * 8 + 16)
                    dve.wait_ge(raw_ready, hd * NBK + NBK)
                    for b0, nb, n in ((0, NB, P), (NB, 1, S)):
                        e, z = ez[0:n, b0:b0 + nb, :], raw[0:n, s, b0:b0 + nb, 3 * P:]
                        ch.link(dve.tensor_scalar(e, e, 1.0, None, ALU.add))
                        ch.link(dve.reciprocal(e, e))
                        ch.link(dve.tensor_tensor(z, z, e, ALU.mult))
                        ch.link(dve.scalar_tensor_tensor(out=z, in0=z, scalar=1.0 - LAM_INIT,
                                                         in1=gnb[0:n, s, :].unsqueeze(1).broadcast_to([n, nb, P]), op0=ALU.mult, op1=ALU.mult))
                    one = bass.ds(hd, 1)
                    dve.tensor_copy(g_s[:, one, :], raw[0:S, s, NB:NBK, 3 * P:])
                    ch.link(dve.tensor_copy(v_s[:, one, :], raw[0:S, s, NB:NBK, 2 * P:3 * P]))
                    dve.sem_inc(gated, 1)

                def maxima(hd, s, j):
                    n, i = (j + 1) * P, j % 2
                    dve.wait_ge(sc_ready, hd * NB + (j + 1))
                    diagonal = sc[:, :, j * P:n]
                    ch.link(dve.tensor_tensor(diagonal, diagonal, mask[:].unsqueeze(1).broadcast_to([P, 2, P]), ALU.add))
                    ch.link(dve.tensor_reduce(mx[:, i, :], sc[:, :, 0:n], AX_X, ALU.max))
                    ch.link(dve.tensor_scalar(mx[:, i, :], mx[:, i, :], -HD ** -0.5, None, ALU.mult))
                    dve.sem_inc(max_ready, 1)

                def difference(hd, s, j):
                    n, i = (j + 1) * P, j % 2
                    dve.wait_ge(sc_taken, hd * NB + (j + 2))
                    ch.link(dve.reciprocal(den[:, i, :], den[:, i, :]))
                    ch.link(dve.tensor_scalar(pr[:, i, 1, 0:n], pr[:, i, 1, 0:n], den[:, i, 1:2], lam[:, 0:1], ALU.mult, ALU.mult))
                    ch.link(dve.scalar_tensor_tensor(out=pr[:, i, 0, 0:n], in0=pr[:, i, 0, 0:n], scalar=den[:, i, 0:1],
                                                     in1=pr[:, i, 1, 0:n], op0=ALU.mult, op1=ALU.subtract))
                    dve.sem_inc(a_ready, 1)

                def finish(hd, s):
                    dve.wait_ge(o_taken, hd * NB + (NB + 1))
                    ch.link(dve.tensor_scalar(ms[:, s, :], ms[:, s, :], 1.0 / P, EPS, ALU.mult, ALU.add))
                    dve.sem_inc(sq_ready, 1)
                    dve.wait_ge(rooted, hd + 1)
                    ch.link(dve.tensor_tensor(o[:, s], o[:, s], rstd[:].unsqueeze(2).broadcast_to([P, NB, P]), ALU.mult))
                    ch.link(dve.tensor_tensor(o[:, s], o[:, s], raw[:, s, 0:NB, 3 * P:], ALU.mult))
                    dve.sem_inc(y_ready, 1)

                rotate(0, 0, 0)

                def step(hd, s, more, first=False):
                    if not first:
                        ch.clear()
                    for j in range(NB):
                        maxima(hd, s, j)
                        difference(hd, s, j)
                        if j == 0:
                            rotate(hd, s, 1)
                            rotate(hd, s, 2)
                            gates(hd, s)
                        if j == 4 and more:
                            rotate(hd + 1, 1 - s, 0)
                    finish(hd, s)

                heads(dve, step)


def attend_sample(c, q_s, k_s, v_s, g_s, lam):
    nc, g = c.nc, c.x
    R = 2 * S
    G = 4
    NG = NPG // G
    GK = G * PAGE
    with Stage(nc, "as") as st:
        pt = st.sb("pt", [1, DB * NPG], I32)
        kp = st.sb("kp", [P, 2 * G, D])
        vp = st.sb("vp", [P, 2 * G, D])
        kT = st.sb("kT", [P, 2, HC, GK])
        s = st.sb("s", [R, 2, PAST + S])
        qz = st.sb("qz", [P, 2, HC * (2 * S + DS) + S])
        aT = st.sb("aT", [P, 2, G, S])
        aN = st.sb("aN", [S, S])
        mx = st.sb("mx", [R, 2, NG + 1])
        top = st.sb("top", [R, 2])
        den = st.sb("den", [R, 2])
        sign = st.sb("sign", [R, 1])
        pair = st.sb("pair", [R, S])
        pick = st.sb("pick", [R, 2, S])
        new_mask = st.sb("new_mask", [R, DB, S])
        own = st.sb("own", [S, HC])
        toq = st.sb("toq", [S, DS])
        om = st.sb("om", [S, D])
        oq = st.sb("oq", [DS, D])
        a = st.sb("a", [S, D])
        sq = st.sb("sq", [S, D])
        ms = st.sb("ms", [S, 2, HC])
        half = st.sb("half", [S, HC])
        tp = [st.ps(f"tp{i}", [P, 2, 512]) for i in range(2)]
        sc = st.ps("sc", [P, 512])
        ap_ = st.ps("ap", [P, 512])
        ov = st.ps("ov", [P, 2, 512])
        s_pt, s_const = st.sem("pt"), st.sem("const")
        k_loaded, v_loaded = st.sems("k_loaded", 2 * G), st.sems("v_loaded", 2 * G)
        k_turned, sc_ready, sc_taken = (st.sem(n) for n in ("k_turned", "sc_ready", "sc_taken"))
        kT_taken = st.sems("kT_taken", 2)
        q_ready, group_max, top_ready, exp_ready, pick_ready = (st.sem(n) for n in ("q_ready", "group_max", "top_ready", "exp_ready", "pick_ready"))
        a_turned, a_taken, v_used, o_ready, o_picked = (st.sem(n) for n in ("a_turned", "a_taken", "v_used", "o_ready", "o_picked"))
        oq_ready, oq_taken, oq_stored, s_a, s_y, start = (st.sem(n) for n in ("oq_ready", "oq_taken", "oq_stored", "a", "y", "start"))
        dve_chain, rooted, squares_ready = st.sem("dve_chain"), st.sem("rooted"), st.sem("squares_ready")
        STEP = 2 * S + DS

        def sequences(eng, keys, both, values):
            keys(0, 0)
            with eng.Fori(0, DB // 2 - 1) as i:
                for s_ in range(2):
                    both(2 * i + s_, s_)
            both(DB - 2, 0)
            values(DB - 1, 1)

        def interleave(k_start, k_group, k_end, v_start, v_group, v_end):
            def keys(b, s_):
                k_start(b, s_)
                for i in range(NG):
                    k_group(b, s_, i)
                k_end(b, s_)

            def both(b, s_):
                k_start(b + 1, 1 - s_)
                v_start(b, s_)
                for i in range(NG):
                    k_group(b + 1, 1 - s_, i)
                    v_group(b, s_, i)
                v_end(b, s_)
                k_end(b + 1, 1 - s_)

            def values(b, s_):
                v_start(b, s_)
                for i in range(NG):
                    v_group(b, s_, i)
                v_end(b, s_)

            return keys, both, values

        def nothing(*_):
            pass

        def loads(b, i):
            return b * (16 * NG // 2) + 16 * (i // 2 + 1)

        with nc.Block() as block:

            @block.sync
            def _(sp):
                sp.dma_start(pt[:], g["page_table"].rearrange("(a b) n -> a (b n)", a=1)).then_inc(s_pt, 16)
                sp.dma_start(pair[:], c.tab["pair_sum"]).then_inc(s_const, 16)
                sp.dma_start(new_mask[:].rearrange("r b k -> r (b k)"), c.tab["new_mask"]).then_inc(s_const, 16)
                sp.dma_start(own[:], c.tab["own_head"]).then_inc(s_const, 16)
                sp.dma_start(toq[:], c.tab["to_query"]).then_inc(s_const, 16)
                sp.wait_ge(s_pt, 16)

                def pages(cache, ring, loaded, free, b, i):
                    for n in range(G):
                        if n == 0:
                            wait_counted(sp, free, b * (NG * G) + (i + 1) * G)
                        at = pt[0:1, bass.ds(b * NPG + (i * G + n), 1)]
                        page = sp.value_load(at, min_val=0, max_val=N_POOL - 1)
                        slot = (i % 2) * G + n
                        sp.dma_start(ring[:, slot, :], cache[0, bass.ds(page, 1)].rearrange("a k h d -> (a k) (h d)")).then_inc(loaded[slot], 16)

                def k_group(b, s_, i):
                    pages(g["cache_k"], kp, k_loaded, k_turned, b, i)

                def v_group(b, s_, i):
                    pages(g["cache_v"], vp, v_loaded, v_used, b, i)

                sequences(sp, *interleave(nothing, k_group, nothing, nothing, v_group, nothing))
                sp.wait_ge(oq_stored, 16 + 16 * DB)
                sp.dma_start(a[:], c.s_a1[:]).then_inc(s_a, 16)
                sp.wait_ge(s_y, 1)
                sp.dma_start(c.s_y1[T:NT, :], a[:]).then_inc(s_a, 16)
                sp.wait_ge(s_a, 32)

            @block.tensor
            def _(pe):
                def k_start(b, s_):
                    pe.wait_ge(q_ready, b + 1)

                def k_group(b, s_, i):
                    for n in range(G):
                        slot = (i % 2) * G + n
                        pe.wait_ge(k_loaded[slot], loads(b, i))
                        for q in kT_taken:
                            wait_counted(pe, q, b * NPG + (i * G + n + 1))
                        for h in range(HC):
                            last = pe.transpose(tp[n % 2][:, h // 4, (h % 4) * P:(h % 4 + 1) * P], kp[:, slot, h * P:(h + 1) * P], c.ident[:])
                        last.then_inc(k_turned, 1)
                    for q in kT_taken:
                        pe.wait_ge(q, b * NPG + (i * G + G + 2))
                    wait_counted(pe, sc_taken, b * (NG + 1) + (i + 1))
                    for h in range(HC):
                        last = pe.matmul(sc[0:R, :], qz[:, s_, h * R:(h + 1) * R], kT[:, i % 2, h, :], start=h == 0, stop=h == HC - 1)
                    last.then_inc(sc_ready, 1)

                def k_end(b, s_):
                    wait_counted(pe, sc_taken, b * (NG + 1) + (NG + 1))
                    for h in range(HC):
                        last = pe.matmul(sc[0:R, 0:S], qz[:, s_, h * R:(h + 1) * R], k_s[:, h, :], start=h == 0, stop=h == HC - 1)
                    last.then_inc(sc_ready, 1)

                def v_start(b, s_):
                    pe.wait_ge(pick_ready, b + 1)

                def v_group(b, s_, i):
                    wait_counted(pe, a_taken, b * (NG + 1) + (i + 1))
                    for n in range(G):
                        k0 = (i * G + n) * PAGE
                        last = pe.matmul(ap_[:, n * S:(n + 1) * S], s[:, s_, k0:k0 + PAGE], pick[:, s_, :], start=True, stop=True)
                    last.then_inc(a_turned, 1)
                    pe.wait_ge(a_taken, b * (NG + 1) + (i + 2))
                    if i == 0:
                        wait_counted(pe, oq_taken, b + 1)
                    for n in range(G):
                        slot = (i % 2) * G + n
                        wait_counted(pe, v_loaded[slot], loads(b, i))
                        for f in range(2):
                            last = pe.matmul(ov[0:S, f, :], aT[:, i % 2, n, :], vp[:, slot, f * 512:(f + 1) * 512],
                                             start=i == 0 and n == 0, stop=False)
                        last.then_inc(v_used, 1)

                def v_end(b, s_):
                    wait_counted(pe, a_taken, b * (NG + 1) + (NG + 1))
                    pe.matmul(ap_[0:S, 0:S], s[:, s_, PAST:], pick[:, s_, :], start=True, stop=True).then_inc(a_turned, 1)
                    wait_counted(pe, a_taken, b * (NG + 1) + (NG + 2))
                    for f in range(2):
                        last = pe.matmul(ov[0:S, f, :], aN[:], v_s[:].rearrange("t h e -> t (h e)")[:, f * 512:(f + 1) * 512], start=False, stop=True)
                    last.then_inc(o_ready, 1)
                    wait_counted(pe, o_picked, b + 1)
                    for f in range(2):
                        last = pe.matmul(ov[0:DS, f, :], toq[:], om[:, f * 512:(f + 1) * 512], start=True, stop=True)
                    last.then_inc(oq_ready, 1)

                pe.wait_ge(start, 1)
                sequences(pe, *interleave(k_start, k_group, k_end, v_start, v_group, v_end))

            def copy_keys(eng, b, i, half_):
                for n in range(G):
                    wait = b * NPG + (i * G + n + 1)
                    eng.wait_ge(k_turned, wait + 2 * G)
                    o_ = kT[:, i % 2, 4 * half_:4 * half_ + 4, n * PAGE:(n + 1) * PAGE]
                    x = tp[n % 2][:, half_, :].rearrange("p (h k) -> p h k", h=4)
                    if half_ == 0:
                        eng.activation(o_, x, ACT.Copy).then_inc(kT_taken[half_], 1)
                    else:
                        eng.tensor_copy(o_, x).then_inc(kT_taken[half_], 1)

            @block.scalar
            def _(act):
                act.wait_ge(start, 1)

                def k_group(b, s_, i):
                    copy_keys(act, b, i, 0)
                    act.wait_ge(sc_ready, b * (NG + 1) + (i + 1))
                    act.activation(s[:, s_, i * GK:(i + 1) * GK], sc[0:R, :], ACT.Copy).then_inc(sc_taken, 1)

                def k_end(b, s_):
                    act.wait_ge(top_ready, b + 1)
                    act.activation(s[:, s_, :], s[:, s_, :], ACT.Exp, bias=top[:, s_:s_ + 1], scale=HD ** -0.5,
                                   accum_out=den[:, s_:s_ + 1]).then_inc(exp_ready, 1)

                def v_group(b, s_, i):
                    act.wait_ge(a_turned, b * (NG + 1) + (i + 1))
                    act.activation(aT[:, i % 2], ap_[:, 0:G * S].rearrange("p (n r) -> p n r", n=G), ACT.Copy).then_inc(a_taken, 1)

                def v_end(b, s_):
                    act.wait_ge(a_turned, b * (NG + 1) + (NG + 1))
                    act.activation(aN[:], ap_[0:S, 0:S], ACT.Copy).then_inc(a_taken, 1)
                    act.wait_ge(oq_ready, b + 1)
                    act.wait_ge(oq_stored, b * 16 + 16)
                    act.activation(oq[:], ov[0:DS].rearrange("p f n -> p (f n)"), ACT.Copy).then_inc(oq_taken, 1)
                    act.wait_ge(oq_taken, b + 2)
                    act.dma_start(c.s_a1[bass.ds(b * DS, DS), :], oq[:]).then_inc(oq_stored, 16)

                sequences(act, *interleave(nothing, k_group, k_end, nothing, v_group, v_end))

            @block.gpsimd
            def _(pool):
                pool.memset(half[:], -0.5).then_inc(rooted, 1)
                pool.wait_ge(rooted, 1)
                pool.wait_ge(squares_ready, 1)
                pool.tensor_tensor(ms[:, 1, :], ms[:, 0, :], half[:], ALU.pow).then_inc(rooted, 1)

            @block.vector
            def _(dve):
                ch = Chain(dve, dve_chain)
                dve.memset(sign[0:S, :], 1.0)
                ch.link(dve.memset(qz[:], 0.0))
                ch.link(dve.tensor_scalar(sign[S:R, :], lam[S:R, :], -1.0, None, ALU.mult))
                dve.wait_ge(s_const, 64)
                dve.sem_inc(k_turned, 2 * G)
                dve.sem_inc(v_used, 2 * G)
                for q in kT_taken:
                    dve.sem_inc(q, 2)
                dve.sem_inc(sc_taken, 1)
                dve.sem_inc(a_taken, 1)
                dve.sem_inc(oq_taken, 1)
                dve.sem_inc(oq_stored, 16)
                dve.sem_inc(start, 1)

                def k_start(b, s_):
                    ch.clear()
                    for m in range(2):
                        part = slice(m * HD, (m + 1) * HD)
                        last = dve.tensor_copy(
                            qz[part, s_, m * S:m * S + HC * STEP].rearrange("p (h t) -> p h t", t=STEP)[:, :, 0:DS],
                            q_s[part, :, bass.ds(b * DS, DS)])
                    ch.link(last)
                    dve.sem_inc(q_ready, 1)

                def k_group(b, s_, i):
                    copy_keys(dve, b, i, 1)
                    dve.wait_ge(sc_taken, b * (NG + 1) + (i + 2))
                    dve.tensor_reduce(mx[:, s_, i:i + 1], s[:, s_, i * GK:(i + 1) * GK], AX_X, ALU.max).then_inc(group_max, 1)

                def k_end(b, s_):
                    dve.wait_ge(sc_ready, b * (NG + 1) + (NG + 1))
                    new = s[:, s_, PAST:]
                    ch.link(dve.tensor_tensor(new, sc[0:R, 0:S], new_mask[:, bass.ds(b, 1), :].rearrange("r a k -> r (a k)"), ALU.add))
                    dve.sem_inc(sc_taken, 1)
                    ch.link(dve.tensor_reduce(mx[:, s_, NG:NG + 1], new, AX_X, ALU.max))
                    ch.link(dve.tensor_reduce(top[:, s_:s_ + 1], mx[:, s_, :], AX_X, ALU.max))
                    ch.link(dve.tensor_scalar(top[:, s_:s_ + 1], top[:, s_:s_ + 1], -HD ** -0.5, None, ALU.mult))
                    dve.sem_inc(top_ready, 1)
                    dve.wait_ge(exp_ready, b + 1)
                    ch.link(dve.reciprocal(den[:, s_:s_ + 1], den[:, s_:s_ + 1]))
                    ch.link(dve.tensor_scalar(pick[:, s_, :], pair[:], den[:, s_:s_ + 1], sign[:, 0:1], ALU.mult, ALU.mult))
                    dve.sem_inc(pick_ready, 1)

                def v_end(b, s_):
                    dve.wait_ge(o_ready, b + 1)
                    for f in range(2):
                        last = dve.tensor_tensor(om[:, f * 512:(f + 1) * 512].rearrange("p (h e) -> p h e", h=HC // 2),
                                                 ov[0:S, f, :].rearrange("p (h e) -> p h e", h=HC // 2),
                                                 own[:, f * (HC // 2):(f + 1) * (HC // 2)].unsqueeze(2).broadcast_to([S, HC // 2, 2 * HD]), ALU.mult)
                    ch.link(last)
                    dve.sem_inc(o_picked, 1)

                sequences(dve, *interleave(k_start, k_group, k_end, nothing, nothing, v_end))
                dve.wait_ge(s_a, 16)
                ch.link(dve.tensor_tensor(sq[:], a[:], a[:], ALU.mult))
                ch.link(dve.tensor_reduce(ms[:, 0, :], sq[:].rearrange("t (h e) -> t h e", h=HC), AX_X, ALU.add))
                ch.link(dve.tensor_scalar(ms[:, 0, :], ms[:, 0, :], 1.0 / (2 * HD), EPS, ALU.mult, ALU.add))
                dve.sem_inc(squares_ready, 1)
                dve.wait_ge(rooted, 2)
                av = a[:].rearrange("t (h e) -> t h e", h=HC)
                ch.link(dve.tensor_tensor(av, av, ms[:, 1, :].unsqueeze(2).broadcast_to([S, HC, 2 * HD]), ALU.mult))
                ch.link(dve.tensor_tensor(av, av, g_s[:], ALU.mult))
                dve.sem_inc(s_y, 1)


def project_out(c):
    nc, g = c.nc, c.x
    with Stage(nc, "po") as st:
        y = st.sb("y", [P, D])
        w_out = st.sb("w_out", [P, KD, D])
        junk = st.sb("junk2", [P, 2, 512])
        banks = [st.ps(f"bank{i}", [P, 512]) for i in range(8)]
        tail = Tail(c, st, D, y, w_out, banks, junk, 1)
        y_loaded, start = st.sem("y_loaded"), st.sem("start")
        out_p = c.out["y_prompt"].rearrange("a t d -> (a t) d")
        out_s = c.out["y_sample"].rearrange("a t d -> (a t) d")

        with nc.Block() as block:

            @block.sync
            def _(sp):
                tail.load_constants(sp)

                def load(at, n):
                    sp.dma_start(y[0:n, :], c.s_y1[at, :]).then_inc(y_loaded, 16)
                    sp.dma_start(tail.res[0:n, :], c.s_x1[at, :]).then_inc(tail.res_loaded, 16)

                load(slice(0, P), P)
                sp.dma_start(w_out[:], g["w_out_c"][0].rearrange("(k p) n -> p k n", p=P)).then_inc(tail.w_loaded, 16)
                with sp.Fori(1, NB) as i:
                    wait_counted(sp, tail.y_turned, i)
                    wait_counted(sp, tail.x1_ready, i)
                    load(bass.ds(i * P, P), P)
                sp.wait_ge(tail.y_turned, NB)
                sp.wait_ge(tail.x1_ready, NB)
                load(slice(T, NT), S)
                sp.wait_ge(tail.x1_stored, 16 * (NB + 2))

            @block.tensor
            def _(pe):
                pe.wait_ge(start, 1)
                with pe.Fori(0, NB) as i:
                    tail.pe(pe, i, P, lambda: wait_counted(pe, y_loaded, i * 16 + 16))
                tail.pe(pe, NB, S, lambda: pe.wait_ge(y_loaded, 16 * NB + 16))

            @block.scalar
            def _(act):
                with act.Fori(0, NB) as i:
                    tail.act(act, i, P, out_p[bass.ds(i * P, P), :])
                tail.act(act, NB, S, out_s)

            @block.gpsimd
            def _(pool):
                tail.pool_start(pool)
                with pool.Fori(0, NB) as i:
                    tail.pool(pool, i, P)
                tail.pool(pool, NB, S)

            @block.vector
            def _(dve):
                tail.dve_start(dve)
                dve.sem_inc(tail.x1_stored, 16)
                dve.sem_inc(start, 1)
                with dve.Fori(0, NB) as i:
                    tail.dve(dve, i, P, None)
                tail.dve(dve, NB, S, None)


INPUTS = ["x_prompt", "x_sample", "state_mlstm_C", "state_mlstm_n", "state_mlstm_m", "state_mlstm_conv",
          "state_ret_S", "cache_k", "cache_v", "page_table", "norm_pre", "norm_post", "w_in_a", "b_gate_i",
          "b_gate_f", "conv_w", "conv_b", "gn_mlstm", "gn_ret", "w_out_a", "w_in_c", "lambda_qk", "gn_diff", "w_out_c"]
OUTPUTS = {
    "y_prompt": (1, T, D), "y_sample": (DB, DS, D),
    "C_p": (1, 1, H, DK, DK), "n_p": (1, 1, H, DK), "m_p": (1, 1, H), "conv_p": (1, 1, CW - 1, QK),
    "S_p": (1, 1, H, DK, DK), "k_p": (1, 1, T, 2 * HC, HD), "v_p": (1, 1, T, HC, 2 * HD),
    "C_s": (1, DB, H, DK, DK), "n_s": (1, DB, H, DK), "m_s": (1, DB, H), "conv_s": (1, DB, CW - 1, QK),
    "S_s": (1, DB, H, DK, DK), "k_s": (1, DB, DS, 2 * HC, HD), "v_s": (1, DB, DS, HC, 2 * HD),
}


def build(nc, ins, tabs, outs):
    with ExitStack() as ctx:
        c = Core(nc, ins, tabs, outs, ctx)
        norm_to_columns(c)
        with ExitStack() as mid:
            rows = mid.enter_context(nc.sbuf_tensor("gate_rows", [H, 2, NT], F32))
            cols = mid.enter_context(nc.sbuf_tensor("gate_cols", [P, NB + 1, 3, H], F32))
            spread = mid.enter_context(nc.sbuf_tensor("gate_spread", [P, 2, NB + DB, H], F32))
            with ExitStack() as early:
                gates = early.enter_context(nc.sbuf_tensor("gates", [H, 2, NT], F32))
                project_layer0(c, gates)
                gate_rows(c, gates, rows, cols, spread)
            mix_prompt(c, rows, cols, spread)
            mix_sample(c, rows, cols, spread)
        with ExitStack() as late:
            q_s = late.enter_context(nc.sbuf_tensor("q_s", [P, HC, S], F32))
            k_s = late.enter_context(nc.sbuf_tensor("k_s", [P, HC, S], F32))
            v_s = late.enter_context(nc.sbuf_tensor("v_s", [S, HC, 2 * HD], F32))
            g_s = late.enter_context(nc.sbuf_tensor("g_s", [S, HC, 2 * HD], F32))
            lam = late.enter_context(nc.sbuf_tensor("lam", [P, 1], F32))
            attend_prompt(c, q_s, k_s, v_s, g_s, lam)
            attend_sample(c, q_s, k_s, v_s, g_s, lam)
        project_out(c)


def kernel(**inputs):
    import concourse.bacc as bacc
    from concourse.bass_utils import run_bass_kernel_spmd as run

    nc = bacc.Bacc("TRN2", target_bir_lowering=False, num_devices=1)
    arrays, ins, tabs, outs = {}, {}, {}, {}

    def give(name, a):
        arrays[name] = np.ascontiguousarray(a)
        return nc.dram_tensor(name, a.shape, mybir.dt.from_np(a.dtype), kind="ExternalInput").ap()

    for name in INPUTS:
        ins[name] = give(f"in_{name}", np.asarray(inputs[name]))
    for name, a in shape_tables().items():
        tabs[name] = give(f"tab_{name}", a)
    for name, shape in OUTPUTS.items():
        outs[name] = nc.dram_tensor(f"out_{name}", shape, F32, kind="ExternalOutput").ap()
    build(nc, ins, tabs, outs)
    r = run(nc, [arrays], core_ids=[0])
    return tuple(r.results[0][f"out_{name}"] for name in OUTPUTS)
```

```python
import math
from contextlib import ExitStack

import numpy as np

import concourse.bass as bass
from concourse import mybir

F32 = mybir.dt.float32
F32R = mybir.dt.float32r
I32 = mybir.dt.int32
ALU = mybir.AluOpType
ACT = mybir.ActivationFunctionType
AX_X = mybir.AxisListType.X

P = 128
D = 1024
KD = D // P
T = 1024
NB = T // P
DB, DS = 8, 4
S = DB * DS
NT = T + S
H = 4
DK = 256
QK = 2 * H * DK
CW = 4
HC, HD = 8, 64
ROT = HD // 8
PAGE = 128
PAST = 4096
NPG = PAST // PAGE
N_POOL = DB * NPG + DB * NPG // 4
EPS = 1e-6
NEG = -1e30
OFF_GATE = QK + 2 * D
OFF_RET = OFF_GATE + 2 * H
PROJ_A = OFF_RET + 4 * D
LAM_INIT = 0.8 - 0.6 * math.exp(-0.3)


def shape_tables():
    f = np.float32
    t = np.arange(P)
    same = (np.arange(S)[:, None] // DS == np.arange(S)[None, :] // DS)
    st = np.arange(S)
    gam = 1.0 - 2.0 ** (-5.0 - np.arange(H))
    rel = t[None, :] - t[:, None]
    dec = np.where(rel[:, None, :] >= 0, gam[None, :, None] ** np.maximum(rel, 0)[:, None, :], 0.0)
    rs = st[None, :] - st[:, None]
    decs = np.where((same & (rs >= 0))[:, None, :], gam[None, :, None] ** np.maximum(rs, 0)[:, None, :], 0.0)
    pos = np.concatenate([np.arange(T), PAST + st % DS]).astype(f)

    def angles(half, theta):
        inv = np.power(f(theta), -np.arange(half, dtype=f) / f(half)).astype(f)
        return (pos[:, None] * inv[None, :]).astype(f).astype(np.float64)

    a0 = angles(DK // 2, 10000.0).T
    a1 = angles(ROT, 500000.0)
    pad = np.zeros((NB * P + P, ROT))
    pad[:NT] = a1
    a1 = pad.reshape(NB + 1, P, ROT).transpose(1, 0, 2)
    reset = np.ones((H, NT))
    reset[:, 0:T:P] = 0
    reset[:, T::DS] = 0
    first = np.zeros((H, DB, DS + 1))
    first[:, :, 0] = -3e38
    newmask = np.full((2 * S, DB, S), NEG)
    for b in range(DB):
        for j in range(DS):
            q = np.arange(2 * S) % DS
            newmask[q >= j, b, DS * b + j] = 0.0
    r2 = np.arange(2 * S)
    tabs = {
        "ident": np.eye(P),
        "mask_st": np.where(rel >= 0, 0.0, NEG),
        "mask_qk": np.where(rel.T >= 0, 0.0, NEG),
        "mask_st_s": np.where(same & (rs >= 0), 0.0, NEG),
        "decay": dec.reshape(P, H * P),
        "decay_s": decs.reshape(S, H * S),
        "gin": np.broadcast_to((gam[:, None] ** (t + 1)).reshape(1, H * P), (P, H * P)),
        "gin_s": np.broadcast_to((gam[:, None] ** (st % DS + 1)).reshape(1, H * S), (P, H * S)),
        "kout": gam[None, :] ** (P - 1 - t)[:, None],
        "kout_s": gam[None, :] ** (DS - 1 - st % DS)[:, None],
        "batch_of": (st[:, None] // DS == np.arange(DB)[None, :]),
        "cos0": np.cos(a0), "sin0": np.sin(a0),
        "rot1": np.stack([np.cos(a1), np.sin(a1)], 1).reshape(P, 2 * (NB + 1) * ROT),
        "reset": reset, "first": first.reshape(H, DB * (DS + 1)),
        "ones4": np.ones((H, P)),
        "select": np.eye(H)[:, :, None] * np.ones((1, 1, P)),
        "own_head": (np.arange(4 * S)[:, None] % S // DS == np.arange(HC)[None, :]),
        "to_query": (np.arange(4 * S)[:, None] % DS == np.arange(DS)[None, :]),
        "new_mask": newmask.reshape(2 * S, DB * S),
    }
    return {k: np.ascontiguousarray(v.reshape(v.shape[0], -1), dtype=f) for k, v in tabs.items()}


class Chain:

    def __init__(self, eng, sem):
        self.eng, self.sem, self.n = eng, sem, 0

    def link(self, ins):
        self.n += 1
        ins.then_inc(self.sem, 1)
        self.eng.wait_ge(self.sem, self.n)

    def clear(self):
        self.eng.sem_clear(self.sem)
        self.n = 0


class Core:

    def __init__(self, nc, ins, tabs, outs, ctx):
        self.nc, self.x, self.tab, self.out, self.ctx = nc, ins, tabs, outs, ctx

        def dram(name, shape):
            return nc.dram_tensor(name, shape, F32, kind="Internal").ap()

        self.s_qk = dram("s_qk", (2 * QK // P, P, NT))
        self.s_v = dram("s_v", (NT, 2 * D))
        self.s_g = dram("s_g", (NT, 2 * D))
        self.s_x1 = dram("s_x1", (NT, D))
        self.s_y1 = dram("s_y1", (NT, D))
        self.s_a1 = dram("s_a1", (S, D))
        self.s_gates = dram("s_gates", (H, 2 * NT))
        SPACER["sem"] = ctx.enter_context(nc.semaphore("spacer"))
        self.ident = ctx.enter_context(nc.sbuf_tensor("ident", [P, P], F32))


class Stage:

    def __init__(self, nc, name):
        self.nc, self.name, self.ctx, self.held = nc, name, ExitStack(), []

    def __enter__(self):
        return self

    def __exit__(self, kind, *a):
        self.ctx.close()
        if kind is None:
            self.nc.clear_and_free_semaphores(self.held)
            self.nc.all_engine_barrier()

    def sb(self, name, shape, dt=F32):
        return self.ctx.enter_context(self.nc.sbuf_tensor(f"{self.name}_{name}", shape, dt))

    def ps(self, name, shape):
        return self.ctx.enter_context(self.nc.psum_tensor(f"{self.name}_{name}", shape, F32))

    def sem(self, name):
        self.held.append(self.nc.alloc_semaphore(name=f"{self.name}_{name}"))
        return self.held[-1]

    def sems(self, name, n):
        return [self.sem(f"{name}{i}") for i in range(n)]


SPACER = {}


def wait_counted(eng, sem, value):
    eng.wait_ge(sem, value)
    eng.sem_inc(SPACER["sem"], 1)


def rows_of(b):
    return S if b == NB else P


def norm_to_columns(c, h_hi, h_lo):
    nc, g = c.nc, c.x
    with Stage(nc, "nx") as st:
        xb = st.sb("xb", [P, 2, D])
        junk = st.sb("junk", [P, D])
        ms = st.sb("ms", [P, 2])
        rstd = st.sb("rstd", [P, 2])
        half = st.sb("half", [P, 1])
        gcol = st.sb("gcol", [P, KD])
        grow = st.sb("grow", [KD, P])
        ps = st.ps("ps", [P, 4, 512])
        psg = st.ps("psg", [P, 512])
        s_const, s_g, s_gcol = st.sem("const"), st.sem("g"), st.sem("gcol")
        loaded = st.sems("loaded", 2)
        summed, scaled, rooted, turned, taken = (st.sem(n) for n in ("summed", "scaled", "rooted", "turned", "taken"))
        act_chain, pool_chain = st.sem("act_chain"), st.sem("pool_chain")
        x_prompt = g["x_prompt"].rearrange("a (n p) d -> (a n) p d", p=P)
        x_sample = g["x_sample"].rearrange("a t d -> (a t) d")

        with nc.Block() as block:

            @block.sync
            def _(sp):
                sp.dma_start(c.ident[:], c.tab["ident"]).then_inc(s_const, 16)
                sp.dma_start(grow[:], g["norm_pre"][0, :].rearrange("(k p) -> k p", p=P)).then_inc(s_g, 16)
                for b in range(2):
                    sp.dma_start(xb[:, b, :], x_prompt[b]).then_inc(loaded[b], 16)
                with sp.Fori(1, NB // 2) as i:
                    for s in range(2):
                        sp.wait_ge(turned, 2 * i + s - 1)
                        sp.dma_start(xb[:, s, :], x_prompt[bass.ds(2 * i + s, 1)].rearrange("a p d -> (a p) d")).then_inc(loaded[s], 16)
                sp.wait_ge(turned, NB - 1)
                sp.dma_start(xb[0:S, 0, :], x_sample).then_inc(loaded[0], 16)

            @block.scalar
            def _(act):
                def one(i, s, rows):
                    act.wait_ge(loaded[s], 16 * i + 16)
                    act.activation(junk[0:rows, :], xb[0:rows, s, :], ACT.Square, accum_out=ms[0:rows, s:s + 1]).then_inc(summed, 1)
                    act.wait_ge(rooted, 2 * i + s + 1)
                    act.activation(xb[0:rows, s, :], xb[0:rows, s, :], ACT.Copy, scale=rstd[0:rows, s:s + 1]).then_inc(scaled, 1)

                with act.Fori(0, NB // 2) as i:
                    for s in range(2):
                        one(i, s, P)
                one(NB // 2, 0, S)

            @block.gpsimd
            def _(pool):
                ch = Chain(pool, pool_chain)
                ch.link(pool.memset(half[:], -0.5))
                ch.clear()

                def one(i, s, rows):
                    wait_counted(pool, summed, 2 * i + s + 1)
                    ch.link(pool.tensor_scalar(ms[0:rows, s:s + 1], ms[0:rows, s:s + 1], 1.0 / D, EPS, ALU.mult, ALU.add))
                    ch.clear()
                    pool.tensor_tensor(rstd[0:rows, s:s + 1], ms[0:rows, s:s + 1], half[0:rows, :], ALU.pow).then_inc(rooted, 1)

                with pool.Fori(0, NB // 2) as i:
                    for s in range(2):
                        one(i, s, P)
                one(NB // 2, 0, S)

            @block.tensor
            def _(pe):
                pe.wait_ge(s_const, 16)
                pe.wait_ge(s_g, 16)
                pe.transpose(psg[:, 0:KD], grow[:], c.ident[0:KD, 0:KD]).then_inc(s_gcol, 1)

                def one(i, s, rows):
                    pe.wait_ge(scaled, 2 * i + s + 1)
                    pe.wait_ge(taken, 2 * i + s + 1)
                    for k in range(KD):
                        last = pe.transpose(ps[:, 2 * s + k // 4, (k % 4) * P:(k % 4) * P + rows],
                                            xb[0:rows, s, k * P:(k + 1) * P], c.ident[0:rows, 0:rows])
                    last.then_inc(turned, 1)

                with pe.Fori(0, NB // 2) as i:
                    for s in range(2):
                        one(i, s, P)
                one(NB // 2, 0, S)

            @block.vector
            def _(dve):
                dve.sem_inc(taken, 2)
                dve.wait_ge(s_gcol, 1)
                dve.tensor_copy(gcol[:], psg[:, 0:KD]).then_inc(act_chain, 1)
                dve.wait_ge(act_chain, 1)

                def one(i, s, rows, token):
                    dve.wait_ge(turned, 2 * i + s + 1)
                    for b in range(2):
                        last = dve.tensor_tensor(
                            h_hi[:, 4 * b:4 * b + 4, token],
                            ps[:, 2 * s + b, :].rearrange("p (k t) -> p k t", t=P)[:, :, 0:rows],
                            gcol[:, 4 * b:4 * b + 4].unsqueeze(2).broadcast_to([P, 4, rows]), ALU.mult)
                    last.then_inc(act_chain, 1)
                    dve.wait_ge(act_chain, 2)
                    dve.sem_clear(act_chain)
                    dve.sem_inc(act_chain, 1)
                    for k in range(KD):
                        last = dve.scalar_tensor_tensor(
                            out=h_lo[:, k, token], in0=ps[:, 2 * s + k // 4, (k % 4) * P:(k % 4) * P + rows],
                            scalar=gcol[:, k:k + 1], in1=h_hi[:, k, token].bitcast(F32), op0=ALU.mult, op1=ALU.subtract)
                    last.then_inc(taken, 1)

                with dve.Fori(0, NB // 2) as i:
                    for s in range(2):
                        one(i, s, P, bass.ds(i * (2 * P) + s * P, P))
                one(NB // 2, 0, S, slice(T, NT))


TN = NT // 3
LASTP = T - 2 * TN
RAW = T + CW - 1 + DB * (DS + CW - 1)


def project_layer0(c, h_hi, h_lo):
    nc, g = c.nc, c.x
    w = g["w_in_a"][0].rearrange("(k p) n -> p k n", p=P)
    with Stage(nc, "p0") as st:
        wst = st.sb("wst", [P, KD, DK])
        wqk = st.sb("wqk", [P, 2, KD, 512], F32R)
        wvz = st.sb("wvz", [P, 2, KD, 512], F32R)
        wg = st.sb("wg", [P, KD, 2 * H])
        wg_hl = st.sb("wg_hl", [P, 2, KD, 32 + H], F32R)
        raw = st.sb("raw", [P, 2, RAW])
        acc = st.sb("acc", [P, 2, NT])
        sig = st.sb("sig", [P, 2, NT])
        cos = st.sb("cos", [P, NT])
        sin = st.sb("sin", [P, NT])
        res = st.sb("res", [P, 2, NT])
        taps = st.sb("taps", [P, QK // P, CW + 1])
        tap_rows = raw[:].rearrange("p a t -> p (a t)")[0:CW + 1, 0:QK]
        buf_rows = acc[:].rearrange("p a t -> p (a t)")[0:DB * (CW - 1), 0:QK]
        gates = sig[0:H]
        bufT = st.sb("bufT", [P, QK // P, DB * (CW - 1)])
        tail = st.sb("tail", [P, 2, CW - 1 + DB * (CW - 1)])
        tail_rows = st.sb("tail_rows", [(DB + 1) * (CW - 1), QK])
        vst = st.sb("vst", [P, 2, 2 * DK])
        gst = st.sb("gst", [P, 2, DK])
        ez = st.sb("ez", [P, 2, DK])
        gnb = st.sb("gnb", [P, DK])
        gate_bias = st.sb("gate_bias", [H, 2])
        col = [st.ps(f"col{i}", [P, 3, 512]) for i in range(2)]
        row = st.ps("row", [P, 2, 512])
        s_const, s_wg, s_tr, s_tr2, s_gate, s_gate0 = (st.sem(n) for n in ("const", "wg", "tr", "tr2", "gate", "gate0"))
        w_loaded, w_taken, qk_split, vz_split, qk_used, vz_used = (st.sem(n) for n in ("w_loaded", "w_taken", "qk_split", "vz_split", "qk_used", "vz_used"))
        wg_high, gates_stored = st.sem("wg_high"), st.sem("gates_stored")
        tile_ready, tile_taken, row_ready = (st.sem(n) for n in ("tile_ready", "tile_taken", "row_ready"))
        raw_ready, raw_free, acc_ready, sig_ready = (st.sem(n) for n in ("raw_ready", "raw_free", "acc_ready", "sig_ready"))
        res_ready, tail_ready, tail_turned, tail_saved = (st.sem(n) for n in ("res_ready", "tail_ready", "tail_turned", "tail_saved"))
        v_taken, e_ready, z_taken = st.sem("v_taken"), st.sem("e_ready"), st.sem("z_taken")
        s_gnb, gnb_used = st.sem("gnb"), st.sem("gnb_used")
        res_stored, v_stored, g_stored = st.sems("res_stored", 2), st.sems("v_stored", 2), st.sems("g_stored", 2)
        s_end = st.sem("end")
        dve_chain, act_chain, pool_chain = st.sem("dve_chain"), st.sem("act_chain"), st.sem("pool_chain")
        HEADS = 2 * H
        NR = CW - 1

        def head_loop(eng, body):
            with eng.Fori(0, H) as m:
                body(m, m, True)
            with eng.Fori(H, HEADS) as m:
                body(m, m - H, False)

        def v_count(m, b):
            per = (NB + 2 - b % 2) // 2
            return m * (16 * per) + (b // 2 + 1) * 16

        with nc.Block() as block:

            @block.sync
            def _(sp):
                sp.dma_start(wg[:], w[:, :, OFF_GATE:OFF_GATE + 2 * H]).then_inc(s_wg, 16)
                sp.dma_start(gate_bias[:, 0:1], g["b_gate_i"].rearrange("a h -> h a")).then_inc(s_wg, 16)
                sp.dma_start(gate_bias[:, 1:2], g["b_gate_f"].rearrange("a h -> h a")).then_inc(s_wg, 16)
                sp.dma_start(tap_rows[0:CW, :], g["conv_w"][0]).then_inc(s_const, 16)
                sp.dma_start(tap_rows[CW:CW + 1, :], g["conv_b"]).then_inc(s_const, 16)
                sp.dma_start(buf_rows[:], g["state_mlstm_conv"].rearrange("a b r n -> (a b r) n")).then_inc(s_const, 16)
                sp.dma_start(cos[:], c.tab["cos0"]).then_inc(s_const, 16)
                sp.dma_start(sin[:], c.tab["sin0"]).then_inc(s_const, 16)

                def load(m, h, piece, ret):
                    wait_counted(sp, w_taken, m * 4 + (piece + 1))
                    base = (OFF_RET if ret else 0) + piece * D
                    sp.dma_start(wst[:], w[:, :, bass.ds(h * DK + base, DK)]).then_inc(w_loaded, 16)

                def load_gn(m, h, ret):
                    wait_counted(sp, gnb_used, m + 1)
                    gn = g["gn_ret"] if ret else g["gn_mlstm"]
                    sp.dma_start(gnb[:], gn[0, bass.ds(h, 1), :].broadcast_to([P, DK])).then_inc(s_gnb, 16)

                def store_tiles(m, h, first_tile, which):
                    for j in which:
                        wait_counted(sp, res_ready, m * 4 + (j + 1))
                        tile = first_tile + (j // 2) * (D // P) + j % 2
                        sp.dma_start(c.s_qk[bass.ds(h * 2 + tile, 1)].rearrange("a p t -> (a p) t"), res[:, j % 2, :]).then_inc(res_stored[j % 2], 16)

                def store_rows(m, blocks):
                    at = bass.ds(m * DK, DK)
                    for b in blocks:
                        n, s = rows_of(b), b % 2
                        wait_counted(sp, v_taken, m * (NB + 1) + (b + 3))
                        sp.dma_start(c.s_v[b * P:b * P + n, at], vst[0:n, s, 0:DK]).then_inc(v_stored[s], 16)
                        wait_counted(sp, z_taken, m * (NB + 1) + (b + 3))
                        sp.dma_start(c.s_g[b * P:b * P + n, at], gst[0:n, s, :]).then_inc(g_stored[s], 16)

                def head(m, h, ret, nxt):
                    tile = QK // P if ret else 0
                    load(m, h, 3, ret)
                    load_gn(m, h, ret)
                    store_tiles(m, h, tile, (0, 1))
                    if nxt:
                        load(m + 1, nxt[0], 0, nxt[1])
                    store_tiles(m, h, tile, (2, 3))
                    store_rows(m, range(0, 3))
                    if nxt:
                        load(m + 1, nxt[0], 1, nxt[1])
                    store_rows(m, range(3, NB))
                    if nxt:
                        load(m + 1, nxt[0], 2, nxt[1])
                    store_rows(m, range(NB, NB + 1))

                for piece in range(3):
                    load(0, 0, piece, False)
                with sp.Fori(0, H - 1) as m:
                    head(m, m, False, (m + 1, False))
                head(H - 1, H - 1, False, (0, True))
                with sp.Fori(H, HEADS - 1) as m:
                    head(m, m - H, True, (m - H + 1, True))
                head(HEADS - 1, H - 1, True, None)
                for s in range(2):
                    sp.wait_ge(res_stored[s], 16 + 32 * HEADS)
                    sp.wait_ge(v_stored[s], 16 + 16 * HEADS * ((NB + 2 - s) // 2))
                    sp.wait_ge(g_stored[s], 16 + 16 * HEADS * ((NB + 2 - s) // 2))
                sp.wait_ge(tail_saved, 4 * H)
                sp.dma_start(c.out["conv_p"][0, 0], tail_rows[0:NR, :]).then_inc(s_end, 16)
                sp.dma_start(c.out["conv_s"].rearrange("a b r n -> (a b r) n"),
                             tail_rows[NR:NR + DB * NR, :]).then_inc(s_end, 16)
                sp.wait_ge(s_end, 32)

            @block.tensor
            def _(pe):
                def columns(out, wx):
                    for r in range(3):
                        at = slice(r * TN, (r + 1) * TN)
                        for k in range(KD):
                            pe.matmul(out[:, r, 0:TN], wx[:, 0, k, :], h_hi[:, k, at], start=k == 0, stop=False)
                            pe.matmul(out[:, r, 0:TN], wx[:, 0, k, :], h_lo[:, k, at], start=False, stop=False)
                            last = pe.matmul(out[:, r, 0:TN], wx[:, 1, k, :], h_hi[:, k, at], start=False, stop=k == KD - 1)
                    return last

                pe.wait_ge(s_const, 80)
                n = QK // P
                for t in range(n):
                    last = pe.transpose(row[:, 0, t * (CW + 1):(t + 1) * (CW + 1)],
                                        tap_rows[:, t * P:(t + 1) * P], c.ident[0:CW + 1, 0:CW + 1])
                for t in range(n):
                    last = pe.transpose(row[:, 1, t * DB * NR:(t + 1) * DB * NR],
                                        buf_rows[:, t * P:(t + 1) * P], c.ident[0:DB * NR, 0:DB * NR])
                last.then_inc(s_tr, 1)
                pe.wait_ge(wg_high, 2)
                columns(col[0][0:32 + H], wg_hl[:]).then_inc(s_gate, 1)
                pe.wait_ge(s_tr2, 4)

                def body(m, h, mlstm):
                    pe.wait_ge(qk_split, m * 2 + 2)
                    for j in range(4):
                        pe.wait_ge(tile_taken, m * 4 + (j + 1))
                        columns(col[j % 2], wqk[:, :, :, j * P:(j + 1) * P]).then_inc(tile_ready, 1)
                        if mlstm and j > 0:
                            turn_tail(m, j - 1)
                    pe.wait_ge(vz_split, m * 2 + 2)
                    for b in range(NB + 1):
                        pe.wait_ge(v_taken, m * (NB + 1) + (b + 1))
                        n = rows_of(b)
                        at = slice(b * P, b * P + n)
                        for k in range(KD):
                            pe.matmul(row[0:n, b % 2, :], h_hi[:, k, at], wvz[:, 0, k, :], start=k == 0, stop=False)
                            pe.matmul(row[0:n, b % 2, :], h_hi[:, k, at], wvz[:, 1, k, :], start=False, stop=False)
                            last = pe.matmul(row[0:n, b % 2, :], h_lo[:, k, at], wvz[:, 0, k, :], start=False, stop=k == KD - 1)
                        last.then_inc(row_ready, 1)
                        if mlstm and b == 0:
                            turn_tail(m, 3)

                def turn_tail(m, j):
                    pe.wait_ge(tail_ready, m * 4 + (j + 1))
                    pe.transpose(col[j % 2][0:(DB + 1) * NR, 2, 3 * P:], tail[:, j % 2, :], c.ident[:]).then_inc(tail_turned, 1)

                head_loop(pe, body)

            @block.scalar
            def _(act):
                act.wait_ge(s_wg, 48)
                act.wait_ge(wg_high, 1)
                for q in range(2):
                    last = act.activation(wg_hl[:, 0, :, 32 * q:32 * q + H], wg[:, :, q * H:(q + 1) * H], ACT.Copy)
                last.then_inc(s_gate0, 1)
                act.wait_ge(s_gate, 1)
                for q in range(2):
                    for r in range(3):
                        last = act.activation(gates[:, q, r * TN:(r + 1) * TN], col[0][32 * q:32 * q + H, r, 0:TN], ACT.Identity,
                                              bias=gate_bias[:, q:q + 1])
                    last.then_inc(s_tr2, 1)
                act.wait_ge(s_tr2, 4)
                act.dma_start(c.s_gates, gates.rearrange("h q t -> h (q t)")).then_inc(gates_stored, 16)
                act.wait_ge(gates_stored, 16)

                def copy_tile(m, j):
                    s = j % 2
                    act.wait_ge(tile_ready, m * 4 + (j + 1))
                    act.wait_ge(raw_free, m * 4 + (j + 1))
                    for r in range(3):
                        n = TN if r < 2 else LASTP
                        act.activation(raw[:, s, NR + r * TN:NR + r * TN + n], col[s][:, r, 0:n], ACT.Copy)
                    act.activation(raw[:, s, NR + T:].rearrange("p (b t) -> p b t", b=DB)[:, :, NR:],
                                   col[s][:, 2, LASTP:TN].rearrange("p (b t) -> p b t", b=DB), ACT.Copy).then_inc(raw_ready, 1)

                def body(m, h, mlstm):
                    for j in range(4):
                        copy_tile(m, j)
                        if mlstm:
                            if j > 0:
                                sigmoid_exp(m, j - 1)
                    if mlstm:
                        sigmoid_exp(m, 3)
                    for b in range(NB + 1):
                        n = rows_of(b)
                        s = b % 2
                        act.wait_ge(row_ready, m * (NB + 1) + (b + 1))
                        act.wait_ge(z_taken, m * (NB + 1) + (b + 1))
                        act.activation(ez[0:n, s, :], row[0:n, s, DK:], ACT.Exp, scale=-1.0).then_inc(e_ready, 1)
                        act.wait_ge(v_stored[s], v_count(m, b))
                        act.activation(vst[0:n, s, :], row[0:n, s, :], ACT.Copy).then_inc(v_taken, 1)

                def sigmoid_exp(m, j):
                    act.wait_ge(acc_ready, m * 4 + (j + 1))
                    act.activation(sig[:, j % 2, :], acc[:, j % 2, :], ACT.Exp, scale=-1.0).then_inc(sig_ready, 1)

                head_loop(act, body)

            @block.gpsimd
            def _(pool):
                ch = Chain(pool, pool_chain)
                pool.sem_inc(w_taken, 1)

                def body(m, h, mlstm):
                    ch.clear()
                    for piece in range(4):
                        into, split, used = (wqk, qk_split, qk_used) if piece < 2 else (wvz, vz_split, vz_used)
                        cols = slice((piece % 2) * DK, (piece % 2 + 1) * DK)
                        if piece % 2 == 0:
                            wait_counted(pool, used, m + 1)
                        wait_counted(pool, w_loaded, m * 64 + (piece * 16 + 16))
                        ch.link(pool.tensor_copy(into[:, 0, :, cols], wst[:]))
                        ch.link(pool.tensor_tensor(into[:, 1, :, cols], wst[:], into[:, 0, :, cols].bitcast(F32), ALU.subtract))
                        pool.sem_inc(split, 1)
                        pool.sem_inc(w_taken, 1)

                head_loop(pool, body)

            @block.vector
            def _(dve):
                ch = Chain(dve, dve_chain)
                ch.link(dve.memset(wg_hl[:].bitcast(F32), 0.0))
                dve.sem_inc(wg_high, 1)
                dve.wait_ge(s_gate0, 1)
                for q in range(2):
                    last = dve.tensor_tensor(wg_hl[:, 1, :, 32 * q:32 * q + H], wg[:, :, q * H:(q + 1) * H],
                                             wg_hl[:, 0, :, 32 * q:32 * q + H].bitcast(F32), ALU.subtract)
                ch.link(last)
                dve.sem_inc(wg_high, 1)
                dve.wait_ge(s_tr, 1)
                dve.tensor_copy(taps[:], row[:, 0, 0:(QK // P) * (CW + 1)].rearrange("p (t n) -> p t n", n=CW + 1)).then_inc(s_tr2, 1)
                dve.tensor_copy(bufT[:], row[:, 1, 0:(QK // P) * DB * NR].rearrange("p (t n) -> p t n", n=DB * NR)).then_inc(s_tr2, 1)
                dve.wait_ge(s_tr2, 4)
                ch.link(dve.memset(raw[:, :, 0:NR], 0.0))
                dve.sem_inc(tile_taken, 2)
                dve.sem_inc(raw_free, 2)
                dve.sem_inc(v_taken, 2)
                dve.sem_inc(z_taken, 2)
                dve.sem_inc(qk_used, 1)
                dve.sem_inc(vz_used, 1)
                dve.sem_inc(gnb_used, 1)
                for s in range(2):
                    for q in (res_stored, v_stored, g_stored):
                        dve.sem_inc(q[s], 16)

                def z_rows(m, h):
                    dve.wait_ge(s_gnb, m * 16 + 16)
                    for b in range(NB + 1):
                        n, s = rows_of(b), b % 2
                        dve.wait_ge(e_ready, m * (NB + 1) + (b + 1))
                        e = ez[0:n, s, :]
                        ch.link(dve.tensor_scalar(e, e, 1.0, None, ALU.add))
                        ch.link(dve.reciprocal(e, e))
                        dve.wait_ge(v_taken, m * (NB + 1) + (b + 3))
                        ch.link(dve.tensor_tensor(e, vst[0:n, s, DK:], e, ALU.mult))
                        dve.wait_ge(g_stored[s], v_count(m, b))
                        last = dve.tensor_tensor(gst[0:n, s, :], e, gnb[0:n, :], ALU.mult)
                        ch.link(last)
                        dve.sem_inc(z_taken, 1)
                    dve.sem_inc(gnb_used, 1)
                    dve.sem_inc(vz_used, 1)

                def conv(m, h):
                    for j in range(4):
                        s = j % 2
                        tile = (j // 2) * (D // P) + j % 2
                        dve.wait_ge(raw_ready, m * 4 + (j + 1))
                        if j == 3:
                            dve.sem_inc(qk_used, 1)
                        r = raw[:, s, :]
                        rs = r[:, NR + T:].rearrange("p (b t) -> p b t", b=DB)
                        ch.link(dve.tensor_copy(rs[:, :, 0:NR], bufT[:, bass.ds(h * 2 + tile, 1), :].rearrange("p a (b t) -> p (a b) t", b=DB)))
                        ch.link(dve.tensor_copy(tail[:, s, 0:NR], r[:, T:T + NR]))
                        dve.tensor_copy(tail[:, s, NR:].rearrange("p (b t) -> p b t", b=DB), rs[:, :, DS:]).then_inc(tail_ready, 1)
                        a = acc[:, s, 0:T]
                        a_s = acc[:, s, T:].rearrange("p (b t) -> p b t", b=DB)
                        cw = taps[:, bass.ds(h * 2 + tile, 1), :].rearrange("p a n -> p (a n)")
                        dve.tensor_scalar(a, r[:, 0:T], cw[:, 0:1], cw[:, CW:CW + 1], ALU.mult, ALU.add)
                        ch.link(dve.tensor_scalar(a_s, rs[:, :, 0:DS], cw[:, 0:1], cw[:, CW:CW + 1], ALU.mult, ALU.add))
                        for k in range(1, CW):
                            dve.scalar_tensor_tensor(out=a, in0=r[:, k:k + T], scalar=cw[:, k:k + 1], in1=a, op0=ALU.mult, op1=ALU.add)
                            ch.link(dve.scalar_tensor_tensor(out=a_s, in0=rs[:, :, k:k + DS], scalar=cw[:, k:k + 1], in1=a_s,
                                                             op0=ALU.mult, op1=ALU.add))
                        dve.sem_inc(acc_ready, 1)
                        dve.sem_inc(raw_free, 1)
                        if j > 0:
                            silu(m, j - 1)
                        save_tail(m, h, j)
                    silu(m, 3)

                def save_tail(m, h, j):
                    tile = (j // 2) * (D // P) + j % 2
                    dve.wait_ge(tail_turned, m * 4 + (j + 1))
                    ch.link(dve.tensor_copy(tail_rows[:, bass.ds((h * 2 + tile) * P, P)], col[j % 2][0:(DB + 1) * NR, 2, 3 * P:]))
                    dve.sem_inc(tail_saved, 1)
                    dve.sem_inc(tile_taken, 1)

                def silu(m, j):
                    s = j % 2
                    dve.wait_ge(sig_ready, m * 4 + (j + 1))
                    e = sig[:, s, :]
                    ch.link(dve.tensor_scalar(e, e, 1.0, None, ALU.add))
                    ch.link(dve.reciprocal(e, e))
                    dve.wait_ge(res_stored[s], m * 32 + (j // 2 + 1) * 16)
                    ch.link(dve.scalar_tensor_tensor(out=res[:, s, :], in0=acc[:, s, :], scalar=DK ** -0.5 if j < 2 else 1.0,
                                                     in1=e, op0=ALU.mult, op1=ALU.mult))
                    dve.sem_inc(res_ready, 1)

                def rotate(m, h):
                    for pair in range(2):
                        dve.wait_ge(raw_ready, m * 4 + (2 * pair + 2))
                        dve.sem_inc(tile_taken, 2)
                        if pair == 1:
                            dve.sem_inc(qk_used, 1)
                        scale = 1.0 if pair == 0 else DK ** -0.5
                        for out, x, table in ((0, 0, cos), (1, 0, sin)):
                            for part in range(2):
                                o, i = spans(part, acc[:, out, :], raw[:, x, :])
                                dve.scalar_tensor_tensor(out=o, in0=i, scalar=scale, in1=spans(part, table[:, :])[0], op0=ALU.mult, op1=ALU.mult)
                        for out, x, table in ((0, 1, sin), (1, 1, cos)):
                            for part in range(2):
                                o, i = spans(part, sig[:, out, :], raw[:, x, :])
                                last = dve.scalar_tensor_tensor(out=o, in0=i, scalar=scale, in1=spans(part, table[:, :])[0], op0=ALU.mult, op1=ALU.mult)
                        ch.link(last)
                        dve.sem_inc(raw_free, 2)
                        for s, op in ((0, ALU.subtract), (1, ALU.add)):
                            dve.wait_ge(res_stored[s], m * 32 + (pair + 1) * 16)
                            ch.link(dve.tensor_tensor(res[:, s, :], acc[:, s, :], sig[:, s, :], op))
                            dve.sem_inc(res_ready, 1)

                def spans(part, o, i=None):
                    if part == 0:
                        return o[:, 0:T], None if i is None else i[:, NR:NR + T]
                    o = o[:, T:NT].rearrange("p (b t) -> p b t", b=DB)
                    return o, None if i is None else i[:, NR + T:].rearrange("p (b t) -> p b t", b=DB)[:, :, NR:]

                def body(m, h, mlstm):
                    ch.clear()
                    if mlstm:
                        conv(m, h)
                    else:
                        rotate(m, h)
                    z_rows(m, h)

                head_loop(dve, body)


A, EM, WS = range(3)
MPREV, SCALE = range(2)


def gate_rows(c, rows, cols, spread):
    nc = c.nc
    NCH = NB + DB
    with Stage(nc, "gr") as st:
        gates = st.sb("gates", [H, 2, NT])
        reset = st.sb("reset", [H, NT])
        first = st.sb("first", [H, DB, DS + 1])
        ext = st.sb("ext", [H, DB, DS + 1])
        mext = st.sb("mext", [H, DB, DS + 1])
        zeros = st.sb("zeros", [H, P])
        ones = st.sb("ones", [H, P])
        b = st.sb("b", [H, NT])
        a = st.sb("a", [H, NT])
        M = st.sb("M", [H, NT])
        em = st.sb("em", [H, NT])
        ws = st.sb("ws", [H, NT])
        mp = st.sb("mp", [H, NCH + 1])
        ml = st.sb("ml", [H, NCH])
        bl = st.sb("bl", [H, NCH])
        mnew = st.sb("mnew", [H, DB])
        sc = st.sb("sc", [H, NCH])
        diag = st.sb("diag", [H, 2, NCH, H])
        pt = st.ps("pt", [P, 512])
        pb = st.ps("pb", [P, 512])
        s_in, s_dve, s_act, s_pe, s_out = (st.sem(n) for n in ("in", "dve", "act", "pe", "out"))
        dve_chain, logs_ready, s_gates = st.sem("dve_chain"), st.sem("logs_ready"), st.sem("gates")

        def by_chunk(x, prompt):
            return x[:, 0:T].rearrange("h (n t) -> h n t", t=P) if prompt else x[:, T:].rearrange("h (n t) -> h n t", t=DS)

        with nc.Block() as block:

            @block.sync
            def _(sp):
                sp.dma_start(gates[:].rearrange("h q t -> h (q t)"), c.s_gates).then_inc(s_gates, 16)
                sp.dma_start(reset[:], c.tab["reset"]).then_inc(s_in, 16)
                sp.dma_start(first[:], c.tab["first"].rearrange("h (b t) -> h b t", b=DB)).then_inc(s_in, 16)
                sp.dma_start(ones[:], c.tab["ones4"]).then_inc(s_in, 16)
                sp.dma_start(mp[:, NB:NCH], c.x["state_mlstm_m"][0].rearrange("b h -> h b"), allow_slow_non_contiguous=True).then_inc(s_in, 16)
                sp.wait_ge(s_dve, 1)
                sp.dma_start(c.out["m_p"].rearrange("a b h -> h (a b)"), mp[:, NCH:NCH + 1]).then_inc(s_out, 16)
                sp.dma_start(c.out["m_s"][0].rearrange("b h -> h b"), mnew[:], allow_slow_non_contiguous=True).then_inc(s_out, 16)
                sp.wait_ge(s_out, 32)

            @block.vector
            def _(dve):
                ch = Chain(dve, dve_chain)
                f = gates[:, 1, :]
                dve.wait_ge(s_gates, 16)
                ch.link(dve.scalar_tensor_tensor(out=b[:], in0=f, scalar=-1.0, in1=f, op0=ALU.mult, op1=ALU.min))
                dve.sem_inc(logs_ready, 1)
                ch.link(dve.memset(zeros[:], 0.0))
                dve.wait_ge(s_act, 2)
                ch.link(dve.scalar_tensor_tensor(out=f, in0=f, scalar=0.0, in1=b[:], op0=ALU.min, op1=ALU.subtract))
                dve.wait_ge(s_in, 64)
                ch.link(dve.tensor_tensor_scan(b[:], reset[:], f, 0.0, ALU.mult, ALU.add))
                ch.link(dve.tensor_tensor(a[:], gates[:, 0, :], b[:], ALU.subtract))
                ch.link(dve.tensor_copy(ext[:, :, 0:1], mp[:, NB:NCH].unsqueeze(2)))
                ch.link(dve.tensor_copy(ext[:, :, 1:], by_chunk(a, False)))
                flat = "h b t -> h (b t)"
                ch.link(dve.tensor_tensor_scan(mext[:].rearrange(flat), first[:].rearrange(flat), ext[:].rearrange(flat), 0.0, ALU.add, ALU.max))
                ch.link(dve.tensor_copy(by_chunk(M, False), mext[:, :, 1:]))
                for prompt, n0, n1 in ((True, 0, NB), (False, NB, NCH)):
                    ch.link(dve.tensor_copy(bl[:, n0:n1].unsqueeze(2), by_chunk(b, prompt)[:, :, -1:]))
                ch.link(dve.tensor_copy(ml[:, NB:].unsqueeze(2), mext[:, :, DS:]))
                ch.link(dve.memset(mp[:, 0:1], 0.0))
                for n in range(NB):
                    ch.link(dve.tensor_tensor_scan(M[:, n * P:(n + 1) * P], zeros[:], a[:, n * P:(n + 1) * P],
                                                   mp[:, n:n + 1], ALU.add, ALU.max))
                    ch.link(dve.tensor_copy(ml[:, n:n + 1], M[:, n * P + P - 1:n * P + P]))
                    after = n + 1 if n < NB - 1 else NCH
                    ch.link(dve.tensor_tensor(mp[:, after:after + 1], ml[:, n:n + 1], bl[:, n:n + 1], ALU.add))
                ch.link(dve.tensor_tensor(mnew[:], ml[:, NB:], bl[:, NB:], ALU.add))
                dve.sem_inc(s_dve, 1)
                ch.link(dve.tensor_scalar(rows[:, 0, :], M[:], -1.0, None, ALU.mult))
                ch.link(dve.tensor_tensor(em[:], rows[:, 0, :], b[:], ALU.subtract))
                for prompt, n0, n1, w in ((True, 0, NB, P), (False, NB, NCH, DS)):
                    shape = [H, n1 - n0, w]
                    ch.link(dve.tensor_tensor(by_chunk(rows[:, 1, :], prompt), by_chunk(rows[:, 0, :], prompt),
                                              mp[:, n0:n1].unsqueeze(2).broadcast_to(shape), ALU.add))
                    ch.link(dve.tensor_tensor(by_chunk(ws, prompt), by_chunk(a, prompt),
                                              ml[:, n0:n1].unsqueeze(2).broadcast_to(shape), ALU.subtract))
                ch.link(dve.tensor_tensor(sc[:], mp[:, 0:NCH], ml[:], ALU.subtract))
                dve.sem_inc(logs_ready, 1)
                dve.wait_ge(s_act, 3)
                for q, x in ((MPREV, mp[:, 0:NCH]), (SCALE, sc[:])):
                    last = dve.tensor_tensor(diag[:, q], x.unsqueeze(2).broadcast_to([H, NCH, H]),
                                             c.ident[0:H, 0:H].unsqueeze(1).broadcast_to([H, NCH, H]), ALU.mult)
                ch.link(last)
                dve.sem_inc(s_dve, 1)
                dve.wait_ge(s_pe, 1)
                dve.tensor_copy(cols[:, 0:NB], pt[:, 0:NB * 3 * H].rearrange("p (n q h) -> p n q h", n=NB, q=3))
                dve.tensor_copy(cols[0:S, NB], pt[0:S, NB * 3 * H:(NB + 1) * 3 * H].rearrange("p (q h) -> p q h", q=3))
                ch.link(dve.tensor_copy(spread[:], pb[:, 0:2 * NCH * H].rearrange("p (q n h) -> p q n h", q=2, n=NCH)))

            @block.scalar
            def _(act):
                act.wait_ge(logs_ready, 1)
                act.activation(b[:], b[:], ACT.Exp).then_inc(s_act, 1)
                act.wait_ge(s_act, 1)
                act.activation(b[:], b[:], ACT.Ln, bias=1.0).then_inc(s_act, 1)
                act.wait_ge(logs_ready, 2)
                act.activation(rows[:, 1, :], rows[:, 1, :], ACT.Exp)
                act.activation(em[:], em[:], ACT.Exp)
                act.activation(ws[:], ws[:], ACT.Exp)
                act.activation(sc[:], sc[:], ACT.Exp).then_inc(s_act, 1)

            @block.tensor
            def _(pe):
                pe.wait_ge(s_dve, 2)
                for n in range(NB + 1):
                    for q, x in ((A, a), (EM, em), (WS, ws)):
                        pe.transpose(pt[0:rows_of(n), (n * 3 + q) * H:(n * 3 + q + 1) * H],
                                     x[:, n * P:n * P + rows_of(n)], c.ident[0:H, 0:H])
                pe.matmul(pb[:, 0:2 * NCH * H], ones[:], diag[:].rearrange("h q n k -> h (q n k)"), start=True, stop=True).then_inc(s_pe, 1)


class Tail:

    def __init__(self, c, st, width, y, w_out, banks, junk, layer):
        self.c, self.ky, self.y, self.w, self.banks, self.layer = c, width // P, y, w_out, banks, layer
        self.last = layer == 1
        self.yT = st.sb("yT", [P, self.ky, P])
        self.res = st.sb("res", [P, D])
        self.x1 = st.sb("x1", [P, D])
        self.post = st.sb("post", [P, D])
        self.gcol = st.sb("gcol", [P, KD])
        self.grow = st.sb("grow", [KD, P])
        self.ss = st.sb("ss", [P, 4])
        self.half = st.sb("half", [P, 8])
        self.junk = junk
        self.norms_loaded, self.w_loaded, self.y_turned, self.yT_copied = (st.sem(n) for n in ("norms_loaded", "w_loaded", "y_turned", "yT_copied"))
        self.out_ready, self.out_squared, self.out_summed, self.rooted = (st.sem(n) for n in ("out_ready", "out_squared", "out_summed", "rooted"))
        self.x1_ready, self.out_taken, self.x1_squared, self.rows_scaled = (st.sem(n) for n in ("x1_ready", "out_taken", "x1_squared", "rows_scaled"))
        self.rows_turned, self.rows_taken, self.res_loaded, self.x1_stored = (st.sem(n) for n in ("rows_turned", "rows_taken", "res_loaded", "x1_stored"))
        self.tail_chain, self.tail_pool, self.gcol_turned = (st.sem(n) for n in ("tail_chain", "tail_pool", "gcol_turned"))

    def load_constants(self, sp):
        g = self.c.x
        sp.dma_start(self.post[:], g["norm_post"][self.layer:self.layer + 1, :].broadcast_to([P, D])).then_inc(self.norms_loaded, 16)
        if not self.last:
            sp.dma_start(self.grow[:], g["norm_pre"][1, :].rearrange("(k p) -> k p", p=P)).then_inc(self.norms_loaded, 16)

    def norms_wait(self, eng):
        eng.wait_ge(self.norms_loaded, 16 if self.last else 32)

    def pe_start(self, pe):
        if not self.last:
            self.norms_wait(pe)
            pe.transpose(self.banks[6][:, 0:KD], self.grow[:], self.c.ident[0:KD, 0:KD]).then_inc(self.gcol_turned, 1)

    def dve_start(self, dve):
        if not self.last:
            dve.wait_ge(self.gcol_turned, 1)
            dve.tensor_copy(self.gcol[:], self.banks[6][:, 0:KD]).then_inc(self.tail_chain, 1)
            dve.wait_ge(self.tail_chain, 1)
            dve.sem_clear(self.tail_chain)
        dve.sem_inc(self.out_taken, 1)
        dve.sem_inc(self.rows_taken, 1)

    def pool_start(self, pool):
        pool.memset(self.half[:], -0.5).then_inc(self.tail_pool, 1)
        pool.wait_ge(self.tail_pool, 1)
        pool.sem_clear(self.tail_pool)

    def pe(self, pe, n, rows, y_wait):
        y_wait()
        for k in range(self.ky):
            last = pe.transpose(self.banks[k // 4][:, (k % 4) * P:(k % 4) * P + rows],
                                self.y[0:rows, k * P:(k + 1) * P], self.c.ident[0:rows, 0:rows])
        last.then_inc(self.y_turned, 1)
        pe.wait_ge(self.yT_copied, (n + 1) * (self.ky // 4))
        pe.wait_ge(self.w_loaded, 16)
        pe.wait_ge(self.out_taken, n + 1)
        for f in range(2):
            for k in range(self.ky):
                last = pe.matmul(self.banks[4 + f][0:rows, :], self.yT[:, k, 0:rows], self.w[:, k, f * 512:(f + 1) * 512],
                                 start=k == 0, stop=k == self.ky - 1)
        last.then_inc(self.out_ready, 1)
        if self.last:
            return
        pe.wait_ge(self.rows_scaled, n + 1)
        pe.wait_ge(self.rows_taken, n + 1)
        for k in range(KD):
            last = pe.transpose(self.banks[6 + k // 4][:, (k % 4) * P:(k % 4) * P + rows],
                                self.res[0:rows, k * P:(k + 1) * P], self.c.ident[0:rows, 0:rows])
        last.then_inc(self.rows_turned, 1)

    def copy_bank(self, eng, n, rows, b):
        eng.wait_ge(self.y_turned, n + 1)
        o = self.yT[:, 4 * b:4 * b + 4, 0:rows]
        i = self.banks[b].rearrange("p (k t) -> p k t", t=P)[:, :, 0:rows]
        if b % 2 == 0:
            eng.activation(o, i, ACT.Copy).then_inc(self.yT_copied, 1)
        else:
            eng.tensor_copy(o, i).then_inc(self.yT_copied, 1)

    def act(self, act, n, rows, x1_out):
        for b in range(0, self.ky // 4, 2):
            self.copy_bank(act, n, rows, b)
        act.wait_ge(self.out_ready, n + 1)
        for f in range(2):
            last = act.activation(self.junk[0:rows, f, :], self.banks[4 + f][0:rows, :], ACT.Square, accum_out=self.ss[0:rows, f:f + 1])
        last.then_inc(self.out_squared, 1)
        act.wait_ge(self.x1_ready, n + 1)
        act.dma_start(x1_out, self.x1[0:rows, :]).then_inc(self.x1_stored, 16)
        if self.last:
            return
        for f in range(2):
            last = act.activation(self.junk[0:rows, f, :], self.x1[0:rows, f * 512:(f + 1) * 512], ACT.Square,
                                  accum_out=self.ss[0:rows, f:f + 1])
        last.then_inc(self.x1_squared, 1)
        act.wait_ge(self.rooted, 2 * n + 2)
        act.activation(self.res[0:rows, :], self.x1[0:rows, :], ACT.Copy, scale=self.ss[0:rows, 3:4]).then_inc(self.rows_scaled, 1)

    def pool(self, pool, n, rows):
        for i in range(1 if self.last else 2):
            wait_counted(pool, self.out_summed, n + 1 if self.last else 2 * n + (i + 1))
            pool.tensor_scalar(self.ss[0:rows, 2:3], self.ss[0:rows, 2:3], 1.0 / D, EPS, ALU.mult, ALU.add).then_inc(self.tail_pool, 1)
            pool.wait_ge(self.tail_pool, 1)
            pool.tensor_tensor(self.ss[0:rows, 3:4], self.ss[0:rows, 2:3], self.half[0:rows, 0:1], ALU.pow).then_inc(self.tail_pool, 1)
            pool.wait_ge(self.tail_pool, 2)
            pool.sem_clear(self.tail_pool)
            pool.sem_inc(self.rooted, 1)

    def dve(self, dve, n, rows, token):
        ch = Chain(dve, self.tail_chain)
        for b in range(1, self.ky // 4, 2):
            self.copy_bank(dve, n, rows, b)
        dve.wait_ge(self.out_squared, n + 1)
        dve.tensor_tensor(self.ss[0:rows, 2:3], self.ss[0:rows, 0:1], self.ss[0:rows, 1:2], ALU.add).then_inc(self.out_summed, 1)
        dve.wait_ge(self.rooted, n + 1 if self.last else 2 * n + 1)
        self.norms_wait(dve)
        dve.wait_ge(self.x1_stored, n * 16 + 16)
        for f in range(2):
            cols = slice(f * 512, (f + 1) * 512)
            last = dve.scalar_tensor_tensor(out=self.x1[0:rows, cols], in0=self.banks[4 + f][0:rows, :], scalar=self.ss[0:rows, 3:4],
                                            in1=self.post[0:rows, cols], op0=ALU.mult, op1=ALU.mult)
        ch.link(last)
        dve.sem_inc(self.out_taken, 1)
        dve.wait_ge(self.res_loaded, n * 16 + 16)
        ch.link(dve.tensor_tensor(self.x1[0:rows, :], self.x1[0:rows, :], self.res[0:rows, :], ALU.add))
        dve.sem_inc(self.x1_ready, 1)
        ch.clear()
        if self.last:
            return
        dve.wait_ge(self.x1_squared, n + 1)
        dve.tensor_tensor(self.ss[0:rows, 2:3], self.ss[0:rows, 0:1], self.ss[0:rows, 1:2], ALU.add).then_inc(self.out_summed, 1)
        dve.wait_ge(self.rows_turned, n + 1)
        for b in range(2):
            last = dve.tensor_tensor(self.c.hT[:, 4 * b:4 * b + 4, token],
                                     self.banks[6 + b].rearrange("p (k t) -> p k t", t=P)[:, :, 0:rows],
                                     self.gcol[:, 4 * b:4 * b + 4].unsqueeze(2).broadcast_to([P, 4, rows]), ALU.mult)
        last.then_inc(self.rows_taken, 1)


def apply_norms(dve, ch, n, hn, ssq, inv, fac, fac2, em, sums_ready, wait_rooted, wait_gates, y):
    HH = 2 * H
    den = hn[0:n, 0:H, DK:DK + 1].rearrange("p h a -> p (h a)")
    ch.link(dve.scalar_tensor_tensor(out=inv[0:n, 0:H], in0=den, scalar=-1.0, in1=den, op0=ALU.mult, op1=ALU.max))
    ch.link(dve.tensor_tensor(inv[0:n, 0:H], inv[0:n, 0:H], em, ALU.max))
    ch.link(dve.reciprocal(inv[0:n, 0:H], inv[0:n, 0:H]))
    f = fac[0:n, :]
    ch.link(dve.tensor_tensor(f, ssq[0:n, :], inv[0:n, :], ALU.mult))
    ch.link(dve.tensor_tensor(f, f, inv[0:n, :], ALU.mult))
    ch.link(dve.tensor_scalar(f, f, 1.0 / DK, EPS, ALU.mult, ALU.add))
    dve.sem_inc(sums_ready, 1)
    wait_rooted()
    ch.link(dve.tensor_tensor(f, fac2[0:n, :], inv[0:n, :], ALU.mult))
    wait_gates()
    for j in range(HH):
        yj = y[0:n, j * DK:(j + 1) * DK]
        last = dve.scalar_tensor_tensor(out=yj, in0=hn[0:n, j, 0:DK], scalar=fac[0:n, j:j + 1], in1=yj, op0=ALU.mult, op1=ALU.mult)
    ch.link(last)


def mix_prompt(c, rows, cols, spread):
    nc, g = c.nc, c.x
    VX = DK + 1
    with Stage(nc, "mp") as st:
        qk = st.sb("qk", [P, 2 * QK // P, P])
        vx = st.sb("vx", [P, 2 * H, VX])
        y = st.sb("y", [P, 2 * D])
        state = st.sb("state", [P, 2 * H, 2, VX])
        hn = st.sb("hn", [P, 2 * H, VX])
        kw = st.sb("kw", [P, 2 * H, DK])
        wt = st.sb("wt", [P, 2, H, P])
        decay = st.sb("decay", [P, H, P])
        gin = st.sb("gin", [P, H, P])
        kout = st.sb("kout", [P, H])
        mask = st.sb("mask", [P, P])
        select = st.sb("select", [H, H, P])
        w_out = st.sb("w_out", [P, 2 * D // P, D])
        ssq = st.sb("ssq", [P, 2 * H])
        inv = st.sb("inv", [P, 2 * H])
        fac = st.sb("fac", [P, 2 * H])
        fac2 = st.sb("fac2", [P, 2 * H])
        junk = st.sb("junk2", [P, 2, DK])
        banks = [st.ps(f"bank{i}", [P, 512]) for i in range(8)]
        bA, bB, bKN, bNUM, bCU = banks[0], banks[1], banks[2:4], banks[4:6], banks[6:8]
        tail = Tail(c, st, 2 * D, y, w_out, banks, hn[:].rearrange("p j v -> p (j v)")[:, 0:D].rearrange("p (f n) -> p f n", f=2), 0)
        s_const, qk_loaded, v_loaded, g_loaded = (st.sem(n) for n in ("const", "qk_loaded", "v_loaded", "g_loaded"))
        rows_spread, masked, st_ready, wt_ready, q_scaled = (st.sem(n) for n in ("rows_spread", "masked", "st_ready", "wt_ready", "q_scaled"))
        weighed, kn_ready, kw_ready, num_ready, num_taken = (st.sem(n) for n in ("weighed", "kn_ready", "kw_ready", "num_ready", "num_taken"))
        cu_ready, updated, sums_ready, fac_rooted, y_ready = (st.sem(n) for n in ("cu_ready", "updated", "sums_ready", "fac_rooted", "y_ready"))
        chunk_done, dve_chain, pool_chain, s_end, s_start = (st.sem(n) for n in ("chunk_done", "dve_chain", "pool_chain", "end", "start"))
        HH = 2 * H

        def q_tile(j, d):
            return (j // H) * (QK // P) + (j % H) * 2 + d

        def k_tile(j, d):
            return q_tile(j, d) + D // P

        with nc.Block() as block:

            @block.sync
            def _(sp):
                sp.dma_start(mask[:], c.tab["mask_st"]).then_inc(s_const, 16)
                sp.dma_start(decay[:].rearrange("p h t -> p (h t)"), c.tab["decay"]).then_inc(s_const, 16)
                sp.dma_start(gin[:].rearrange("p h t -> p (h t)"), c.tab["gin"]).then_inc(s_const, 16)
                sp.dma_start(kout[:], c.tab["kout"]).then_inc(s_const, 16)
                sp.dma_start(select[:].rearrange("p h t -> p (h t)"), c.tab["select"]).then_inc(s_const, 16)
                tail.load_constants(sp)

                def loads(n):
                    at = bass.ds(n * P, P)
                    sp.dma_start(qk[:], c.s_qk[:, :, at].rearrange("n p t -> p n t")).then_inc(qk_loaded, 16)
                    sp.dma_start(vx[:, :, 0:DK], c.s_v[at, :].rearrange("t (h n) -> t h n", h=HH)).then_inc(v_loaded, 16)

                def late_loads(n):
                    at = bass.ds(n * P, P)
                    sp.dma_start(y[:], c.s_g[at, :]).then_inc(g_loaded, 16)
                    sp.dma_start(tail.res[:], g["x_prompt"][0, at, :]).then_inc(tail.res_loaded, 16)

                loads(0)
                late_loads(0)
                sp.dma_start(w_out[:], g["w_out_a"][0].rearrange("(k p) n -> p k n", p=P)).then_inc(tail.w_loaded, 16)
                with sp.Fori(1, NB) as n:
                    wait_counted(sp, chunk_done, n)
                    loads(n)
                    wait_counted(sp, tail.rows_turned, n)
                    late_loads(n)
                sp.wait_ge(updated, HH * NB + HH)
                for q, out in ((0, "C_p"), (1, "S_p")):
                    for d in range(2):
                        sp.dma_start(c.out[out][0, 0, :, d * P:(d + 1) * P, :].rearrange("h p v -> p h v"),
                                     state[:, q * H:(q + 1) * H, d, 0:DK]).then_inc(s_end, 16)
                for d in range(2):
                    sp.dma_start(c.out["n_p"][0, 0, :, d * P:(d + 1) * P].rearrange("h p -> p h"),
                                 state[:, 0:H, d, DK:VX].rearrange("p h a -> p (h a)"), allow_slow_non_contiguous=True).then_inc(s_end, 16)
                sp.wait_ge(s_end, 96)
                sp.wait_ge(tail.x1_stored, 16 * NB + 16)

            @block.tensor
            def _(pe):
                pe.wait_ge(s_const, 80)
                tail.pe_start(pe)
                pe.wait_ge(s_start, 1)

                def chunk(n):
                    at = bass.ds(n * P, P)
                    for q, bank in ((0, bA), (1, bB)):
                        for h in range(H):
                            last = pe.matmul(bank[:, h * P:(h + 1) * P], select[:, h, :], rows[:, q, at], start=True, stop=True)
                    last.then_inc(rows_spread, 1)
                    pe.wait_ge(qk_loaded, n * 16 + 16)
                    turn_k(n, 0)
                    pe.wait_ge(masked, n + 1)
                    scores(n, 0)
                    num(n, 0)
                    update(n, 0)
                    scores(n, 1)
                    for j in range(1, HH):
                        if j == H:
                            pe.wait_ge(kw_ready, n * HH + H)
                            turn_k(n, 1)
                        num(n, j)
                        update(n, j)
                    tail.pe(pe, n, P, lambda: pe.wait_ge(y_ready, n + 1))

                def turn_k(n, q):
                    for j in range(q * H, (q + 1) * H):
                        for d in range(2):
                            last = pe.transpose(bKN[(j % H) // 2][:, (j % 2) * DK + d * P:(j % 2) * DK + (d + 1) * P],
                                                qk[:, k_tile(j, d), :], c.ident[:])
                    last.then_inc(kn_ready, 1)

                def scores(n, q):
                    for j in range(q * H, (q + 1) * H):
                        for d in range(2):
                            last = pe.matmul(bA[:, (j % H) * P:(j % H + 1) * P], qk[:, k_tile(j, d), :], qk[:, q_tile(j, d), :],
                                             start=d == 0, stop=d == 1)
                    last.then_inc(st_ready, 1)

                def num(n, j):
                    w = VX if j < H else DK
                    q = j // H
                    if j % H == 0:
                        pe.wait_ge(v_loaded, n * 16 + 16)
                        pe.wait_ge(weighed, n * 2 + (q + 1))
                        pe.wait_ge(q_scaled, n * 2 + (q + 1))
                    pe.wait_ge(num_taken, n * HH + (j + 1))
                    if j < 2:
                        pe.wait_ge(tail.out_taken, n + 1)
                    pe.wait_ge(updated, n * HH + (j + 1))
                    out = bNUM[j % 2][:, 0:w]
                    pe.matmul(out, wt[:, q, j % H, :], vx[:, j, 0:w], start=True, stop=False)
                    pe.matmul(out, qk[:, q_tile(j, 0), :], state[:, j, 0, 0:w], start=False, stop=False)
                    pe.matmul(out, qk[:, q_tile(j, 1), :], state[:, j, 1, 0:w], start=False, stop=True).then_inc(num_ready, 1)

                def update(n, j):
                    w = VX if j < H else DK
                    pe.wait_ge(kw_ready, n * HH + (j + 1))
                    pe.wait_ge(updated, n * HH + (j + HH))
                    if j == 0:
                        pe.wait_ge(tail.rows_taken, n + 1)
                    for d in range(2):
                        last = pe.matmul(bCU[d][:, 0:w], kw[:, j, d * P:(d + 1) * P], vx[:, j, 0:w], start=True, stop=True)
                    last.then_inc(cu_ready, 1)
                    if j == HH - 1:
                        pass

                with pe.Fori(0, NB) as n:
                    chunk(n)

            @block.scalar
            def _(act):
                def chunk(n):
                    act.wait_ge(masked, n + 1)
                    for h in range(H):
                        last = act.activation(wt[:, 0, h, :], wt[:, 0, h, :], ACT.Exp,
                                              bias=cols[:, bass.ds(n, 1), A, h:h + 1].rearrange("p a b -> p (a b)"))
                    last.then_inc(wt_ready, 1)
                    rows_k(n, 0)
                    for j in range(HH):
                        if j == H:
                            rows_k(n, 1)
                        w = VX if j < H else DK
                        act.wait_ge(num_ready, n * HH + (j + 1))
                        act.activation(hn[:, j, 0:w], bNUM[j % 2][:, 0:w], ACT.Copy)
                        act.wait_ge(num_taken, n * HH + (j + 1))
                        act.activation(junk[:, j % 2, :], bNUM[j % 2][:, 0:DK], ACT.Square, accum_out=ssq[:, j:j + 1]).then_inc(num_taken, 1)
                    tail.act(act, n, P, c.s_x1[bass.ds(n * P, P), :])

                def rows_k(n, q):
                    act.wait_ge(kn_ready, 2 * n + (q + 1))
                    for j in range(q * H, (q + 1) * H):
                        scale = cols[:, bass.ds(n, 1), WS, j:j + 1].rearrange("p a b -> p (a b)") if q == 0 else kout[:, j - H:j - H + 1]
                        act.activation(kw[:, j, :], bKN[(j % H) // 2][:, (j % 2) * DK:(j % 2 + 1) * DK], ACT.Copy, scale=scale).then_inc(kw_ready, 1)

                act.wait_ge(s_const, 80)
                with act.Fori(0, NB) as n:
                    chunk(n)

            @block.gpsimd
            def _(pool):
                tail.pool_start(pool)
                with pool.Fori(0, NB) as n:
                    wait_counted(pool, sums_ready, n + 1)
                    pool.tensor_tensor(fac2[:], fac[:], tail.half[:, 0:HH], ALU.pow).then_inc(fac_rooted, 1)
                    tail.pool(pool, n, P)

            @block.vector
            def _(dve):
                ch = Chain(dve, dve_chain)
                dve.memset(vx[:, :, DK:VX], 1.0)
                dve.memset(inv[:], 1.0)
                ch.link(dve.memset(state[:], 0.0))
                tail.dve_start(dve)
                dve.sem_inc(tail.x1_stored, 16)
                dve.sem_inc(num_taken, 2)
                dve.sem_inc(updated, HH)
                dve.sem_inc(s_start, 1)
                dve.wait_ge(s_const, 80)

                def chunk(n):
                    ch.clear()
                    dve.wait_ge(rows_spread, n + 1)
                    ch.link(dve.tensor_tensor(wt[:, 0], bA[:].rearrange("p (h t) -> p h t", t=P),
                                              mask[:].unsqueeze(1).broadcast_to([P, H, P]), ALU.add))
                    dve.sem_inc(masked, 1)
                    weigh(n, 0, bB[:].rearrange("p (h t) -> p h t", t=P))
                    updates(n, 0)
                    weigh(n, 1, gin[:])
                    for j in range(1, HH):
                        updates(n, j)
                    head_norms(n)
                    dve.sem_inc(chunk_done, 1)
                    tail.dve(dve, n, P, bass.ds(n * P, P))

                def weigh(n, q, q_weight):
                    dve.wait_ge(st_ready, 2 * n + (q + 1))
                    t0 = q_tile(q * H, 0)
                    qs = qk[:, t0:t0 + 2 * H, :].rearrange("p (h d) t -> p h d t", d=2)
                    if q == 0:
                        dve.wait_ge(wt_ready, n + 1)
                    ch.link(dve.tensor_tensor(wt[:, q], bA[:].rearrange("p (h t) -> p h t", t=P),
                                              wt[:, 0] if q == 0 else decay[:], ALU.mult))
                    dve.sem_inc(weighed, 1)
                    ch.link(dve.tensor_tensor(qs, qs, q_weight.unsqueeze(2).broadcast_to([P, H, 2, P]), ALU.mult))
                    dve.sem_inc(q_scaled, 1)

                def updates(n, j):
                    w = VX if j < H else DK
                    dve.wait_ge(cu_ready, n * HH + (j + 1))
                    for d in range(2):
                        s = state[:, j, d, 0:w]
                        scale = spread[:, SCALE, bass.ds(n, 1), j:j + 1].rearrange("p a b -> p (a b)") if j < H \
                            else float((1.0 - 2.0 ** (-5.0 - (j - H))) ** P)
                        last = dve.scalar_tensor_tensor(out=s, in0=s, scalar=scale, in1=bCU[d][:, 0:w], op0=ALU.mult, op1=ALU.add)
                    ch.link(last)
                    dve.sem_inc(updated, 1)

                def head_norms(n):
                    dve.wait_ge(num_taken, n * HH + (HH + 2))
                    apply_norms(dve, ch, P, hn, ssq, inv, fac, fac2, cols[:, bass.ds(n, 1), EM, :].rearrange("p a b -> p (a b)"),
                                sums_ready, lambda: dve.wait_ge(fac_rooted, n + 1), lambda: dve.wait_ge(g_loaded, n * 16 + 16), y)
                    dve.sem_inc(y_ready, 1)

                with dve.Fori(0, NB) as n:
                    chunk(n)


def mix_sample(c, rows, cols, spread):
    nc, g = c.nc, c.x
    VX = DK + 1
    HH = 2 * H
    STEP = S + DS
    with Stage(nc, "ms") as st:
        qk = st.sb("qk", [P, 2, 4, S])
        vh = st.sb("vh", [S, 2, VX])
        state = st.sb("state", [P, 2, DB, 2, VX])
        qz = st.sb("qz", [P, 2, 2, DB * STEP])
        kwz = st.sb("kwz", [S, 2, DB, DK])
        w = st.sb("w", [S, 2, S])
        wz = st.sb("wz", [S, 2, DB])
        wt = st.sb("wt", [S, HH, S])
        qw = st.sb("qw", [P, HH, S])
        ko = st.sb("ko", [S, HH])
        own = st.sb("own", [S, DB])
        mask = st.sb("mask", [S, S])
        select = st.sb("select", [H, H, P])
        scale = st.sb("scale", [P, HH, DB])
        y = st.sb("y", [S, 2 * D])
        hn = st.sb("hn", [S, HH, VX])
        w_out = st.sb("w_out", [P, 2 * D // P, D])
        ssq, inv, fac, fac2 = (st.sb(n, [S, HH]) for n in ("ssq", "inv", "fac", "fac2"))
        junk = st.sb("junk2", [S, 2, DK])
        banks = [st.ps(f"bank{i}", [P, 512]) for i in range(8)]
        bKN, bST, bNUM, bCU = banks[0:2], banks[2], banks[3], banks[4:8]
        tail = Tail(c, st, 2 * D, y, w_out, banks, hn[:].rearrange("p j v -> p (j v)")[:, 0:D].rearrange("p (f n) -> p f n", f=2), 0)
        loaded, stored = st.sems("loaded", 2), st.sems("stored", 2)
        s_const, s_m, rows_spread, masked, start = (st.sem(n) for n in ("const", "m", "rows_spread", "masked", "start"))
        kn_ready, st_ready, w_ready, qz_ready, kwz_ready = (st.sem(n) for n in ("kn_ready", "st_ready", "w_ready", "qz_ready", "kwz_ready"))
        num_ready, num_taken, cu_ready, updated = (st.sem(n) for n in ("num_ready", "num_taken", "cu_ready", "updated"))
        g_loaded, sums_ready, fac_rooted, y_ready, dve_chain = (st.sem(n) for n in ("g_loaded", "sums_ready", "fac_rooted", "y_ready", "dve_chain"))

        cu_taken = st.sem("cu_taken")

        def stores_before(j):
            return 16 + 16 * sum(4 if i < H else 2 for i in range(j % 2, j, 2))

        def loads_of(q, h, s):
            per = 16 * (7 if q == 0 else 5)
            return (h - s) * (per // 2) + (per + q * 16 * 7 * (H // 2))

        def heads(eng, body):
            for q in range(2):
                with eng.Fori(0, H // 2) as i:
                    for s in range(2):
                        body(q, i * 2 + s, i * 2 + (q * H + s), s)

        with nc.Block() as block:

            @block.sync
            def _(sp):
                sp.dma_start(mask[:], c.tab["mask_st_s"]).then_inc(s_const, 16)
                sp.dma_start(wt[:, H:, :].rearrange("p h t -> p (h t)"), c.tab["decay_s"]).then_inc(s_const, 16)
                sp.dma_start(qw[:, H:, :].rearrange("p h t -> p (h t)"), c.tab["gin_s"]).then_inc(s_const, 16)
                sp.dma_start(ko[:, H:], c.tab["kout_s"]).then_inc(s_const, 16)
                sp.dma_start(own[:], c.tab["batch_of"]).then_inc(s_const, 16)
                sp.dma_start(select[:].rearrange("p h t -> p (h t)"), c.tab["select"]).then_inc(s_const, 16)
                tail.load_constants(sp)

                def load(j):
                    q, h, s = j // H, j % H, j % 2
                    sp.wait_ge(stored[s], stores_before(j))
                    base = q * (QK // P)
                    for t in range(2):
                        at = base + t * (D // P) + 2 * h
                        sp.dma_start(qk[:, s, 2 * t:2 * t + 2, :], c.s_qk[at:at + 2, :, T:NT].rearrange("n p t -> p n t")).then_inc(loaded[s], 16)
                    sp.dma_start(vh[:, s, 0:DK], c.s_v[T:NT, j * DK:(j + 1) * DK]).then_inc(loaded[s], 16)
                    old = g["state_mlstm_C"] if q == 0 else g["state_ret_S"]
                    for d in range(2):
                        part = slice(d * P, (d + 1) * P)
                        sp.dma_start(state[:, s, :, d, 0:DK], old[0, :, h, part, :].rearrange("b p v -> p b v")).then_inc(loaded[s], 16)
                        if q == 0:
                            sp.dma_start(state[:, s, :, d, DK:VX], g["state_mlstm_n"][0, :, h, part].rearrange("b p -> p b").unsqueeze(2),
                                         allow_slow_non_contiguous=True).then_inc(loaded[s], 16)

                def store(j):
                    q, h, s = j // H, j % H, j % 2
                    sp.wait_ge(updated, (j + 1) * DB)
                    new = c.out["C_s"] if q == 0 else c.out["S_s"]
                    for d in range(2):
                        part = slice(d * P, (d + 1) * P)
                        sp.dma_start(new[0, :, h, part, :].rearrange("b p v -> p b v"), state[:, s, :, d, 0:DK]).then_inc(stored[s], 16)
                        if q == 0:
                            sp.dma_start(c.out["n_s"][0, :, h, part].rearrange("b p -> p b").unsqueeze(2),
                                         state[:, s, :, d, DK:VX], allow_slow_non_contiguous=True).then_inc(stored[s], 16)

                load(0)
                load(1)
                sp.dma_start(w_out[:], g["w_out_a"][0].rearrange("(k p) n -> p k n", p=P)).then_inc(tail.w_loaded, 16)
                sp.dma_start(y[:], c.s_g[T:NT, :]).then_inc(g_loaded, 16)
                sp.dma_start(tail.res[0:S, :], g["x_sample"].rearrange("b t d -> (b t) d")).then_inc(tail.res_loaded, 16)
                for j in range(HH):
                    store(j)
                    if j + 2 < HH:
                        load(j + 2)
                for s in range(2):
                    sp.wait_ge(stored[s], stores_before(HH + s))
                sp.wait_ge(tail.x1_stored, 32)

            @block.tensor
            def _(pe):
                pe.wait_ge(s_const, 96)
                tail.pe_start(pe)
                for q, bank in ((0, banks[0]), (1, banks[1])):
                    for h in range(H):
                        last = pe.matmul(bank[:, h * S:(h + 1) * S], select[:, h, :], rows[:, q, T:NT], start=True, stop=True)
                last.then_inc(rows_spread, 1)
                pe.wait_ge(start, 1)

                def body(q, h, j, s):
                    w_ = VX if q == 0 else DK
                    pe.wait_ge(loaded[s], loads_of(q, h, s))
                    pe.wait_ge(kwz_ready, j + 1)
                    for d in range(2):
                        last = pe.transpose(bKN[s][0:S, d * P:(d + 1) * P], qk[:, s, 2 + d, :], c.ident[:])
                    last.then_inc(kn_ready, 1)
                    pe.wait_ge(w_ready, j + 1)
                    for d in range(2):
                        last = pe.matmul(bST[0:S, 0:S], qk[:, s, 2 + d, :], qk[:, s, d, :], start=d == 0, stop=d == 1)
                    last.then_inc(st_ready, 1)
                    pe.wait_ge(w_ready, j + 2)
                    pe.wait_ge(qz_ready, j + 1)
                    wait_counted(pe, num_taken, j + 1)
                    out = bNUM[0:S, 0:w_]
                    pe.matmul(out, w[:, s, :], vh[:, s, 0:w_], start=True, stop=False)
                    for b in range(DB):
                        for d in range(2):
                            last = pe.matmul(out, qz[:, s, d, b * S:(b + 1) * S], state[:, s, b, d, 0:w_],
                                             start=False, stop=b == DB - 1 and d == 1)
                    last.then_inc(num_ready, 1)
                    pe.wait_ge(kwz_ready, j + 2)
                    for b in range(DB):
                        pe.wait_ge(cu_taken, j * DB + (b + 1))
                        for d in range(2):
                            last = pe.matmul(bCU[2 * (b % 2) + d][:, 0:w_], kwz[:, s, b, d * P:(d + 1) * P], vh[:, s, 0:w_], start=True, stop=True)
                        last.then_inc(cu_ready, 1)

                heads(pe, body)
                tail.pe(pe, 0, S, lambda: (pe.wait_ge(y_ready, 1), pe.wait_ge(cu_taken, HH * DB + 2)))

            @block.scalar
            def _(act):
                act.wait_ge(masked, 1)
                for h in range(H):
                    last = act.activation(wt[:, h, :], wt[:, h, :], ACT.Exp, bias=cols[0:S, NB, A, h:h + 1])
                last.then_inc(s_m, 1)

                def body(q, h, j, s):
                    w_ = VX if q == 0 else DK
                    act.wait_ge(num_ready, j + 1)
                    act.activation(hn[:, bass.ds(j, 1), 0:w_], bNUM[0:S, 0:w_].unsqueeze(1), ACT.Copy)
                    act.wait_ge(num_taken, j + 1)
                    act.activation(junk[:, s, :], bNUM[0:S, 0:DK], ACT.Square, accum_out=ssq[:, bass.ds(j, 1)]).then_inc(num_taken, 1)

                heads(act, body)
                tail.act(act, 0, S, c.s_x1[T:NT, :])

            @block.gpsimd
            def _(pool):
                tail.pool_start(pool)
                pool.wait_ge(sums_ready, 1)
                pool.tensor_tensor(fac2[:], fac[:], tail.half[0:S, 0:HH], ALU.pow).then_inc(fac_rooted, 1)
                tail.pool(pool, 0, S)

            @block.vector
            def _(dve):
                ch = Chain(dve, dve_chain)
                ch.link(dve.memset(vh[:, :, DK:VX], 1.0))
                dve.memset(inv[:], 1.0)
                ch.link(dve.memset(qz[:], 0.0))
                for s in range(2):
                    dve.sem_inc(stored[s], 16)
                tail.dve_start(dve)
                dve.sem_inc(tail.x1_stored, 16)
                dve.wait_ge(s_const, 96)
                dve.wait_ge(rows_spread, 1)
                ch.link(dve.tensor_tensor(wt[:, 0:H, :], banks[0][0:S, 0:H * S].rearrange("p (h t) -> p h t", t=S),
                                          mask[:].unsqueeze(1).broadcast_to([S, H, S]), ALU.add))
                dve.sem_inc(masked, 1)
                dve.tensor_copy(qw[:, 0:H, :], banks[1][:, 0:H * S].rearrange("p (h t) -> p h t", t=S))
                dve.tensor_copy(ko[:, 0:H], cols[0:S, NB, WS, :])
                dve.tensor_copy(scale[:, 0:H, :], spread[:, SCALE, NB:, :].rearrange("p b h -> p h b"))
                for h in range(H):
                    last = dve.memset(scale[:, H + h, :], float((1.0 - 2.0 ** (-5.0 - h)) ** DS))
                ch.link(last)
                dve.wait_ge(s_m, 1)
                dve.sem_inc(kwz_ready, 1)
                dve.sem_inc(w_ready, 1)
                dve.sem_inc(num_taken, 1)
                dve.sem_inc(cu_taken, 2)
                dve.sem_inc(start, 1)

                def body(q, h, j, s):
                    w_ = VX if q == 0 else DK
                    if s == 0:
                        ch.clear()
                    dve.wait_ge(kn_ready, j + 1)
                    one = bass.ds(j, 1)
                    ch.link(dve.tensor_scalar(wz[:, s, :], own[:], ko[:, one], None, ALU.mult))
                    ch.link(dve.tensor_tensor(kwz[:, s], bKN[s][0:S, 0:DK].unsqueeze(1).broadcast_to([S, DB, DK]),
                                              wz[:, s, :].unsqueeze(2).broadcast_to([S, DB, DK]), ALU.mult))
                    dve.sem_inc(kwz_ready, 1)
                    dve.wait_ge(st_ready, j + 1)
                    ch.link(dve.tensor_tensor(w[:, s, :].unsqueeze(1), bST[0:S, 0:S].unsqueeze(1), wt[:, one, :], ALU.mult))
                    dve.sem_inc(w_ready, 1)
                    for d in range(2):
                        last = dve.tensor_tensor(qz[:, s, d, :].rearrange("p (b t) -> p b t", t=STEP)[:, :, 0:DS],
                                                 qk[:, s, d, :].rearrange("p (b t) -> p b t", t=DS),
                                                 qw[:, one, :].rearrange("p a (b t) -> p (a b) t", t=DS), ALU.mult)
                    ch.link(last)
                    dve.sem_inc(qz_ready, 1)
                    for b in range(DB):
                        dve.wait_ge(cu_ready, j * DB + (b + 1))
                        for d in range(2):
                            x = state[:, s, b, d, 0:w_]
                            last = dve.scalar_tensor_tensor(out=x, in0=x, scalar=scale[:, one, b:b + 1].rearrange("p a b -> p (a b)"),
                                                            in1=bCU[2 * (b % 2) + d][:, 0:w_], op0=ALU.mult, op1=ALU.add)
                        ch.link(last)
                        dve.sem_inc(cu_taken, 1)
                        dve.sem_inc(updated, 1)

                heads(dve, body)
                dve.wait_ge(num_taken, HH + 1)
                apply_norms(dve, ch, S, hn, ssq, inv, fac, fac2, cols[0:S, NB, EM, :], sums_ready,
                            lambda: dve.wait_ge(fac_rooted, 1), lambda: dve.wait_ge(g_loaded, 16), y)
                dve.sem_inc(y_ready, 1)
                tail.dve(dve, 0, S, slice(T, NT))


def attend_prompt(c, q_s, k_s, v_s, g_s, lam):
    nc, g = c.nc, c.x
    W4 = 4 * 2 * HD
    NBK = NB + 1
    w = g["w_in_c"][0].rearrange("(k p) (q n) -> p k q n", p=P, q=4)
    USES = NB + 3
    with Stage(nc, "ap") as st:
        wh = st.sb("wh", [P, 2, KD, W4])
        raw = st.sb("raw", [P, 2, NBK, W4])
        ez = st.sb("ez", [P, NBK, P])
        gnb = st.sb("gnb", [P, 2, P])
        rot = st.sb("rot", [P, 2, NBK, ROT])
        tmp = st.sb("tmp", [P, 4, 4, 4, ROT])
        qT = st.sb("qT", [P, 2, T])
        kT = st.sb("kT", [P, 2, T])
        pr = st.sb("pr", [P, 2, 2, T])
        aT = st.sb("aT", [P, NB, P])
        o = st.sb("o", [P, 2, NB, P])
        ms = st.sb("ms", [P, 2, NB])
        rstd = st.sb("rstd", [P, NB])
        half = st.sb("half", [P, NB])
        junk = st.sb("junk", [P, 2, P])
        mask = st.sb("mask", [P, P])
        mx = st.sb("mx", [P, 2, 2])
        den = st.sb("den", [P, 2, 2])
        lq = st.sb("lq", [P, 4, HD])
        lsum = st.sb("lsum", [P, 2])
        sc = st.ps("sc", [P, 2, T])
        gm = st.ps("gm", [P, 512])
        at = st.ps("at", [P, 2, 512])
        ob = st.ps("ob", [P, 512])
        s_const, s_lam, w_loaded, g_loaded = st.sem("const"), st.sem("lam"), st.sems("w_loaded", 2), st.sems("g_loaded", 2)
        kv_stored, y_stored = st.sems("kv_stored", 2), st.sems("y_stored", 2)
        gm_ready, raw_ready, roped, gated = (st.sem(n) for n in ("gm_ready", "raw_ready", "roped", "gated"))
        at_turned, at_taken = st.sem("at_turned"), st.sem("at_taken")
        sc_ready, max_ready, sc_taken, a_ready, o_ready, o_taken = (
            st.sem(n) for n in ("sc_ready", "max_ready", "sc_taken", "a_ready", "o_ready", "o_taken"))
        sq_ready, rooted, y_ready, dve_chain, pool_chain, start = (
            st.sem(n) for n in ("sq_ready", "rooted", "y_ready", "dve_chain", "pool_chain", "start"))

        def heads(eng, step):
            with eng.Fori(0, HC // 2 - 1) as i:
                for s in range(2):
                    step(2 * i + s, s, True)
            step(HC - 2, 0, True)
            step(HC - 1, 1, False)

        def use(hd, k, more=True):
            return hd * USES + (k + 1)

        def weights_use(j, more):
            return j if j < 3 else j + 2 if j < 6 or not more else j + 3

        Q1, Q2, Q0 = 3, 4, 8

        with nc.Block() as block:

            @block.sync
            def _(sp):
                def load_w(hd, s):
                    for q in range(4):
                        sp.dma_start(wh[:, s, :, q * P:(q + 1) * P], w[:, :, q, bass.ds(hd * P, P)]).then_inc(w_loaded[s], 16)
                    sp.dma_start(gnb[:, s, :], g["gn_diff"][0, bass.ds(hd, 1), :].broadcast_to([P, P])).then_inc(g_loaded[s], 16)

                load_w(0, 0)
                load_w(1, 1)
                sp.dma_start(rot[:].rearrange("p q b r -> p (q b r)"), c.tab["rot1"]).then_inc(s_const, 16)
                sp.dma_start(mask[:], c.tab["mask_qk"]).then_inc(s_const, 16)
                sp.dma_start(lq[:].rearrange("p a b -> p (a b)"),
                             g["lambda_qk"].rearrange("a b c -> a (b c)").broadcast_to([P, 4 * HD])).then_inc(s_const, 16)

                def step(hd, s, more):
                    wait_counted(sp, roped, hd * 3 + 3)
                    at_h = bass.ds(hd * P, P)
                    for name, q in (("k", 1), ("v", 2)):
                        flat = "a b t h d -> (a b t) (h d)"
                        cols = slice(q * P, (q + 1) * P)
                        sp.dma_start(c.out[name + "_p"].rearrange(flat)[:, at_h].rearrange("(n p) d -> p n d", p=P),
                                     raw[:, s, 0:NB, cols]).then_inc(kv_stored[s], 16)
                        sp.dma_start(c.out[name + "_s"].rearrange(flat)[:, at_h], raw[0:S, s, NB, cols]).then_inc(kv_stored[s], 16)
                    if more is True and not isinstance(hd, int):
                        wait_counted(sp, gm_ready, hd * NBK + NBK)
                        wait_counted(sp, gated, hd + 2)
                        load_w(hd + 2, s)
                    wait_counted(sp, y_ready, hd + 3)
                    sp.dma_start(c.s_y1[0:T, at_h].rearrange("(n p) d -> p n d", p=P), o[:, s]).then_inc(y_stored[s], 16)

                heads(sp, step)
                for s in range(2):
                    sp.wait_ge(kv_stored[s], 16 + 16 * 4 * (HC // 2))
                    sp.wait_ge(y_stored[s], 16 + 16 * (HC // 2))

            @block.tensor
            def _(pe):
                def project(hd, s, b):
                    if b == 0:
                        pe.wait_ge(w_loaded[s], (hd - s) * 32 + 64)
                    if not (isinstance(hd, int) and hd == 0 and b == 0):
                        pe.wait_ge(raw_ready, hd * NBK + b)
                    n = rows_of(b)
                    for k in range(KD):
                        last = pe.matmul(gm[0:n, :], c.hT[:, k, b * P:b * P + n], wh[:, s, k, :], start=k == 0, stop=k == KD - 1)
                    last.then_inc(gm_ready, 1)

                def turn_qk(hd, s, part, count):
                    pe.wait_ge(roped, hd * 3 + (part + 1))
                    wait_counted(pe, at_taken, count + 1)
                    for q in range(2):
                        if part == 2:
                            last = pe.transpose(at[:, 0, q * S:(q + 1) * S], raw[0:S, s, NB, q * P:(q + 1) * P], c.ident[0:S, 0:S])
                        else:
                            for b in range(4):
                                last = pe.transpose(at[:, q, b * P:(b + 1) * P], raw[:, s, 4 * part + b, q * P:(q + 1) * P], c.ident[:])
                    last.then_inc(at_turned, 1)

                def scores(hd, s, j):
                    wait_counted(pe, sc_taken, hd * NB + (j + 1))
                    n = (j + 1) * P
                    for m in range(2):
                        half_rows = slice(m * HD, (m + 1) * HD)
                        for k0 in range(0, n, 512):
                            kn = min(512, n - k0)
                            last = pe.matmul(sc[:, m, k0:k0 + kn], qT[half_rows, s, j * P:(j + 1) * P], kT[half_rows, s, k0:k0 + kn],
                                             start=True, stop=True)
                    last.then_inc(sc_ready, 1)

                def turn_weights(hd, s, j, more):
                    pe.wait_ge(a_ready, hd * NB + (j + 1))
                    pe.wait_ge(at_taken, use(hd, weights_use(j, more)) + 1)
                    for k in range(j + 1):
                        last = pe.transpose(at[:, k // 4, (k % 4) * P:(k % 4 + 1) * P], pr[:, j % 2, 0, k * P:(k + 1) * P], c.ident[:])
                    last.then_inc(at_turned, 1)

                def values(hd, s, j, more):
                    pe.wait_ge(at_taken, use(hd, weights_use(j, more)) + 2)
                    pe.wait_ge(o_taken, hd * NB + (j + 1))
                    for k in range(j + 1):
                        last = pe.matmul(ob[:, 0:P], aT[:, k, :], raw[:, s, k, 2 * P:3 * P], start=k == 0, stop=k == j)
                    last.then_inc(o_ready, 1)

                pe.wait_ge(start, 1)
                for b in range(NBK):
                    project(0, 0, b)
                turn_qk(0, 0, 0, 0)
                pe.wait_ge(at_taken, 2)
                scores(0, 0, 0)

                def step(hd, s, more):
                    for j in range(NB):
                        if more:
                            project(hd + 1, 1 - s, j)
                        turn_weights(hd, s, j, more)
                        if j < NB - 1:
                            scores(hd, s, j + 1)
                        elif more:
                            scores(hd + 1, 1 - s, 0)
                        values(hd, s, j, more)
                        if j == 2:
                            turn_qk(hd, s, 1, use(hd, Q1))
                            turn_qk(hd, s, 2, use(hd, Q2))
                        if j == 5 and more:
                            turn_qk(hd + 1, 1 - s, 0, use(hd, Q0))
                    if more:
                        project(hd + 1, 1 - s, NB)

                heads(pe, step)

            @block.scalar
            def _(act):
                act.wait_ge(start, 1)
                act.activation(lsum[:], lsum[:], ACT.Exp).then_inc(s_lam, 1)

                def take_rows(hd, s, b):
                    n = rows_of(b)
                    if b == 0:
                        act.wait_ge(y_ready, hd + 1)
                        act.wait_ge(kv_stored[s], (hd - s) * 32 + 16)
                        act.wait_ge(gated, hd + 1)
                    act.wait_ge(gm_ready, hd * NBK + (b + 1))
                    act.activation(ez[0:n, b, :], gm[0:n, 3 * P:], ACT.Exp, scale=-1.0)
                    act.activation(raw[0:n, s, b, :], gm[0:n, :], ACT.Copy).then_inc(raw_ready, 1)

                def take_qk(hd, s, part, count):
                    act.wait_ge(at_turned, count + 1)
                    if part == 2:
                        one = bass.ds(hd, 1)
                        act.activation(q_s[:, one, :], at[:, 0, 0:S].unsqueeze(1), ACT.Copy)
                        act.activation(k_s[:, one, :], at[:, 0, S:2 * S].unsqueeze(1), ACT.Copy).then_inc(at_taken, 1)
                    else:
                        act.activation(qT[:, s, part * 512:(part + 1) * 512], at[:, 0, :], ACT.Copy)
                        act.activation(kT[:, s, part * 512:(part + 1) * 512], at[:, 1, :], ACT.Copy).then_inc(at_taken, 1)

                def exps(hd, s, j):
                    n = (j + 1) * P
                    act.wait_ge(max_ready, hd * NB + (j + 1))
                    for m in range(2):
                        last = act.activation(pr[:, j % 2, m, 0:n], sc[:, m, 0:n], ACT.Exp, bias=mx[:, j % 2, m:m + 1], scale=HD ** -0.5,
                                              accum_out=den[:, j % 2, m:m + 1])
                    last.then_inc(sc_taken, 1)

                def take_weights(hd, s, j, more):
                    act.wait_ge(at_turned, use(hd, weights_use(j, more)) + 1)
                    last = act.activation(aT[:, 0:min(4, j + 1), :], at[:, 0, 0:min(4, j + 1) * P].rearrange("p (k t) -> p k t", t=P), ACT.Copy)
                    if j >= 4:
                        last = act.activation(aT[:, 4:j + 1, :], at[:, 1, 0:(j - 3) * P].rearrange("p (k t) -> p k t", t=P), ACT.Copy)
                    last.then_inc(at_taken, 1)

                def take_out(hd, s, j):
                    act.wait_ge(o_ready, hd * NB + (j + 1))
                    if j == 0:
                        act.wait_ge(y_stored[s], (hd - s) * 8 + 16)
                    act.activation(o[:, s, j, :], ob[:, 0:P], ACT.Copy)
                    act.wait_ge(o_taken, hd * NB + (j + 1))
                    act.activation(junk[:, j % 2, :], ob[:, 0:P], ACT.Square, accum_out=ms[:, s, j:j + 1]).then_inc(o_taken, 1)

                for b in range(NBK):
                    take_rows(0, 0, b)
                take_qk(0, 0, 0, 0)

                def step(hd, s, more):
                    for j in range(NB):
                        exps(hd, s, j)
                        if more:
                            take_rows(hd + 1, 1 - s, j)
                        take_weights(hd, s, j, more)
                        take_out(hd, s, j)
                        if j == 2:
                            take_qk(hd, s, 1, use(hd, Q1))
                            take_qk(hd, s, 2, use(hd, Q2))
                        if j == 5 and more:
                            take_qk(hd + 1, 1 - s, 0, use(hd, Q0))
                    if more:
                        take_rows(hd + 1, 1 - s, NB)

                heads(act, step)

            @block.gpsimd
            def _(pool):
                pool.memset(half[:], -0.5).then_inc(pool_chain, 1)
                pool.wait_ge(pool_chain, 1)

                def step(hd, s, more):
                    wait_counted(pool, sq_ready, hd + 1)
                    pool.tensor_tensor(rstd[:], ms[:, s, :], half[:], ALU.pow).then_inc(rooted, 1)

                heads(pool, step)

            @block.vector
            def _(dve):
                ch = Chain(dve, dve_chain)
                dve.wait_ge(s_const, 48)
                pair = lq[:].rearrange("p (a b) d -> p a b d", b=2)
                ch.link(dve.tensor_tensor(pair[:, :, 0, :], pair[:, :, 0, :], pair[:, :, 1, :], ALU.mult))
                ch.link(dve.tensor_reduce(lsum[:], pair[:, :, 0, :], AX_X, ALU.add))
                for q in (at_taken, sc_taken, o_taken, gated):
                    dve.sem_inc(q, 1)
                dve.sem_inc(y_ready, 2)
                for s in range(2):
                    dve.sem_inc(kv_stored[s], 16)
                    dve.sem_inc(y_stored[s], 16)
                dve.sem_inc(start, 1)
                dve.wait_ge(s_lam, 1)
                ch.link(dve.tensor_tensor(lam[:], lsum[:, 0:1], lsum[:, 1:2], ALU.subtract))
                ch.link(dve.tensor_scalar(lam[:], lam[:], LAM_INIT, None, ALU.add))

                def rotate(hd, s, part):
                    b0, nb, n = (4 * part, 4, P) if part < 2 else (NB, 1, S)
                    dve.wait_ge(raw_ready, hd * NBK + (b0 + nb))
                    for b in range(b0, b0 + nb, 4):
                        x = raw[0:n, s, b0:b0 + nb, 0:2 * P].rearrange("p b (m d) -> p b m d", d=HD)
                        x1, x2 = x[:, :, :, 0:ROT], x[:, :, :, ROT:2 * ROT]
                        cos, sin = (rot[0:n, i, b0:b0 + nb, :].unsqueeze(2).broadcast_to([n, nb, 4, ROT]) for i in range(2))
                        t = [tmp[0:n, i, 0:nb] for i in range(4)]
                        for o_, x_, f_ in ((t[0], x1, cos), (t[1], x2, sin), (t[2], x1, sin), (t[3], x2, cos)):
                            last = dve.tensor_tensor(o_, x_, f_, ALU.mult)
                        ch.link(last)
                        dve.tensor_tensor(x1, t[0], t[1], ALU.subtract)
                        ch.link(dve.tensor_tensor(x2, t[2], t[3], ALU.add))
                    dve.sem_inc(roped, 1)

                def gates(hd, s):
                    dve.wait_ge(g_loaded[s], (hd - s) * 8 + 16)
                    dve.wait_ge(raw_ready, hd * NBK + NBK)
                    for b0, nb, n in ((0, NB, P), (NB, 1, S)):
                        e, z = ez[0:n, b0:b0 + nb, :], raw[0:n, s, b0:b0 + nb, 3 * P:]
                        ch.link(dve.tensor_scalar(e, e, 1.0, None, ALU.add))
                        ch.link(dve.reciprocal(e, e))
                        ch.link(dve.tensor_tensor(z, z, e, ALU.mult))
                        ch.link(dve.scalar_tensor_tensor(out=z, in0=z, scalar=1.0 - LAM_INIT,
                                                         in1=gnb[0:n, s, :].unsqueeze(1).broadcast_to([n, nb, P]), op0=ALU.mult, op1=ALU.mult))
                    one = bass.ds(hd, 1)
                    dve.tensor_copy(g_s[:, one, :], raw[0:S, s, NB:NBK, 3 * P:])
                    ch.link(dve.tensor_copy(v_s[:, one, :], raw[0:S, s, NB:NBK, 2 * P:3 * P]))
                    dve.sem_inc(gated, 1)

                def maxima(hd, s, j):
                    n, i = (j + 1) * P, j % 2
                    dve.wait_ge(sc_ready, hd * NB + (j + 1))
                    diagonal = sc[:, :, j * P:n]
                    ch.link(dve.tensor_tensor(diagonal, diagonal, mask[:].unsqueeze(1).broadcast_to([P, 2, P]), ALU.add))
                    ch.link(dve.tensor_reduce(mx[:, i, :], sc[:, :, 0:n], AX_X, ALU.max))
                    ch.link(dve.tensor_scalar(mx[:, i, :], mx[:, i, :], -HD ** -0.5, None, ALU.mult))
                    dve.sem_inc(max_ready, 1)

                def difference(hd, s, j):
                    n, i = (j + 1) * P, j % 2
                    dve.wait_ge(sc_taken, hd * NB + (j + 2))
                    ch.link(dve.reciprocal(den[:, i, :], den[:, i, :]))
                    ch.link(dve.tensor_scalar(pr[:, i, 1, 0:n], pr[:, i, 1, 0:n], den[:, i, 1:2], lam[:, 0:1], ALU.mult, ALU.mult))
                    ch.link(dve.scalar_tensor_tensor(out=pr[:, i, 0, 0:n], in0=pr[:, i, 0, 0:n], scalar=den[:, i, 0:1],
                                                     in1=pr[:, i, 1, 0:n], op0=ALU.mult, op1=ALU.subtract))
                    dve.sem_inc(a_ready, 1)

                def finish(hd, s):
                    dve.wait_ge(o_taken, hd * NB + (NB + 1))
                    ch.link(dve.tensor_scalar(ms[:, s, :], ms[:, s, :], 1.0 / P, EPS, ALU.mult, ALU.add))
                    dve.sem_inc(sq_ready, 1)
                    dve.wait_ge(rooted, hd + 1)
                    ch.link(dve.tensor_tensor(o[:, s], o[:, s], rstd[:].unsqueeze(2).broadcast_to([P, NB, P]), ALU.mult))
                    ch.link(dve.tensor_tensor(o[:, s], o[:, s], raw[:, s, 0:NB, 3 * P:], ALU.mult))
                    dve.sem_inc(y_ready, 1)

                rotate(0, 0, 0)

                def step(hd, s, more, first=False):
                    if not first:
                        ch.clear()
                    for j in range(NB):
                        maxima(hd, s, j)
                        difference(hd, s, j)
                        if j == 0:
                            rotate(hd, s, 1)
                            rotate(hd, s, 2)
                            gates(hd, s)
                        if j == 4 and more:
                            rotate(hd + 1, 1 - s, 0)
                    finish(hd, s)

                heads(dve, step)


def attend_sample(c, q_s, k_s, v_s, g_s, lam):
    nc, g = c.nc, c.x
    R = 2 * S
    G = 2
    NG = NPG // G
    GK = G * PAGE
    DEEP = 4
    with Stage(nc, "as") as st:
        pt = st.sb("pt", [1, DB * NPG], I32)
        kp = st.sb("kp", [P, DEEP * G, D])
        vp = st.sb("vp", [P, DEEP * G, D])
        v_hl = st.sb("v_hl", [P, 2, 2 * G, D], F32R)
        kT = st.sb("kT", [P, 2, 2, HC, GK], F32R)
        s = c.hT[:].rearrange("p k t -> p (k t)")[0:R, 0:2 * (PAST + S)].rearrange("r (a n) -> r a n", a=2)
        qz = st.sb("qz", [P, 2, HC * (2 * S + DS) + S])
        q_hl = st.sb("q_hl", [P, 2, HC, 2, R], F32R)
        aT = st.sb("aT", [P, 2, G, 2, R], F32R)
        aN = st.sb("aN", [S, 2, R], F32R)
        vs_hi, vs_lo = st.sb("vs_hi", [S, D], F32R), st.sb("vs_lo", [S, D], F32R)
        low_rows = st.sb("low_rows", [R, GK])
        mx = st.sb("mx", [R, 2, NG + 1])
        top = st.sb("top", [R, 2])
        den = st.sb("den", [R, 2])
        fac = st.sb("fac", [2 * R, 2])
        sign = st.sb("sign", [R, 1])
        new_mask = st.sb("new_mask", [R, DB, S])
        own = st.sb("own", [2 * R, HC])
        toq = st.sb("toq", [2 * R, DS])
        om = st.sb("om", [2 * R, D])
        oq = st.sb("oq", [DS, D])
        a, sq = vp[0:S, 0, :], vp[0:S, 1, :]
        ms = st.sb("ms", [S, 2, HC])
        half = st.sb("half", [S, HC])
        tp = [st.ps(f"tp{i}", [P, 512]) for i in range(2 * G)]
        sc = st.ps("sc", [P, 512])
        ap_ = st.ps("ap", [P, 512])
        ov = st.ps("ov", [P, 2, 512])
        s_pt, s_const = st.sem("pt"), st.sem("const")
        k_loaded, v_loaded = st.sems("k_loaded", DEEP * G), st.sems("v_loaded", DEEP * G)
        k_turned, k_hi, k_lo, sc_ready, sc_low, sc_taken = (st.sem(n) for n in ("k_turned", "k_hi", "k_lo", "sc_ready", "sc_low", "sc_taken"))
        q_ready, q_copied, q_high, top_ready, exp_ready = (st.sem(n) for n in ("q_ready", "q_copied", "q_high", "top_ready", "exp_ready"))
        a_turned, a_hi, a_taken, v_used = (st.sem(n) for n in ("a_turned", "a_hi", "a_taken", "v_used"))
        v_high, v_split = st.sems("v_high", G), st.sems("v_split", G)
        o_ready, o_picked, vs_high = st.sem("o_ready"), st.sem("o_picked"), st.sem("vs_high")
        oq_ready, oq_taken, oq_stored, s_a, s_y, start = (st.sem(n) for n in ("oq_ready", "oq_taken", "oq_stored", "a", "y", "start"))
        dve_chain, rooted, squares_ready = st.sem("dve_chain"), st.sem("rooted"), st.sem("squares_ready")
        STEP = 2 * S + DS
        C = NG + 1

        def interleave(k_start, k_group, k_end, v_group, v_end, v_pick):
            def keys(b, s_):
                k_start(b, s_)
                for i in range(NG):
                    k_group(b, s_, i)
                k_end(b, s_)

            def both(b, s_):
                k_start(b + 1, 1 - s_)
                for i in range(NG):
                    k_group(b + 1, 1 - s_, i)
                    v_group(b, s_, i)
                v_end(b, s_)
                k_end(b + 1, 1 - s_)
                v_pick(b, s_)

            def values(b, s_):
                for i in range(NG):
                    v_group(b, s_, i)
                v_end(b, s_)
                v_pick(b, s_)

            return keys, both, values

        def sequences(eng, keys, both, values):
            keys(0, 0)
            with eng.Fori(0, DB // 2 - 1) as i:
                for s_ in range(2):
                    both(2 * i + s_, s_)
            both(DB - 2, 0)
            values(DB - 1, 1)

        def values_low(eng, i, n):
            hi, lo = (v_hl[:, part, (i % 2) * G + n, :] for part in range(2))
            eng.tensor_tensor(lo, vp[:, (i % DEEP) * G + n, :], hi.bitcast(F32), ALU.subtract).then_inc(v_split[n], 1)

        def nothing(*_):
            pass

        def loads(b, i):
            return b * (16 * NG // DEEP) + 16 * (i // DEEP + 1)

        with nc.Block() as block:

            @block.sync
            def _(sp):
                sp.dma_start(pt[:], g["page_table"].rearrange("(a b) n -> a (b n)", a=1)).then_inc(s_pt, 16)
                sp.dma_start(new_mask[:].rearrange("r b k -> r (b k)"), c.tab["new_mask"]).then_inc(s_const, 16)
                sp.dma_start(own[:], c.tab["own_head"]).then_inc(s_const, 16)
                sp.dma_start(toq[:], c.tab["to_query"]).then_inc(s_const, 16)
                sp.wait_ge(s_pt, 16)

                def pages(cache, ring, loaded, b, i):
                    for n in range(G):
                        at = pt[0:1, bass.ds(b * NPG + (i * G + n), 1)]
                        page = sp.value_load(at, min_val=0, max_val=N_POOL - 1)
                        slot = (i % DEEP) * G + n
                        sp.dma_start(ring[:, slot, :], cache[0, bass.ds(page, 1)].rearrange("a k h d -> (a k) (h d)")).then_inc(loaded[slot], 16)

                def k_group(b, s_, i):
                    wait_counted(sp, k_turned, b * (2 * G * NG) + 2 * G * (i + 1))
                    pages(g["cache_k"], kp, k_loaded, b, i)

                def v_group(b, s_, i):
                    for q in v_split:
                        wait_counted(sp, q, b * NG + (i + 1))
                    pages(g["cache_v"], vp, v_loaded, b, i)

                sequences(sp, *interleave(nothing, k_group, nothing, v_group, nothing, nothing))
                sp.wait_ge(oq_stored, 16 + 16 * DB)
                sp.dma_start(a, c.s_a1[:]).then_inc(s_a, 16)
                sp.wait_ge(s_y, 1)
                sp.dma_start(c.s_y1[T:NT, :], a).then_inc(s_a, 16)
                sp.wait_ge(s_a, 32)

            @block.tensor
            def _(pe):
                def k_group(b, s_, i):
                    for n in range(G):
                        slot = (i % DEEP) * G + n
                        wait_counted(pe, k_loaded[slot], loads(b, i))
                        for f in range(2):
                            wait_counted(pe, k_lo, b * (2 * G * NG) + (2 * G * i + 2 * n + f + 1))
                            for h in range(HC // 2):
                                last = pe.transpose(tp[2 * n + f][:, h * P:(h + 1) * P],
                                                    kp[:, slot, (4 * f + h) * P:(4 * f + h + 1) * P], c.ident[:])
                            last.then_inc(k_turned, 1)
                    if i > 0:
                        scores(b, s_, i - 1)

                def scores(b, s_, i):
                    if i == 0:
                        pe.wait_ge(q_ready, b + 1)
                    pe.wait_ge(k_lo, b * (2 * G * NG) + 2 * G * (i + 2))
                    pe.wait_ge(sc_taken, b * C + (i + 1))
                    for h in range(HC):
                        for part in range(2):
                            last = pe.matmul(sc[:, 0:GK], q_hl[:, s_, h].rearrange("p l r -> p (l r)"), kT[:, i % 2, part, h, :],
                                             start=h == 0 and part == 0, stop=h == HC - 1 and part == 1)
                    last.then_inc(sc_ready, 1)

                def k_end(b, s_):
                    scores(b, s_, NG - 1)
                    wait_counted(pe, sc_taken, b * C + C)
                    for h in range(HC):
                        last = pe.matmul(sc[0:R, 0:S], qz[:, s_, h * R:(h + 1) * R], k_s[:, h, :], start=h == 0, stop=h == HC - 1)
                    last.then_inc(sc_ready, 1)

                def v_group(b, s_, i):
                    if i == 0:
                        pe.wait_ge(exp_ready, b + 1)
                    wait_counted(pe, a_taken, b * C + (i + 1))
                    for n in range(G):
                        k0 = (i * G + n) * PAGE
                        last = pe.transpose(ap_[:, n * R:(n + 1) * R], s[:, s_, k0:k0 + PAGE], c.ident[0:R, 0:R])
                    last.then_inc(a_turned, 1)
                    if i > 0:
                        weighted(b, i - 1)

                def weighted(b, i):
                    pe.wait_ge(a_taken, b * C + (i + 2))
                    for q in v_split:
                        pe.wait_ge(q, b * NG + (i + DEEP + 1))
                    if i == 0:
                        pe.wait_ge(oq_taken, b + 1)
                    for n in range(G):
                        w = aT[:, i % 2, n].rearrange("p l r -> p (l r)")
                        for part in range(2):
                            for f in range(2):
                                last = pe.matmul(ov[:, f, :], w, v_hl[:, part, (i % 2) * G + n, f * 512:(f + 1) * 512],
                                                 start=i == 0 and n == 0 and part == 0, stop=False)
                    last.then_inc(v_used, 1)

                def v_end(b, s_):
                    weighted(b, NG - 1)
                    wait_counted(pe, a_taken, b * C + C)
                    pe.transpose(ap_[0:S, 0:R], s[:, s_, PAST:], c.ident[0:R, 0:R]).then_inc(a_turned, 1)
                    wait_counted(pe, a_taken, b * C + (C + 1))
                    for part in (vs_hi, vs_lo):
                        for f in range(2):
                            last = pe.matmul(ov[:, f, :], aN[:].rearrange("p l r -> p (l r)"), part[:, f * 512:(f + 1) * 512],
                                             start=False, stop=part is vs_lo)
                    last.then_inc(o_ready, 1)

                def v_pick(b, s_):
                    wait_counted(pe, o_picked, b + 1)
                    for f in range(2):
                        last = pe.matmul(ov[0:DS, f, :], toq[:], om[:, f * 512:(f + 1) * 512], start=True, stop=True)
                    last.then_inc(oq_ready, 1)

                pe.wait_ge(start, 1)
                sequences(pe, *interleave(nothing, k_group, k_end, v_group, v_end, v_pick))

            @block.scalar
            def _(act):
                act.activation(vs_hi[:], v_s[:].rearrange("t h e -> t (h e)"), ACT.Copy).then_inc(vs_high, 1)
                act.wait_ge(start, 1)

                def k_start(b, s_):
                    act.wait_ge(q_copied, b + 1)
                    act.activation(q_hl[:, s_, :, 0, :], qz[:, s_, 0:HC * R].rearrange("p (h r) -> p h r", h=HC), ACT.Copy).then_inc(q_high, 1)

                def k_group(b, s_, i):
                    for j in range(2 * G):
                        act.wait_ge(k_turned, b * (2 * G * NG) + (2 * G * (i + DEEP) + j + 1))
                        act.activation(kT[:, i % 2, 0, 4 * (j % 2):4 * (j % 2) + 4, (j // 2) * PAGE:(j // 2 + 1) * PAGE],
                                       tp[j][:].rearrange("p (h k) -> p h k", h=4), ACT.Copy).then_inc(k_hi, 1)
                    if i > 0:
                        scores_low(b, i - 1)

                def scores_low(b, i):
                    act.wait_ge(sc_ready, b * C + (i + 1))
                    act.activation(low_rows[:], sc[R:2 * R, 0:GK], ACT.Copy).then_inc(sc_low, 1)

                def k_end(b, s_):
                    scores_low(b, NG - 1)
                    act.wait_ge(top_ready, b + 1)
                    act.activation(s[:, s_, :], s[:, s_, :], ACT.Exp, bias=top[:, s_:s_ + 1], scale=HD ** -0.5,
                                   accum_out=den[:, s_:s_ + 1]).then_inc(exp_ready, 1)

                def v_group(b, s_, i):
                    act.wait_ge(a_turned, b * C + (i + 1))
                    act.activation(aT[:, i % 2, :, 0, :], ap_[:, 0:G * R].rearrange("p (n r) -> p n r", n=G), ACT.Copy).then_inc(a_hi, 1)
                    wait_counted(act, v_used, b * NG + (i + 1))
                    for n in range(G):
                        slot = (i % DEEP) * G + n
                        act.wait_ge(v_loaded[slot], loads(b, i))
                        act.activation(v_hl[:, 0, (i % 2) * G + n, :], vp[:, slot, :], ACT.Copy).then_inc(v_high[n], 1)

                def v_end(b, s_):
                    act.wait_ge(a_turned, b * C + C)
                    act.activation(aN[:, 0, :], ap_[0:S, 0:R], ACT.Copy).then_inc(a_hi, 1)

                def v_pick(b, s_):
                    act.wait_ge(oq_ready, b + 1)
                    act.wait_ge(oq_stored, b * 16 + 16)
                    act.activation(oq[:], ov[0:DS].rearrange("p f n -> p (f n)"), ACT.Copy).then_inc(oq_taken, 1)
                    act.wait_ge(oq_taken, b + 2)
                    act.dma_start(c.s_a1[bass.ds(b * DS, DS), :], oq[:]).then_inc(oq_stored, 16)

                sequences(act, *interleave(k_start, k_group, k_end, v_group, v_end, v_pick))

            @block.gpsimd
            def _(pool):
                pool.sem_inc(v_split[0], DEEP)
                pool.memset(half[:], -0.5).then_inc(rooted, 1)
                pool.wait_ge(rooted, 1)

                def v_group(b, s_, i):
                    wait_counted(pool, v_high[0], b * NG + (i + 1))
                    values_low(pool, i, 0)

                sequences(pool, *interleave(nothing, nothing, nothing, v_group, nothing, nothing))
                pool.wait_ge(squares_ready, 1)
                pool.tensor_tensor(ms[:, 1, :], ms[:, 0, :], half[:], ALU.pow).then_inc(rooted, 1)

            @block.vector
            def _(dve):
                ch = Chain(dve, dve_chain)
                dve.memset(sign[0:S, :], 1.0)
                ch.link(dve.memset(qz[:], 0.0))
                ch.link(dve.tensor_scalar(sign[S:R, :], lam[S:R, :], -1.0, None, ALU.mult))
                dve.wait_ge(vs_high, 1)
                ch.link(dve.tensor_tensor(vs_lo[:], v_s[:].rearrange("t h e -> t (h e)"), vs_hi[:].bitcast(F32), ALU.subtract))
                dve.wait_ge(s_const, 48)
                dve.sem_inc(k_turned, 2 * G * DEEP)
                dve.sem_inc(v_used, 2)
                dve.sem_inc(v_split[1], DEEP)
                dve.sem_inc(k_lo, 2 * G)
                dve.sem_inc(sc_taken, 1)
                dve.sem_inc(a_taken, 1)
                dve.sem_inc(oq_taken, 1)
                dve.sem_inc(oq_stored, 16)
                dve.sem_inc(start, 1)

                def k_start(b, s_):
                    ch.clear()
                    for m in range(2):
                        part = slice(m * HD, (m + 1) * HD)
                        last = dve.tensor_copy(
                            qz[part, s_, m * S:m * S + HC * STEP].rearrange("p (h t) -> p h t", t=STEP)[:, :, 0:DS],
                            q_s[part, :, bass.ds(b * DS, DS)])
                    ch.link(last)
                    dve.sem_inc(q_copied, 1)
                    dve.wait_ge(q_high, b + 1)
                    ch.link(dve.tensor_tensor(q_hl[:, s_, :, 1, :], qz[:, s_, 0:HC * R].rearrange("p (h r) -> p h r", h=HC),
                                              q_hl[:, s_, :, 0, :].bitcast(F32), ALU.subtract))
                    dve.sem_inc(q_ready, 1)

                def k_group(b, s_, i):
                    for j in range(2 * G):
                        dve.wait_ge(k_hi, b * (2 * G * NG) + (2 * G * i + j + 1))
                        hi, lo = (kT[:, i % 2, part, 4 * (j % 2):4 * (j % 2) + 4, (j // 2) * PAGE:(j // 2 + 1) * PAGE] for part in range(2))
                        dve.tensor_tensor(lo, tp[j][:].rearrange("p (h k) -> p h k", h=4), hi.bitcast(F32), ALU.subtract).then_inc(k_lo, 1)
                    if i > 0:
                        scores_sum(b, s_, i - 1)

                def scores_sum(b, s_, i):
                    dve.wait_ge(sc_low, b * NG + (i + 1))
                    dve.tensor_tensor(s[:, s_, i * GK:(i + 1) * GK], sc[0:R, 0:GK], low_rows[:], ALU.add).then_inc(sc_taken, 1)
                    dve.wait_ge(sc_taken, b * C + (i + 2))
                    dve.tensor_reduce(mx[:, s_, i:i + 1], s[:, s_, i * GK:(i + 1) * GK], AX_X, ALU.max)

                def k_end(b, s_):
                    scores_sum(b, s_, NG - 1)
                    dve.wait_ge(sc_ready, b * C + C)
                    new = s[:, s_, PAST:]
                    ch.link(dve.tensor_tensor(new, sc[0:R, 0:S], new_mask[:, bass.ds(b, 1), :].rearrange("r a k -> r (a k)"), ALU.add))
                    dve.sem_inc(sc_taken, 1)
                    ch.link(dve.tensor_reduce(mx[:, s_, NG:NG + 1], new, AX_X, ALU.max))
                    ch.link(dve.tensor_reduce(top[:, s_:s_ + 1], mx[:, s_, :], AX_X, ALU.max))
                    ch.link(dve.tensor_scalar(top[:, s_:s_ + 1], top[:, s_:s_ + 1], -HD ** -0.5, None, ALU.mult))
                    dve.sem_inc(top_ready, 1)

                def v_start(b, s_):
                    dve.wait_ge(exp_ready, b + 1)
                    ch.link(dve.reciprocal(den[:, s_:s_ + 1], den[:, s_:s_ + 1]))
                    ch.link(dve.tensor_tensor(fac[0:R, s_:s_ + 1], den[:, s_:s_ + 1], sign[:], ALU.mult))
                    ch.link(dve.tensor_copy(fac[R:2 * R, s_:s_ + 1], fac[0:R, s_:s_ + 1]))

                def v_group(b, s_, i):
                    if i == 0:
                        v_start(b, s_)
                    dve.wait_ge(a_hi, b * C + (i + 1))
                    dve.tensor_tensor(aT[:, i % 2, :, 1, :], ap_[:, 0:G * R].rearrange("p (n r) -> p n r", n=G),
                                      aT[:, i % 2, :, 0, :].bitcast(F32), ALU.subtract).then_inc(a_taken, 1)
                    dve.wait_ge(v_high[1], b * NG + (i + 1))
                    values_low(dve, i, 1)

                def v_end(b, s_):
                    dve.wait_ge(a_hi, b * C + C)
                    dve.tensor_tensor(aN[:, 1, :], ap_[0:S, 0:R], aN[:, 0, :].bitcast(F32), ALU.subtract).then_inc(a_taken, 1)
                    dve.wait_ge(o_ready, b + 1)
                    for f in range(2):
                        last = dve.scalar_tensor_tensor(
                            out=om[:, f * 512:(f + 1) * 512].rearrange("p (h e) -> p h e", h=HC // 2),
                            in0=ov[:, f, :].rearrange("p (h e) -> p h e", h=HC // 2), scalar=fac[:, s_:s_ + 1],
                            in1=own[:, f * (HC // 2):(f + 1) * (HC // 2)].unsqueeze(2).broadcast_to([2 * R, HC // 2, 2 * HD]),
                            op0=ALU.mult, op1=ALU.mult)
                    ch.link(last)
                    dve.sem_inc(o_picked, 1)

                sequences(dve, *interleave(k_start, k_group, k_end, v_group, v_end, nothing))
                dve.wait_ge(s_a, 16)
                ch.link(dve.tensor_tensor(sq, a, a, ALU.mult))
                ch.link(dve.tensor_reduce(ms[:, 0, :], sq.rearrange("t (h e) -> t h e", h=HC), AX_X, ALU.add))
                ch.link(dve.tensor_scalar(ms[:, 0, :], ms[:, 0, :], 1.0 / (2 * HD), EPS, ALU.mult, ALU.add))
                dve.sem_inc(squares_ready, 1)
                dve.wait_ge(rooted, 2)
                av = a.rearrange("t (h e) -> t h e", h=HC)
                ch.link(dve.tensor_tensor(av, av, ms[:, 1, :].unsqueeze(2).broadcast_to([S, HC, 2 * HD]), ALU.mult))
                ch.link(dve.tensor_tensor(av, av, g_s[:], ALU.mult))
                dve.sem_inc(s_y, 1)


def project_out(c):
    nc, g = c.nc, c.x
    with Stage(nc, "po") as st:
        w_raw = st.sb("w_raw", [P, KD, D])
        w_hl = st.sb("w_hl", [P, 2, KD, D], F32R)
        y = st.sb("y", [P, 2, D])
        yT = st.sb("yT", [P, 2, 2, KD, P], F32R)
        res = st.sb("res", [P, 2, D])
        x1 = st.sb("x1", [P, 2, D])
        post = st.sb("post", [P, D])
        junk = st.sb("junk", [P, 2, D])
        ss = st.sb("ss", [P, 2, 2])
        half = st.sb("half", [P, 1])
        turn = [st.ps(f"turn{i}", [P, 2, 512]) for i in range(2)]
        out = [st.ps(f"out{i}", [P, 2, 512]) for i in range(2)]
        w_loaded, y_loaded, res_loaded, x1_stored = st.sems("w_loaded", KD), st.sems("y_loaded", 2), st.sems("res_loaded", 2), st.sems("x1_stored", 2)
        w_high, w_split, y_turned, y_high, y_split, out_ready, out_squared, averaged, rooted, out_taken, x1_ready = (st.sem(n) for n in (
            "w_high", "w_split", "y_turned", "y_high", "y_split", "out_ready", "out_squared", "averaged", "rooted", "out_taken", "x1_ready"))
        post_loaded, dve_chain, pool_chain = st.sem("post_loaded"), st.sem("dve_chain"), st.sem("pool_chain")
        out_p = c.out["y_prompt"].rearrange("a t d -> (a t) d")
        out_s = c.out["y_sample"].rearrange("a t d -> (a t) d")

        def blocks(eng, turned, projected):
            turned(0, 0, P)
            with eng.Fori(0, NB // 2 - 1) as i:
                for s in range(2):
                    turned(2 * i + s + 1, 1 - s, P)
                    projected(2 * i + s, s, P)
            turned(NB - 1, 1, P)
            projected(NB - 2, 0, P)
            turned(NB, 0, S)
            projected(NB - 1, 1, P)
            projected(NB, 0, S)

        def at(b, n):
            return slice(T, NT) if n == S else bass.ds(b * P, P)

        with nc.Block() as block:

            @block.sync
            def _(sp):
                def turned(b, s, n):
                    wait_counted(sp, y_turned, b + 1)
                    sp.dma_start(y[0:n, s, :], c.s_y1[at(b, n), :]).then_inc(y_loaded[s], 16)
                    wait_counted(sp, x1_ready, b + 1)
                    sp.dma_start(res[0:n, s, :], c.s_x1[at(b, n), :]).then_inc(res_loaded[s], 16)

                for k in range(KD):
                    sp.dma_start(w_raw[:, k, :], g["w_out_c"][0, k * P:(k + 1) * P, :]).then_inc(w_loaded[k], 16)
                sp.dma_start(post[:], g["norm_post"][1:2, :].broadcast_to([P, D])).then_inc(post_loaded, 16)
                blocks(sp, turned, lambda *_: None)
                sp.wait_ge(x1_stored[0], 16 * (NB // 2 + 2))
                sp.wait_ge(x1_stored[1], 16 * (NB // 2 + 1))

            @block.tensor
            def _(pe):
                def turned(b, s, n):
                    wait_counted(pe, y_loaded[s], (b - s) * 8 + 16)
                    wait_counted(pe, y_split, b + 1)
                    for k in range(KD):
                        last = pe.transpose(turn[s][:, k // 4, (k % 4) * P:(k % 4) * P + n], y[0:n, s, k * P:(k + 1) * P], c.ident[0:n, 0:n])
                    last.then_inc(y_turned, 1)

                def projected(b, s, n):
                    pe.wait_ge(y_split, b + 3)
                    pe.wait_ge(out_taken, b + 1)
                    for f in range(2):
                        cols = slice(f * 512, (f + 1) * 512)
                        for k in range(KD):
                            if f == 0:
                                pe.wait_ge(w_split, k + 1)
                            pe.matmul(out[s][0:n, f, :], yT[:, s, 0, k, 0:n], w_hl[:, 0, k, cols], start=k == 0, stop=False)
                            pe.matmul(out[s][0:n, f, :], yT[:, s, 0, k, 0:n], w_hl[:, 1, k, cols], start=False, stop=False)
                            last = pe.matmul(out[s][0:n, f, :], yT[:, s, 1, k, 0:n], w_hl[:, 0, k, cols], start=False, stop=k == KD - 1)
                    last.then_inc(out_ready, 1)

                blocks(pe, turned, projected)

            def turned_columns(s, n):
                return turn[s][:].rearrange("p f (k t) -> p (f k) t", t=P)[:, :, 0:n]

            @block.scalar
            def _(act):
                def turned(b, s, n):
                    act.wait_ge(y_turned, b + 3)
                    if not (isinstance(b, int) and b < 2):
                        act.wait_ge(out_squared, b - 1)
                    act.activation(yT[:, s, 0, :, 0:n], turned_columns(s, n), ACT.Copy).then_inc(y_high, 1)

                def projected(b, s, n):
                    act.wait_ge(out_ready, b + 1)
                    act.wait_ge(out_taken, b + 1)
                    act.activation(junk[0:n, s, :], out[s][0:n].rearrange("p f c -> p (f c)"), ACT.Square, accum_out=ss[0:n, s, 0:1]).then_inc(out_squared, 1)
                    act.wait_ge(x1_ready, b + 3)
                    act.dma_start(out_s if n == S else out_p[at(b, n), :], x1[0:n, s, :]).then_inc(x1_stored[s], 16)

                for k in range(KD):
                    act.wait_ge(w_loaded[k], 16)
                    act.activation(w_hl[:, 0, k, :], w_raw[:, k, :], ACT.Copy).then_inc(w_high, 1)
                blocks(act, turned, projected)

            @block.gpsimd
            def _(pool):
                ch = Chain(pool, pool_chain)
                ch.link(pool.memset(half[:], -0.5))

                def projected(b, s, n):
                    wait_counted(pool, averaged, b + 1)
                    pool.tensor_tensor(ss[0:n, s, 1:2], ss[0:n, s, 1:2], half[0:n, :], ALU.pow).then_inc(rooted, 1)

                blocks(pool, lambda *_: None, projected)

            @block.vector
            def _(dve):
                ch = Chain(dve, dve_chain)
                for q in (y_turned, y_split, out_taken, x1_ready):
                    dve.sem_inc(q, 2)
                for s in range(2):
                    dve.sem_inc(x1_stored[s], 16)
                for k in range(KD):
                    dve.wait_ge(w_high, k + 1)
                    dve.tensor_tensor(w_hl[:, 1, k, :], w_raw[:, k, :], w_hl[:, 0, k, :].bitcast(F32), ALU.subtract).then_inc(w_split, 1)
                dve.wait_ge(post_loaded, 16)

                def turned(b, s, n):
                    dve.wait_ge(y_high, b + 1)
                    dve.tensor_tensor(yT[:, s, 1, :, 0:n], turned_columns(s, n), yT[:, s, 0, :, 0:n].bitcast(F32), ALU.subtract).then_inc(y_split, 1)

                def projected(b, s, n):
                    ch.clear()
                    dve.wait_ge(out_squared, b + 1)
                    ch.link(dve.tensor_scalar(ss[0:n, s, 1:2], ss[0:n, s, 0:1], 1.0 / D, EPS, ALU.mult, ALU.add))
                    dve.sem_inc(averaged, 1)
                    dve.wait_ge(rooted, b + 1)
                    dve.wait_ge(x1_stored[s], (b - s) * 8 + 16)
                    o = x1[0:n, s, :]
                    ch.link(dve.scalar_tensor_tensor(out=o, in0=out[s][0:n].rearrange("p f c -> p (f c)"), scalar=ss[0:n, s, 1:2],
                                                     in1=post[0:n, :], op0=ALU.mult, op1=ALU.mult))
                    dve.sem_inc(out_taken, 1)
                    dve.wait_ge(res_loaded[s], (b - s) * 8 + 16)
                    ch.link(dve.tensor_tensor(o, o, res[0:n, s, :], ALU.add))
                    dve.sem_inc(x1_ready, 1)

                blocks(dve, turned, projected)


INPUTS = ["x_prompt", "x_sample", "state_mlstm_C", "state_mlstm_n", "state_mlstm_m", "state_mlstm_conv",
          "state_ret_S", "cache_k", "cache_v", "page_table", "norm_pre", "norm_post", "w_in_a", "b_gate_i",
          "b_gate_f", "conv_w", "conv_b", "gn_mlstm", "gn_ret", "w_out_a", "w_in_c", "lambda_qk", "gn_diff", "w_out_c"]
OUTPUTS = {
    "y_prompt": (1, T, D), "y_sample": (DB, DS, D),
    "C_p": (1, 1, H, DK, DK), "n_p": (1, 1, H, DK), "m_p": (1, 1, H), "conv_p": (1, 1, CW - 1, QK),
    "S_p": (1, 1, H, DK, DK), "k_p": (1, 1, T, 2 * HC, HD), "v_p": (1, 1, T, HC, 2 * HD),
    "C_s": (1, DB, H, DK, DK), "n_s": (1, DB, H, DK), "m_s": (1, DB, H), "conv_s": (1, DB, CW - 1, QK),
    "S_s": (1, DB, H, DK, DK), "k_s": (1, DB, DS, 2 * HC, HD), "v_s": (1, DB, DS, HC, 2 * HD),
}


def build(nc, ins, tabs, outs):
    with ExitStack() as ctx:
        c = Core(nc, ins, tabs, outs, ctx)
        with ExitStack() as first:
            h_hi = first.enter_context(nc.sbuf_tensor("h_hi", [P, KD, NT], F32R))
            h_lo = first.enter_context(nc.sbuf_tensor("h_lo", [P, KD, NT], F32R))
            norm_to_columns(c, h_hi, h_lo)
            project_layer0(c, h_hi, h_lo)
        c.hT = ctx.enter_context(nc.sbuf_tensor("hT", [P, KD, NT], F32))
        with ExitStack() as mid:
            rows = mid.enter_context(nc.sbuf_tensor("gate_rows", [H, 2, NT], F32))
            cols = mid.enter_context(nc.sbuf_tensor("gate_cols", [P, NB + 1, 3, H], F32))
            spread = mid.enter_context(nc.sbuf_tensor("gate_spread", [P, 2, NB + DB, H], F32))
            gate_rows(c, rows, cols, spread)
            mix_prompt(c, rows, cols, spread)
            mix_sample(c, rows, cols, spread)
        with ExitStack() as late:
            q_s = late.enter_context(nc.sbuf_tensor("q_s", [P, HC, S], F32))
            k_s = late.enter_context(nc.sbuf_tensor("k_s", [P, HC, S], F32))
            v_s = late.enter_context(nc.sbuf_tensor("v_s", [S, HC, 2 * HD], F32))
            g_s = late.enter_context(nc.sbuf_tensor("g_s", [S, HC, 2 * HD], F32))
            lam = late.enter_context(nc.sbuf_tensor("lam", [P, 1], F32))
            attend_prompt(c, q_s, k_s, v_s, g_s, lam)
            attend_sample(c, q_s, k_s, v_s, g_s, lam)
        project_out(c)


def kernel(**inputs):
    import concourse.bacc as bacc
    from concourse.bass_utils import run_bass_kernel_spmd as run

    nc = bacc.Bacc("TRN2", target_bir_lowering=False, num_devices=1)
    arrays, ins, tabs, outs = {}, {}, {}, {}

    def give(name, a):
        arrays[name] = np.ascontiguousarray(a)
        return nc.dram_tensor(name, a.shape, mybir.dt.from_np(a.dtype), kind="ExternalInput").ap()

    for name in INPUTS:
        ins[name] = give(f"in_{name}", np.asarray(inputs[name]))
    for name, a in shape_tables().items():
        tabs[name] = give(f"tab_{name}", a)
    for name, shape in OUTPUTS.items():
        outs[name] = nc.dram_tensor(f"out_{name}", shape, F32, kind="ExternalOutput").ap()
    build(nc, ins, tabs, outs)
    r = run(nc, [arrays], core_ids=[0])
    return tuple(r.results[0][f"out_{name}"] for name in OUTPUTS)
```
